# Optimizing a Trainium2 kernel written in Bass

```python
import functools
import jax, jax.numpy as jnp
from jax import lax
import numpy as np

D_MODEL = 1024
BATCH = 1
SEQ = 512
DEPTH = 1
DEC_BATCH = 8
DEC_SEQ = 8
PAST_LEN = 4096
PAGE_SIZE = 128

N_HEADS = 8
HEAD_DIM = 64
D_ATTN = N_HEADS * HEAD_DIM
D_CV = D_MODEL // 2
D_MIX = D_ATTN + D_CV
D_IN = 3 * D_ATTN + 2 * D_CV
MOBA_BLOCK = 256
MOBA_TOPK = 3
CV_WIDTH = 31
D_FF = 2816
FFN_CONV_WIDTH = 3
Q_CHUNK = 16
RMS_EPS = 1e-6
LN_EPS = 1e-5

kernel_name = 'hymba_moba_conformer_convffn_step'

def _rmsnorm(x, g):
    xf = x.astype(jnp.float32)
    y = xf * lax.rsqrt(jnp.mean(xf * xf, axis=-1, keepdims=True) + RMS_EPS)
    return (y * g.astype(jnp.float32)).astype(x.dtype)

def _layernorm(x, g, b):
    xf = x.astype(jnp.float32)
    mu = jnp.mean(xf, axis=-1, keepdims=True)
    var = jnp.mean(jnp.square(xf - mu), axis=-1, keepdims=True)
    y = (xf - mu) * lax.rsqrt(var + LN_EPS) * g.astype(jnp.float32) + b.astype(jnp.float32)
    return y.astype(x.dtype)

def _causal_dwconv(x_ext, w, b):
    W = w.shape[0]
    L = x_ext.shape[1] - W + 1
    y = x_ext[:, 0:L] * w[0]
    for j in range(1, W):
        y = y + x_ext[:, j:j + L] * w[j]
    return y + b

def _select_blocks(q, k_means, n_past, k_sel):
    s = jnp.einsum('bhqd,bhnd->bhqn', q, k_means).astype(jnp.float32)
    elig = jnp.arange(k_means.shape[2]) < n_past
    s = jnp.where(elig, s, -jnp.inf)
    _, idx = lax.top_k(s, k_sel)
    slot_ok = jnp.arange(k_sel) < jnp.minimum(n_past, k_sel)
    return idx, slot_ok

def _attend(q, k_sel, v_sel, sel_mask, k_own, v_own, own_mask):
    scale = HEAD_DIM ** -0.5
    lo = jnp.einsum('bhqd,bhkd->bhqk', q, k_own).astype(jnp.float32) * scale
    lo = jnp.where(own_mask, lo, -jnp.inf)
    if k_sel is None:
        p = jax.nn.softmax(lo, axis=-1).astype(v_own.dtype)
        return jnp.einsum('bhqk,bhkd->bhqd', p, v_own)
    ls = jnp.einsum('bhqd,bhqkd->bhqk', q, k_sel).astype(jnp.float32) * scale
    ls = jnp.where(sel_mask, ls, -jnp.inf)
    n_s = ls.shape[-1]
    p = jax.nn.softmax(jnp.concatenate([ls, lo], axis=-1), axis=-1).astype(v_own.dtype)
    return (jnp.einsum('bhqk,bhqkd->bhqd', p[..., :n_s], v_sel)
            + jnp.einsum('bhqk,bhkd->bhqd', p[..., n_s:], v_own))

def _moba_prompt(q, k, v):
    B, S, H, D = q.shape
    nb = -(-S // MOBA_BLOCK)
    pad = nb * MOBA_BLOCK - S
    qh = q.transpose(0, 2, 1, 3)
    def blocks(a):
        a = jnp.pad(a, ((0, 0), (0, pad), (0, 0), (0, 0)))
        return a.reshape(B, nb, MOBA_BLOCK, H, D).transpose(0, 3, 1, 2, 4)
    kb = blocks(k)
    vb = blocks(v)
    k_means = jnp.mean(kb.astype(jnp.float32), axis=3).astype(k.dtype)
    k_sel = min(MOBA_TOPK, nb)
    bi = jnp.arange(B)[:, None, None, None]
    hi = jnp.arange(H)[None, :, None, None]

    def chunk(c):
        start = c * Q_CHUNK
        qc = lax.dynamic_slice_in_dim(qh, start, Q_CHUNK, axis=2)
        blk = start // MOBA_BLOCK
        k_own = lax.dynamic_index_in_dim(kb, blk, axis=2, keepdims=False)
        v_own = lax.dynamic_index_in_dim(vb, blk, axis=2, keepdims=False)
        q_pos = start + jnp.arange(Q_CHUNK)
        k_pos = blk * MOBA_BLOCK + jnp.arange(MOBA_BLOCK)
        own_mask = k_pos[None, :] <= q_pos[:, None]
        idx, slot_ok = _select_blocks(qc, k_means, blk, k_sel)
        k_s = kb[bi, hi, idx].reshape(B, H, Q_CHUNK, k_sel * MOBA_BLOCK, D)
        v_s = vb[bi, hi, idx].reshape(B, H, Q_CHUNK, k_sel * MOBA_BLOCK, D)
        sel_mask = jnp.repeat(slot_ok, MOBA_BLOCK)
        return _attend(qc, k_s, v_s, sel_mask, k_own, v_own, own_mask)

    out = lax.map(chunk, jnp.arange(S // Q_CHUNK))
    return out.transpose(1, 0, 3, 2, 4).reshape(B, S, H * D)

def _moba_sample(q, k_new, v_new, *, pool_k, pool_v, page_table):
    DB, T, H, D = q.shape
    n_pages = page_table.shape[1]
    ppb = MOBA_BLOCK // PAGE_SIZE
    npb = (n_pages * PAGE_SIZE) // MOBA_BLOCK
    n_rem = n_pages - npb * ppb
    qh = q.transpose(0, 2, 1, 3)
    own_pt = page_table[:, npb * ppb:]
    k_own_c = pool_k[own_pt].reshape(DB, n_rem * PAGE_SIZE, H, D)
    v_own_c = pool_v[own_pt].reshape(DB, n_rem * PAGE_SIZE, H, D)
    k_own = jnp.concatenate([k_own_c, k_new], axis=1).transpose(0, 2, 1, 3)
    v_own = jnp.concatenate([v_own_c, v_new], axis=1).transpose(0, 2, 1, 3)
    own_mask = jnp.concatenate([jnp.ones((T, n_rem * PAGE_SIZE), bool),
                                jnp.tril(jnp.ones((T, T), bool))], axis=1)
    if npb == 0:
        out = _attend(qh, None, None, None, k_own, v_own, own_mask)
    else:
        k_sel = min(MOBA_TOPK, npb)
        kp = pool_k[page_table[:, :npb * ppb]]
        k_means = jnp.mean(kp.reshape(DB, npb, MOBA_BLOCK, H, D).astype(jnp.float32), axis=2)
        k_means = k_means.astype(q.dtype).transpose(0, 2, 1, 3)
        idx, slot_ok = _select_blocks(qh, k_means, npb, k_sel)
        logical = idx[..., None] * ppb + jnp.arange(ppb)
        phys = page_table[jnp.arange(DB)[:, None, None, None, None], logical]
        hi = jnp.arange(H)[None, :, None, None, None]
        k_s = pool_k[phys, :, hi, :].reshape(DB, H, T, k_sel * MOBA_BLOCK, D)
        v_s = pool_v[phys, :, hi, :].reshape(DB, H, T, k_sel * MOBA_BLOCK, D)
        sel_mask = jnp.repeat(slot_ok, MOBA_BLOCK)
        out = _attend(qh, k_s, v_s, sel_mask, k_own, v_own, own_mask)
    return out.transpose(0, 2, 1, 3).reshape(DB, T, H * D)

def _layer(x, moba_fn, cv_hist, ffn_hist, g_pre_mix, w_in, b_in, w_cv_dw, b_cv_dw, g_cv_ln, b_cv_ln,
           w_cv_pw, b_cv_pw, w_out, g_post_mix, g_pre_ffn, w_up, w_ffn_dw, b_ffn_dw, w_down, g_post_ffn):
    B, L, _ = x.shape
    h = _rmsnorm(x, g_pre_mix)
    z = h @ w_in + b_in
    q, k, v, cva, cvg = jnp.split(z, [D_ATTN, 2 * D_ATTN, 3 * D_ATTN, 3 * D_ATTN + D_CV], axis=-1)
    q = q.reshape(B, L, N_HEADS, HEAD_DIM)
    k = k.reshape(B, L, N_HEADS, HEAD_DIM)
    v = v.reshape(B, L, N_HEADS, HEAD_DIM)
    attn = moba_fn(q, k, v)
    glu = cva * jax.nn.sigmoid(cvg)
    glu_ext = jnp.concatenate([cv_hist, glu], axis=1)
    c = _causal_dwconv(glu_ext, w_cv_dw, b_cv_dw)
    c = jax.nn.silu(_layernorm(c, g_cv_ln, b_cv_ln))
    c = c @ w_cv_pw + b_cv_pw
    mix = jnp.concatenate([attn, c], axis=-1) @ w_out
    x = x + _rmsnorm(mix, g_post_mix)
    h = _rmsnorm(x, g_pre_ffn)
    u = h @ w_up
    u_ext = jnp.concatenate([ffn_hist, u], axis=1)
    u = _causal_dwconv(u_ext, w_ffn_dw, b_ffn_dw)
    gate, val = jnp.split(u, 2, axis=-1)
    f = (jax.nn.silu(gate) * val) @ w_down
    x = x + _rmsnorm(f, g_post_ffn)
    new_cv = glu_ext[:, -(CV_WIDTH - 1):]
    new_ffn = u_ext[:, -(FFN_CONV_WIDTH - 1):]
    return x, k, v, new_cv, new_ffn

def setup_inputs(seed: int = 0) -> dict:
    key = jax.random.key(seed)
    ks = jax.random.split(key, 24)
    f32 = jnp.float32
    n_pages = PAST_LEN // PAGE_SIZE
    n_phys = (DEC_BATCH * n_pages * 5 + 3) // 4
    def nrm(k, shape, s):
        return jax.random.normal(k, shape, f32) * s
    def gain(k, shape):
        return 1.0 + 0.02 * jax.random.normal(k, shape, f32)
    perm = jax.random.permutation(ks[2], n_phys)
    page_table = perm[:DEC_BATCH * n_pages].reshape(DEC_BATCH, n_pages).astype(jnp.int32)
    return {
        'x_prompt': nrm(ks[0], (BATCH, SEQ, D_MODEL), 1.0),
        'x_sample': nrm(ks[1], (DEC_BATCH, DEC_SEQ, D_MODEL), 1.0),
        'cache_k': nrm(ks[3], (DEPTH, n_phys, PAGE_SIZE, N_HEADS, HEAD_DIM), 1.0),
        'cache_v': nrm(ks[4], (DEPTH, n_phys, PAGE_SIZE, N_HEADS, HEAD_DIM), 1.0),
        'page_table': page_table,
        'state_cv': nrm(ks[5], (DEPTH, DEC_BATCH, CV_WIDTH - 1, D_CV), 0.5),
        'state_ffn': nrm(ks[6], (DEPTH, DEC_BATCH, FFN_CONV_WIDTH - 1, 2 * D_FF), 1.0),
        'g_pre_mix': gain(ks[7], (DEPTH, D_MODEL)),
        'w_in': nrm(ks[8], (DEPTH, D_MODEL, D_IN), D_MODEL ** -0.5),
        'b_in': nrm(ks[9], (DEPTH, D_IN), 0.02),
        'w_cv_dw': nrm(ks[10], (DEPTH, CV_WIDTH, D_CV), CV_WIDTH ** -0.5),
        'b_cv_dw': nrm(ks[11], (DEPTH, D_CV), 0.02),
        'g_cv_ln': gain(ks[12], (DEPTH, D_CV)),
        'b_cv_ln': nrm(ks[13], (DEPTH, D_CV), 0.02),
        'w_cv_pw': nrm(ks[14], (DEPTH, D_CV, D_CV), D_CV ** -0.5),
        'b_cv_pw': nrm(ks[15], (DEPTH, D_CV), 0.02),
        'w_out': nrm(ks[16], (DEPTH, D_MIX, D_MODEL), D_MIX ** -0.5),
        'g_post_mix': gain(ks[17], (DEPTH, D_MODEL)),
        'g_pre_ffn': gain(ks[18], (DEPTH, D_MODEL)),
        'w_up': nrm(ks[19], (DEPTH, D_MODEL, 2 * D_FF), D_MODEL ** -0.5),
        'w_ffn_dw': nrm(ks[20], (DEPTH, FFN_CONV_WIDTH, 2 * D_FF), FFN_CONV_WIDTH ** -0.5),
        'b_ffn_dw': nrm(ks[21], (DEPTH, 2 * D_FF), 0.02),
        'w_down': nrm(ks[22], (DEPTH, D_FF, D_MODEL), D_FF ** -0.5),
        'g_post_ffn': gain(ks[23], (DEPTH, D_MODEL)),
    }

def reference(x_prompt, x_sample, cache_k, cache_v, page_table, state_cv, state_ffn,
              g_pre_mix, w_in, b_in, w_cv_dw, b_cv_dw, g_cv_ln, b_cv_ln, w_cv_pw, b_cv_pw,
              w_out, g_post_mix, g_pre_ffn, w_up, w_ffn_dw, b_ffn_dw, w_down, g_post_ffn):
    yp = x_prompt
    ys = x_sample
    B = x_prompt.shape[0]
    kp_l, vp_l, cvp_l, ffp_l = [], [], [], []
    ks_l, vs_l, cvs_l, ffs_l = [], [], [], []
    for l in range(DEPTH):
        prm = (g_pre_mix[l], w_in[l], b_in[l], w_cv_dw[l], b_cv_dw[l], g_cv_ln[l], b_cv_ln[l],
               w_cv_pw[l], b_cv_pw[l], w_out[l], g_post_mix[l], g_pre_ffn[l], w_up[l],
               w_ffn_dw[l], b_ffn_dw[l], w_down[l], g_post_ffn[l])
        cv0 = jnp.zeros((B, CV_WIDTH - 1, D_CV), x_prompt.dtype)
        ff0 = jnp.zeros((B, FFN_CONV_WIDTH - 1, 2 * D_FF), x_prompt.dtype)
        yp, kp, vp, cvp, ffp = _layer(yp, _moba_prompt, cv0, ff0, *prm)
        moba_s = functools.partial(_moba_sample, pool_k=cache_k[l], pool_v=cache_v[l],
                                   page_table=page_table)
        ys, ksm, vsm, cvs, ffs = _layer(ys, moba_s, state_cv[l], state_ffn[l], *prm)
        kp_l.append(kp); vp_l.append(vp); cvp_l.append(cvp); ffp_l.append(ffp)
        ks_l.append(ksm); vs_l.append(vsm); cvs_l.append(cvs); ffs_l.append(ffs)
    return (yp, ys, jnp.stack(kp_l), jnp.stack(vp_l), jnp.stack(cvp_l), jnp.stack(ffp_l),
            jnp.stack(ks_l), jnp.stack(vs_l), jnp.stack(cvs_l), jnp.stack(ffs_l))


_drawn_inputs = setup_inputs


def setup_inputs(seed=0):
    import zlib

    import numpy as np

    out = dict(_drawn_inputs(seed))
    spreads = {}
    factors = {'g_pre_mix': 2.697,
     'g_cv_ln': 3.085,
     'b_cv_ln': 3.387,
     'g_post_mix': 3.481,
     'g_pre_ffn': 2.876,
     'b_ffn_dw': 3.319,
     'g_post_ffn': 17.818,
     'b_cv_pw': 5.526}
    for name, (base, spread) in spreads.items():
        noise = np.random.default_rng([zlib.crc32(name.encode()), seed]).standard_normal(out[name].shape)
        drawn = base * np.exp(spread * noise) if base else spread * noise
        out[name] = __import__('jax').numpy.asarray(drawn.astype(out[name].dtype))
    for name, factor in factors.items():
        out[name] = (out[name] * factor).astype(out[name].dtype)
    return out
```

```python
from contextlib import ExitStack

import concourse.bass as bass
from concourse import mybir

ALU = mybir.AluOpType
ACT = mybir.ActivationFunctionType
AX = mybir.AxisListType
F32 = mybir.dt.float32
I32 = mybir.dt.int32
P = 128

D = 1024
KC = D // P
TP_ = 512
NB, NT = 8, 8
TS = NB * NT
TOK = TP_ + TS
HALF = TOK // 2
TT = 5
H, DH = 8, 64
HP = H // 2
DA = H * DH
PAGES, PAGE = 32, 128
SUPER = 8
BLK = 16
CW = 31
CT = 4
GX = (CW - 1) + TP_
SX = CW - 1 + NT
GLUW = GX + NB * SX
DFF = 2816
FT_N = DFF // P
UXS = 2 + NT
UXW = 2 + TP_ + NB * UXS
SCALE = DH ** -0.5
BIG = 1.0e30
TOPK = 3

CONST = {}
_at = 0
for _n, _w in (("ident", 128), ("causal", 128), ("ownmask", 2 * TS), ("order", BLK * BLK), ("denmap", 256),
               ("b_in", 20), ("w_cv", CT * (CW + 1)), ("g_ln", CT), ("b_ln", CT), ("b_pw", CT),
               ("g_pre", KC), ("g_ffn", KC), ("dw", 44 * 4)):
    CONST[_n] = (_at, _w)
    _at += _w
NCONST = _at


def tok(t):
    return P if t < 4 else TS


class Steps:

    def __init__(self, eng, sem, base=0):
        self.eng, self.sem, self.base, self.n = eng, sem, base, 0

    def then(self, ins):
        self.n += 1
        ins.then_inc(self.sem, 1)
        self.eng.wait_ge(self.sem, self.base + self.n)


def build_layer(nc, a):
    ctx = ExitStack()
    with ctx:
        def sem(name):
            return ctx.enter_context(nc.semaphore(name))

        def sb(name, shape, dt=F32):
            return ctx.enter_context(nc.sbuf_tensor(name, shape, dt))

        consts = sb("consts", [P, NCONST])
        small = sb("small", [P, 384])
        ones = sb("ones", [P, P])
        pages = sb("pages", [1, NB * PAGES], I32)
        hT_ = sb("hT", [P, KC * TOK])
        A = sb("A", [P, 19064])
        B = sb("B", [P, 30720])

        def cst(name, rows=P):
            o, w = CONST[name]
            return consts[0:rows, o:o + w]

        def at(mem, off, *dims):
            n = 1
            for d in dims:
                n *= d
            v = mem[:, off:off + n]
            if len(dims) == 2:
                return v.rearrange("p (a b) -> p a b", a=dims[0])
            if len(dims) == 3:
                return v.rearrange("p (a b c) -> p a b c", a=dims[0], b=dims[1])
            if len(dims) == 4:
                return v.rearrange("p (a b c d) -> p a b c d", a=dims[0], b=dims[1], c=dims[2])
            return v

        ident = cst("ident")
        causal = cst("causal")
        ownmask = cst("ownmask")
        order = cst("order").rearrange("p (n m) -> p n m", n=BLK)
        denmap = cst("denmap").rearrange("p (g r) -> p g r", g=2)
        b_in = cst("b_in")
        w_cv = cst("w_cv").rearrange("p (c j) -> p c j", c=CT)
        dwv = cst("dw").rearrange("p (u f j) -> p u f j", u=2, f=FT_N)

        hT = hT_[:, :].rearrange("p (k t) -> p k t", k=KC)
        mixT = hT
        qZ = at(A, 0, HP, 2, TP_)
        kP = at(A, 4096, HP, TP_)
        vP = at(A, 6144, TT, DA)
        glu = at(A, 8704, CT, GLUW)
        conv = at(A, 12088, CT, TOK)
        oT = at(A, 14392, NB, P)
        qR = at(A, 15416, 2 * H, TS)
        qS = at(A, 16440, 2 * H, 32)
        kTs = at(A, 16952, HP, TS)
        kOwn = at(A, 17208, 2 * H, TS)
        sig = at(A, 18232, TOK)
        qTs = at(A, 18232, HP, TS)
        kN = at(B, 0, 4, 4, DA)
        kT = at(B, 8192, 4, 2 * H, P)
        vN = at(B, 16384, 4, 4, DA)
        wz = at(B, 24576, KC, 2, P)
        S = at(B, 26624, 2, 1024)
        pT = at(B, 28672, 2, SUPER, P)
        rank = at(B, 28672, 2 * BLK * BLK)
        rankv = rank.rearrange("p (g n m) -> p g n m", g=2, n=BLK)
        vT = at(B, 28672, TP_)
        xA = at(B, 8192, TT, D)
        junkA = at(B, 13312, D)
        histN = at(B, 14336, 2, DA)
        bvB = at(B, 15360, DA)
        wq = at(B, 16384, KC, DA)
        wv = wq
        wk = at(B, 26624, KC, DA)
        pP = at(B, 0, 2, 4, TP_)
        pPT = at(B, 4096, 2, 4, TP_)
        x1 = at(B, 8192, TT, D)
        kNat = at(B, 13312, TT, DA)
        wpw = at(B, 15872, CT, DA)
        gPost = at(B, 17920, D)
        cvN = at(B, 18944, 2, DA)
        mu = at(B, 19968, TOK)
        sd = at(B, 20544, TOK)
        sq = at(B, 21120, CT, TOK)
        histF = at(B, 24576, 2 * DFF)
        gluS = at(A, 17208, CT, TS)
        wo = at(B, 0, KC, D)
        t1 = at(A, 0, 2, D)
        junk = at(A, 2048, D)
        h2T = at(A, 14392, KC, TOK)
        fT = at(A, 0, FT_N, TOK)
        histT = at(A, 12672, 2, FT_N, 16)
        last = at(A, 13376, 2, FT_N, 18)
        ux = at(B, 0, 2, 2, UXW)
        cvo = at(B, 2376, 2, 2, TOK)
        sg2 = at(B, 4680, 2, TOK)
        wu = [at(B, 13312 + 2048 * i, KC, 2, P) for i in range(2)]
        wd = at(B, 19968, 4, 2, TP_)
        gFfn = at(B, 18944, D)
        y0 = at(B, 0, TT, TP_)
        yo = at(B, 2560, 2, D)
        junkY = at(B, 5832, TP_)
        ss = small[:, 0:8]
        rstd = small[:, 8:16]
        bsum, bmax, pen, tA, tB, tC = (small[:, 32 + 32 * i:64 + 32 * i] for i in range(6))
        mcol = small[:, 224:256]
        nb = small[:, 16:18]
        rs = small[:, 18:22]
        rsum = small[:, 22:24]
        rden = small[:, 24:25]
        nbg = small[:, 25:29]
        epsr = small[:, 29:30]
        epsl = small[:, 30:31]
        mx2 = small[:, 256:260]
        pm = small[:, 260:268]
        pnb = small[:, 268:276]
        prs = small[:, 276:284]
        prr = small[:, 284:292]
        ss2 = small[:, 292:312]
        r2 = small[:, 312:332]
        wdw = at(small, 332, 2, 2, 4)
        ss3 = small[:, 348:364]
        r3 = small[:, 364:372]
        own = sb("own", [P, 2 * TS])
        ownS = own[:, :].rearrange("p (g k) -> p g k", g=2)
        pTo_ = sb("pTo", [P, 2 * P])
        pTo = pTo_[:, :].rearrange("p (g r) -> p g r", g=2)
        oN = sb("oN", [P, P])

        banks = {n: ctx.enter_context(nc.psum_tensor(n, [P, 512], F32))
                 for n in ("z0", "z1", "sc0", "sc1", "tp0", "tp1", "ob", "sm")}
        Z = [banks["z0"], banks["z1"]]
        SC = [banks["sc0"], banks["sc1"]]
        TB = [banks["tp0"], banks["tp1"]]
        OB, SM = banks["ob"], banks["sm"]
        own_ps = SM[:, 0:128].rearrange("p (g k) -> p g k", g=2)
        den_ps = OB[:, 384:385]

        names = """c_loaded x_loaded pt_loaded hist_loaded bv_loaded wq_loaded wk_loaded wv_loaded
            pool_set x_summed x_scaled xt_done ht_ready hist_done hist_put zq_done zq_putA zq_putV
            ks_done ks_put kown_put vs_done vs_put qr_ready qs_ready act_step dve_step pool_step
            kn_full0 kn_full1 kn_full2 kn_full3 v_full0 v_full1 v_full2 v_full3 kt_ready scores_done s_put own_done
            soft_step nb_ready probs_ready rsum_ready p_turned pt_put own_turned pto_put den_done
            pv_done den_inv o_norm ot_done ot_put wz_full z1_done g_exp sig_ready g_bias z1_put
            v2_done v2_put v2_turned v2_home k2_done k2_put
            xr_loaded wpw_loaded gpost_loaded histf_loaded wo_loaded wu_full0 wu_full1 wd_full0 wd_full1 wd_full2 wd_full3
            gffn_loaded knat_done knat_put glus_put glun_done glun_put st1_done mu_put sq_ready st2_done sd_put sd_inv
            ln_ready sg_put c_ready ps_done pst_step pnb_ready pexp pr_step pnorm pt2_done ptt_put pv2_done o2_put
            mix_put pw_done pw_put hf_done hf_put mo_done mo_sq mo_sum mo_rt mo_step t1_put x1_ready x1_sq x1_step h2_ready h2_done
            h2_put up_done ux_put taps_put hist_in last_put cv_done g_sig ft_ready f_step ul_done ul_put dn_done y_sq
            y0_put y_step y_sum y_rt x1_rt g_conv conv_step yo_ready stored_kv stored_ffn stored_y0 stored_y1 conv_done""".split()
        s = {n: sem(n) for n in names}
        block = ctx.enter_context(nc.Block())

        w_in = a["w_in"][0].rearrange("(k p) n -> p k n", p=P)
        ck = a["cache_k"][0].rearrange("f k h d -> f k (h d)")
        cv = a["cache_v"][0].rearrange("f k h d -> f k (h d)")
        kn_full = [s[f"kn_full{i}"] for i in range(4)]
        v_full = [s[f"v_full{i}"] for i in range(4)]

        @block.sync
        def _(sp):
            sp.dma_start(pages[:], a["page_table"].rearrange("(o b) n -> o (b n)", o=1)).then_inc(s["pt_loaded"], 16)
            sp.dma_start(xA[:, 0:4, :], a["x_prompt"][0].rearrange("(t p) n -> p t n", p=P)).then_inc(s["x_loaded"], 16)
            sp.dma_start(xA[0:TS, 4, :], a["x_sample"].rearrange("b t n -> (b t) n")).then_inc(s["x_loaded"], 16)
            sp.dma_start(wq, w_in[:, :, 0:DA]).then_inc(s["wq_loaded"], 16)
            sp.dma_start(wk, w_in[:, :, DA:2 * DA]).then_inc(s["wk_loaded"], 16)
            sp.wait_ge(s["pt_loaded"], 16)

            def page_numbers(b, u):
                _, numbers = nc.values_load_multi_w_load_instructions(
                    pages[0:1, bass.ds(b * PAGES + 4 * u, 4)], engines=[mybir.EngineType.SP], min_val=0,
                    max_val=ck.shape[0] - 1)
                return numbers

            def load_k(b, u):
                for i, pg in enumerate(page_numbers(b, u)):
                    sp.dma_start(kN[:, u % 4, i, :], ck[bass.ds(pg, 1)].rearrange("a k n -> (a k) n")).then_inc(kn_full[u % 4], 16)

            def load_v(b, u):
                for i, pg in enumerate(page_numbers(b, u)):
                    sp.dma_start(vN[32 * i:32 * i + 32, u % 4, :, :],
                                 cv[bass.ds(pg, 1)].rearrange("a (g r) n -> (a r) g n", g=4)).then_inc(v_full[u % 4], 16)

            for u in range(4):
                load_k(0, u)
            sp.wait_ge(s["zq_done"], 2 * HP)
            sp.dma_start(wv, w_in[:, :, 2 * DA:3 * DA]).then_inc(s["wv_loaded"], 16)
            for u in range(4, 8):
                sp.wait_ge(s["kt_ready"], u - 3)
                load_k(0, u)

            def wz_glu(i):
                sp.dma_start(wz[:, :, 0, :], w_in[:, :, bass.ds(4 * DA + i * P, P)]).then_inc(s["wz_full"], 16)
                sp.dma_start(wz[:, :, 1, :], w_in[:, :, bass.ds(3 * DA + i * P, P)]).then_inc(s["wz_full"], 16)

            def wz_kv(i):
                sp.dma_start(wz[:, :, 0, :], w_in[:, :, bass.ds(2 * DA + i * P, P)]).then_inc(s["wz_full"], 16)
                sp.dma_start(wz[:, :, 1, :], w_in[:, :, bass.ds(DA + i * P, P)]).then_inc(s["wz_full"], 16)

            def step(b, last, load_w):
                load_w()
                sp.wait_ge(s["pv_done"], b * 8)
                for u in range(4):
                    load_v(b, u)
                if not last:
                    for u in range(6):
                        sp.wait_ge(s["kt_ready"], b * 8 + (8 + u - 3))
                        load_k(b + 1, u)
                for u in range(4, 8):
                    sp.wait_ge(s["pv_done"], b * 8 + (u - 3))
                    load_v(b, u)
                if not last:
                    for u in (6, 7):
                        sp.wait_ge(s["kt_ready"], b * 8 + (8 + u - 3))
                        load_k(b + 1, u)

            sp.wait_ge(s["vs_done"], 1)

            def w1(i):
                sp.wait_ge(s["z1_done"], i * 4)
                wz_glu(i)

            def w2(i):
                sp.wait_ge(s["z1_done"], 16)
                sp.wait_ge(s["k2_done"], i)
                wz_kv(i)

            with sp.Fori(0, 4) as i:
                step(i, False, lambda: w1(i))
            with sp.Fori(0, 3) as i:
                step(i + 4, False, lambda: w2(i))
            step(7, True, lambda: w2(3))
            sp.wait_ge(s["scores_done"], 4 * NB)
            sp.wait_ge(s["p_turned"], 4 * NB)
            sp.wait_ge(s["pv_done"], SUPER * NB)
            sp.dma_start(wpw, a["w_cv_pw"][0].rearrange("(k p) n -> p k n", p=P)).then_inc(s["wpw_loaded"], 16)
            sp.dma_start(x1[:, 0:4, :], a["x_prompt"][0].rearrange("(t p) n -> p t n", p=P)).then_inc(s["xr_loaded"], 16)
            sp.dma_start(x1[0:TS, 4, :], a["x_sample"].rearrange("b t n -> (b t) n")).then_inc(s["xr_loaded"], 16)
            sp.dma_start(gPost, a["g_post_mix"][0].partition_broadcast(P)).then_inc(s["gpost_loaded"], 16)
            sp.dma_start(histF[0:16, :], a["state_ffn"][0].rearrange("b w n -> (b w) n")).then_inc(s["histf_loaded"], 16)
            sp.wait_ge(s["pv2_done"], H)
            sp.dma_start(wo, a["w_out"][0].rearrange("(k p) n -> p k n", p=P)).then_inc(s["wo_loaded"], 16)
            w_up = a["w_up"][0].rearrange("(k p) n -> p k n", p=P)
            wu_full = [s["wu_full0"], s["wu_full1"]]

            def load_up(f, slot):
                for u in range(2):
                    sp.dma_start(wu[slot][:, :, u, :], w_up[:, :, bass.ds(f * P + u * DFF, P)]).then_inc(wu_full[slot], 16)

            sp.wait_ge(s["pw_done"], 2 * CT)
            sp.wait_ge(s["stored_kv"], 16 * 7)
            load_up(0, 0)
            load_up(1, 1)
            sp.dma_start(gFfn, a["g_post_ffn"][0].partition_broadcast(P)).then_inc(s["gffn_loaded"], 16)
            with sp.Fori(0, FT_N // 2 - 1) as i:
                for slot in range(2):
                    sp.wait_ge(s["up_done"], i * 8 + 4 * (slot + 1))
                    load_up(i * 2 + (2 + slot), slot)
            w_dn = a["w_down"][0].rearrange("(k p) n -> p k n", p=P)
            wd_full = [s[f"wd_full{i}"] for i in range(4)]
            for n in range(FT_N):
                if n >= 4:
                    sp.wait_ge(s["dn_done"], n - 3)
                nh, kk = n // 11, n % 11
                sp.dma_start(wd[:, n % 4, :, :], w_dn[:, 2 * kk:2 * kk + 2, nh * TP_:(nh + 1) * TP_]).then_inc(wd_full[n % 4], 16)
            sp.wait_ge(s["ul_put"], 11)
            sp.dma_start(a["ffn_p"][0, 0], histF[0:2, :]).then_inc(s["stored_ffn"], 16)
            sp.dma_start(a["ffn_s"][0].rearrange("b w n -> (b w) n"), histF[2:18, :]).then_inc(s["stored_ffn"], 16)
            for t in range(TT):
                sp.wait_ge(s["yo_ready"], t + 1)
                dst = a["y_p"][0, t * P:(t + 1) * P, :] if t < 4 else a["y_s"].rearrange("b t n -> (b t) n")
                sp.dma_start(dst, yo[0:tok(t), t % 2, :]).then_inc(s[f"stored_y{t % 2}"], 16)
            sp.wait_ge(s["stored_ffn"], 32)
            sp.wait_ge(s["stored_y0"], 16 * 3)
            sp.wait_ge(s["stored_y1"], 16 * 2)

        @block.tensor
        def _(pe):
            pe.wait_ge(s["c_loaded"], 16)
            pe.wait_ge(s["pool_set"], 1)
            turn = [TB[0], TB[1], SC[0], SC[1]]
            for t in range(TT):
                pe.wait_ge(s["x_scaled"], t + 1)
                for j in range(2):
                    n = 2 * t + j
                    if n >= 4:
                        pe.wait_ge(s["ht_ready"], n - 3)
                    for k in range(4):
                        ins = pe.transpose(turn[n % 4][:, k * P:k * P + tok(t)],
                                           xA[0:tok(t), t, (4 * j + k) * P:(4 * j + k + 1) * P],
                                           ident[0:tok(t), 0:tok(t)])
                    ins.then_inc(s["xt_done"], 1)
            pe.wait_ge(s["ht_ready"], 2 * TT)
            pe.wait_ge(s["wq_loaded"], 16)
            for hp in range(HP):
                for half in range(2):
                    if hp:
                        pe.wait_ge((s["zq_putA"], s["zq_putV"])[half], hp)
                    for k in range(KC):
                        ins = pe.matmul(Z[half][:, 0:HALF], wq[:, k, hp * P:(hp + 1) * P],
                                        hT[:, k, half * HALF:(half + 1) * HALF], start=(k == 0), stop=(k == KC - 1))
                    ins.then_inc(s["zq_done"], 1)
            pe.wait_ge(s["hist_loaded"], 16)
            for r in range(2):
                for c in range(CT):
                    ins = pe.transpose((OB, SM)[r][:, c * 120:(c + 1) * 120], histN[0:120, r, c * P:(c + 1) * P],
                                       ident[0:120, 0:120])
                ins.then_inc(s["hist_done"], 1)
            pe.wait_ge(s["wk_loaded"], 16)
            for hp in range(HP):
                for k in range(KC):
                    ins = pe.matmul(TB[0][:, hp * TS:(hp + 1) * TS], wk[:, k, hp * P:(hp + 1) * P],
                                    hT[:, k, TP_:TOK], start=(k == 0), stop=(k == KC - 1))
            ins.then_inc(s["ks_done"], 1)
            pe.wait_ge(s["wv_loaded"], 16)
            for k in range(KC):
                ins = pe.matmul(TB[1][0:TS, :], hT[:, k, TP_:TOK], wv[:, k, :], start=(k == 0), stop=(k == KC - 1))
            ins.then_inc(s["vs_done"], 1)

            def scores(b):
                pe.wait_ge(s["qs_ready"], b + 1)
                for j in range(4):
                    pe.wait_ge(s["kt_ready"], b * 8 + (2 * j + 2))
                    pe.wait_ge(s["s_put"], b * 4 + max(j - 1, 0))
                    for g in range(2):
                        for c in range(2):
                            for h4 in range(4):
                                hc = 2 * (4 * g + h4) + c
                                ins = pe.matmul(SC[j % 2][32 * h4:32 * h4 + 32, g * 256:(g + 1) * 256]
                                                .rearrange("p (a k) -> p a k", a=2),
                                                qS[:, hc, :], kT[:, 2 * (j % 2):2 * (j % 2) + 2, hc, :],
                                                start=(c == 0), stop=(c == 1))
                    ins.then_inc(s["scores_done"], 1)
                for g in range(2):
                    for c in range(2):
                        for h4 in range(4):
                            hc = 2 * (4 * g + h4) + c
                            ins = pe.matmul(SM[32 * h4:32 * h4 + 32, g * TS:(g + 1) * TS], qS[:, hc, :], kOwn[:, hc, :],
                                            start=(c == 0), stop=(c == 1))
                ins.then_inc(s["own_done"], 1)

            def values(b):
                for n in range(4):
                    g, quad = n // 2, n % 2
                    pe.wait_ge(s["probs_ready"], b * 3 + (g + 1 if n < 3 else 3))
                    pe.wait_ge(s["pt_put"], b * 4 + max(n - 1, 0))
                    for u in range(4):
                        v = 4 * quad + u
                        ins = pe.transpose(TB[n % 2][:, u * P:(u + 1) * P], S[:, g, v * P:(v + 1) * P], ident)
                    ins.then_inc(s["p_turned"], 1)
                for g in range(2):
                    ins = pe.transpose(SM[0:TS, P + g * P:P + (g + 1) * P], ownS[:, g, :], ident)
                ins.then_inc(s["own_turned"], 1)
                pe.wait_ge(s["rsum_ready"], b + 1)
                pe.wait_ge(s["o_norm"], b)
                for g in range(2):
                    ins = pe.matmul(den_ps, denmap[:, g, :], rsum[:, g:g + 1], start=(g == 0), stop=(g == 1))
                ins.then_inc(s["den_done"], 1)
                pe.wait_ge(s["pto_put"], b + 1)
                pTo4 = pTo.rearrange("p g (r i) -> p g i r", i=4)
                for hp in range(HP):
                    pe.matmul(OB[32 * hp:32 * hp + 32, 0:P], pTo4[:, hp // 2, 0, :], vP[:, 4, hp * P:(hp + 1) * P],
                              start=True, stop=False)
                for u in range(SUPER):
                    pe.wait_ge(v_full[u % 4], b * 128 + 64 * (u // 4 + 1))
                    if u == 0:
                        pe.wait_ge(s["pt_put"], b * 4 + 4)
                    for i in range(4):
                        for hp in range(HP):
                            w = pT[:, hp // 2, u, :].rearrange("p (r i) -> p i r", i=4)[:, i, :]
                            ins = pe.matmul(OB[32 * hp:32 * hp + 32, 0:P], w, vN[:, u % 4, i, hp * P:(hp + 1) * P],
                                            start=False, stop=(u == SUPER - 1 and i == 3))
                    ins.then_inc(s["pv_done"], 1)
                pe.wait_ge(s["o_norm"], b + 1)
                pe.wait_ge(s["pt_put"], b * 4 + 4)
                pe.transpose(TB[0][:, 0:P], oN[:, :], ident).then_inc(s["ot_done"], 1)

            def glu_tiles(i):
                pe.wait_ge(s["wz_full"], i * 32 + 32)
                for n in range(4):
                    u, half = n // 2, n % 2
                    if u:
                        pe.wait_ge(s["g_exp"], i * 2 + (half + 1))
                    else:
                        pe.wait_ge(s["z1_put"], i * 2)
                    for k in range(KC):
                        ins = pe.matmul(Z[half][:, 0:HALF], wz[:, k, u, :], hT[:, k, half * HALF:(half + 1) * HALF],
                                        start=(k == 0), stop=(k == KC - 1))
                    ins.then_inc(s["z1_done"], 1)

            def kv_tiles(i):
                pe.wait_ge(s["wz_full"], i * 32 + 160)
                pe.wait_ge(s["z1_put"], 8)
                pe.wait_ge(s["v2_put"], i)
                for k in range(KC):
                    ins = pe.matmul(Z[0][:, 0:TP_], wz[:, k, 0, :], hT[:, k, 0:TP_], start=(k == 0), stop=(k == KC - 1))
                ins.then_inc(s["v2_done"], 1)
                pe.wait_ge(s["k2_put"], i)
                for k in range(KC):
                    ins = pe.matmul(Z[1][:, 0:TP_], wz[:, k, 1, :], hT[:, k, 0:TP_], start=(k == 0), stop=(k == KC - 1))
                ins.then_inc(s["k2_done"], 1)
                pe.wait_ge(s["v2_put"], i + 1)
                pe.wait_ge(s["ot_put"], i + 4)
                for t in range(4):
                    ins = pe.transpose(TB[0][:, t * P:(t + 1) * P], vT[:, t * P:(t + 1) * P], ident)
                ins.then_inc(s["v2_turned"], 1)
                pe.wait_ge(s["v2_home"], i + 1)

            with pe.Fori(0, 4) as i:
                scores(i)
                glu_tiles(i)
                pe.wait_ge(s["ot_put"], i)
                values(i)
            with pe.Fori(0, 4) as i:
                scores(i + 4)
                kv_tiles(i)
                values(i + 4)
            pe.wait_ge(s["k2_put"], 4)
            pe.wait_ge(s["ot_put"], NB)
            nat = [TB[0], TB[1], SM, TB[0], TB[1]]
            for t in range(TT):
                if t >= 3:
                    pe.wait_ge(s["knat_put"], t - 2)
                for hp in range(HP):
                    src = kP[:, hp, t * P:(t + 1) * P] if t < 4 else kTs[:, hp, :]
                    ins = pe.transpose(nat[t][0:tok(t), hp * P:(hp + 1) * P], src, ident)
                ins.then_inc(s["knat_done"], 1)
            pe.wait_ge(s["knat_put"], 3)
            pe.wait_ge(s["glus_put"], 1)
            for c in range(CT):
                ins = pe.transpose(SM[0:CW - 1, c * P:(c + 1) * P], glu[:, c, TP_:GX], ident)
            ins.then_inc(s["glun_done"], 1)
            pe.wait_ge(s["o_norm"], NB)
            for c in range(CT):
                ins = pe.transpose(OB[0:TS, c * P:(c + 1) * P], gluS[:, c, :], ident)
            ins.then_inc(s["glun_done"], 1)
            pe.wait_ge(s["conv_done"], CT)
            pe.wait_ge(s["knat_put"], TT)
            for half in range(2):
                for c in range(CT):
                    ins = pe.matmul(TB[half][:, 0:HALF], ones[:, :], conv[:, c, half * HALF:(half + 1) * HALF],
                                    start=(c == 0), stop=(c == CT - 1))
                ins.then_inc(s["st1_done"], 1)
            sb_ = [Z[0], Z[1], SC[0], SC[1]]
            pe.wait_ge(s["s_put"], 4 * NB)
            pe.wait_ge(s["v2_home"], 4)

            def s_head(h):
                hp, e = h // 2, h % 2
                for t in range(4):
                    if h:
                        pe.wait_ge(s["pexp"], 4 * (h - 1) + t + 1)
                    n = (t + 1) * P
                    pe.matmul(sb_[t][:, 0:n], qZ[:, hp, e, t * P:(t + 1) * P], kP[:, hp, 0:n],
                              start=True, stop=True).then_inc(s["ps_done"], 1)

            def t_head(h):
                pe.wait_ge(s["pnorm"], 4 * h + 4)
                for kb in range(4):
                    n = 4 * h + kb
                    if n >= 2:
                        pe.wait_ge(s["ptt_put"], n - 1)
                    for t in range(kb, 4):
                        ins = pe.transpose(TB[kb % 2][:, t * P:(t + 1) * P], pP[:, h % 2, t, kb * P:(kb + 1) * P], ident)
                    ins.then_inc(s["pt2_done"], 1)

            def pv_head(h):
                hp, e = h // 2, h % 2
                bank = (OB, SM)[hp % 2]
                if hp >= 2:
                    pe.wait_ge(s["o2_put"], hp - 1)
                else:
                    pe.wait_ge(s["glun_put"], 2)
                for kb in range(4):
                    pe.wait_ge(s["ptt_put"], 4 * h + kb + 1)
                    ins = pe.matmul(bank[64 * e:64 * e + 64, kb * P:TP_], vP[:, kb, h * DH:(h + 1) * DH],
                                    pPT[:, h % 2, kb, kb * P:TP_], start=(kb == 0), stop=(kb == 3))
                ins.then_inc(s["pv2_done"], 1)

            s_head(0)
            pe.wait_ge(s["mu_put"], 2)
            for h in range(H):
                if h + 1 < H:
                    s_head(h + 1)
                t_head(h)
                pv_head(h)
                if h == 2:
                    pe.wait_ge(s["sq_ready"], 1)
                    for half in range(2):
                        pe.wait_ge(s["ptt_put"], 4 * h + 4)
                        for c in range(CT):
                            ins = pe.matmul(TB[half][:, 0:HALF], ones[:, :], sq[:, c, half * HALF:(half + 1) * HALF],
                                            start=(c == 0), stop=(c == CT - 1))
                        ins.then_inc(s["st2_done"], 1)
                    pe.wait_ge(s["sd_put"], 2)
            pe.wait_ge(s["histf_loaded"], 16)
            pe.wait_ge(s["ptt_put"], 4 * H)
            for r in range(2):
                for f in range(FT_N):
                    g = r * FT_N + f
                    ins = pe.transpose(TB[r][:, f * 16:(f + 1) * 16], histF[0:16, g * P:(g + 1) * P], ident[0:16, 0:16])
                ins.then_inc(s["hf_done"], 1)
            pe.wait_ge(s["wpw_loaded"], 16)
            pe.wait_ge(s["c_ready"], 1)
            for m in range(CT):
                for half in range(2):
                    n = 2 * m + half
                    if n >= 4:
                        pe.wait_ge(s["pw_put"], n - 3)
                    for c in range(CT):
                        ins = pe.matmul(sb_[n % 4][:, 0:HALF], wpw[:, c, m * P:(m + 1) * P],
                                        conv[:, c, half * HALF:(half + 1) * HALF], start=(c == 0), stop=(c == CT - 1))
                    ins.then_inc(s["pw_done"], 1)
            pe.wait_ge(s["wo_loaded"], 16)
            pe.wait_ge(s["pw_put"], 2 * CT)
            pe.wait_ge(s["mix_put"], 1)
            pe.wait_ge(s["o2_put"], HP)
            turn2 = [TB[0], TB[1], OB, SM]
            pe.wait_ge(s["hf_put"], 2)

            def mix_tile(t):
                m = tok(t)
                for nh in range(2):
                    if t >= 2:
                        pe.wait_ge(s["t1_put"], 2 * (t - 2) + nh + 1)
                    for k in range(KC):
                        ins = pe.matmul(sb_[2 * (t % 2) + nh][0:m, :], mixT[:, k, t * P:t * P + m],
                                        wo[:, k, nh * TP_:(nh + 1) * TP_], start=(k == 0), stop=(k == KC - 1))
                    ins.then_inc(s["mo_done"], 1)

            def h2_tile(t):
                m = tok(t)
                pe.wait_ge(s["h2_ready"], t + 1)
                for j in range(2):
                    n = 2 * t + j
                    if n >= 4:
                        pe.wait_ge(s["h2_put"], n - 3)
                    for k in range(4):
                        ins = pe.transpose(turn2[n % 4][:, k * P:k * P + m], t1[0:m, t % 2, (4 * j + k) * P:(4 * j + k + 1) * P],
                                           ident[0:m, 0:m])
                    ins.then_inc(s["h2_done"], 1)

            mix_tile(0)
            for t in range(TT):
                if t + 1 < TT:
                    mix_tile(t + 1)
                h2_tile(t)
            wu_full = [s["wu_full0"], s["wu_full1"]]
            bank8 = sb_ + turn2
            pe.wait_ge(s["h2_put"], 2 * TT)
            pe.wait_ge(s["t1_put"], 2 * TT)
            with pe.Fori(0, FT_N // 2) as i:
                for slot in range(2):
                    pe.wait_ge(wu_full[slot], i * 32 + 32)
                    for u in range(2):
                        for half in range(2):
                            n = 2 * u + half
                            pe.wait_ge(s["ux_put"], i * 8 + (4 * slot + n + 1))
                            for k in range(KC):
                                ins = pe.matmul(bank8[4 * slot + n][:, 0:HALF], wu[slot][:, k, u, :],
                                                h2T[:, k, half * HALF:(half + 1) * HALF], start=(k == 0), stop=(k == KC - 1))
                            ins.then_inc(s["up_done"], 1)
            pe.wait_ge(s["last_put"], FT_N + 2)
            pe.wait_ge(s["ux_put"], 8 + 4 * FT_N)
            for n in range(11):
                if n >= 3:
                    pe.wait_ge(s["ul_put"], n - 2)
                for j in range(4):
                    g = 4 * n + j
                    ins = pe.transpose((TB[1], OB, SM)[n % 3][0:18, j * P:(j + 1) * P], last[:, g // FT_N, g % FT_N, :], ident)
                ins.then_inc(s["ul_done"], 1)
            pe.wait_ge(s["ft_ready"], FT_N)
            db = [[Z[0], Z[1], SC[0], SC[1], TB[0]], [TB[1], OB, SM, Z[0], Z[1]]]
            for n in range(FT_N):
                nh, kk = n // 11, n % 11
                pe.wait_ge(s[f"wd_full{n % 4}"], 16 * (n // 4 + 1))
                for k2 in range(2):
                    k = 2 * kk + k2
                    for t in range(TT):
                        m = tok(t)
                        if n == 11 and k2 == 0:
                            if t >= 3:
                                pe.wait_ge(s["y0_put"], t - 2)
                            else:
                                pe.wait_ge(s["ul_put"], 11)
                        ins = pe.matmul(db[nh][t][0:m, :], fT[:, k, t * P:t * P + m], wd[:, n % 4, k2, :],
                                        start=(k == 0), stop=(k == FT_N - 1))
                ins.then_inc(s["dn_done"], 1)

        @block.scalar
        def _(act):
            act.dma_start(consts[:], a["consts"]).then_inc(s["c_loaded"], 16)
            act.dma_start(bvB[0:TS, :], a["b_in_v"].partition_broadcast(TS)).then_inc(s["bv_loaded"], 16)
            act.dma_start(histN[0:120, :, :], a["state_cv"][0].rearrange("(r b) w n -> (b w) r n", r=2)).then_inc(s["hist_loaded"], 16)
            me = Steps(act, s["act_step"])
            act.wait_ge(s["x_loaded"], 32)
            act.wait_ge(s["pool_set"], 1)
            for t in range(TT):
                me.then(act.activation(junkA[0:tok(t), :], xA[0:tok(t), t, :], ACT.Square, accum_out=ss[0:tok(t), t:t + 1]))
            act.activation(rstd[:, 0:TT], ss[:, 0:TT], ACT.Sqrt, bias=epsr, scale=1.0 / D).then_inc(s["x_summed"], 1)
            act.wait_ge(s["c_loaded"], 16)
            for hp in range(HP):
                act.wait_ge(s["zq_done"], 2 * hp + 1)
                for e in range(2):
                    ins = act.activation(qZ[64 * e:64 * e + 64, hp, e, 0:HALF], Z[0][64 * e:64 * e + 64, 0:HALF], ACT.Identity,
                                         bias=b_in[64 * e:64 * e + 64, hp:hp + 1])
                ins.then_inc(s["zq_putA"], 1)
            gs = glu[:, :, GX:GLUW].rearrange("p c (b x) -> p c b x", b=NB)
            for r in range(2):
                act.wait_ge(s["hist_done"], r + 1)
                for c in range(CT):
                    ins = act.activation(gs[:, c, 4 * r:4 * r + 4, 0:CW - 1],
                                         (OB, SM)[r][:, c * 120:(c + 1) * 120].rearrange("p (b w) -> p b w", b=4), ACT.Copy)
                ins.then_inc(s["hist_put"], 1)
            act.wait_ge(s["ks_done"], 1)
            for hp in range(HP):
                ins = act.activation(kTs[:, hp, :], TB[0][:, hp * TS:(hp + 1) * TS], ACT.Identity, bias=b_in[:, 4 + hp:5 + hp])
            ins.then_inc(s["ks_put"], 1)

            qS4 = qS.rearrange("p c (q g) -> p c g q", g=4)

            def spread_q(b):
                act.wait_ge(s["own_done"], b)
                act.nop()
                for g in range(4):
                    ins = act.activation(qS4[32 * g:32 * g + 32, :, g, :],
                                         qR[32 * g:32 * g + 32, :, bass.ds(b * NT, NT)], ACT.Copy)
                ins.then_inc(s["qs_ready"], 1)

            act.wait_ge(s["qr_ready"], 1)
            spread_q(0)

            def put_scores(b):
                act.wait_ge(s["p_turned"], b * 4)
                act.wait_ge(s["vs_done"], 1)
                for j in range(4):
                    act.wait_ge(s["scores_done"], b * 4 + (j + 1))
                    act.activation(S[:, :, j * 256:(j + 1) * 256], SC[j % 2][:, :].rearrange("p (g k) -> p g k", g=2),
                                   ACT.Copy).then_inc(s["s_put"], 1)

            def exps(b):
                for g in range(2):
                    act.wait_ge(s["nb_ready"], b * 2 + (g + 1))
                    act.activation(S[:, g, :], S[:, g, :], ACT.Exp, bias=nb[:, g:g + 1], scale=SCALE,
                                   accum_out=rs[:, g:g + 1]).then_inc(s["probs_ready"], 1)
                for g in range(2):
                    ins = act.activation(ownS[:, g, :], ownS[:, g, :], ACT.Exp, bias=nb[:, g:g + 1], scale=SCALE,
                                         accum_out=rs[:, 2 + g:3 + g])
                ins.then_inc(s["probs_ready"], 1)

            def put_turned(b):
                act.wait_ge(s["pv_done"], b * 8)
                for n in range(4):
                    act.wait_ge(s["p_turned"], b * 4 + (n + 1))
                    act.activation(pT[:, n // 2, 4 * (n % 2):4 * (n % 2) + 4, :],
                                   TB[n % 2][:, :].rearrange("p (u r) -> p u r", u=4), ACT.Copy).then_inc(s["pt_put"], 1)
                act.wait_ge(s["own_turned"], b + 1)
                act.activation(pTo[0:TS, :, :], SM[0:TS, P:3 * P].rearrange("p (g r) -> p g r", g=2), ACT.Copy).then_inc(s["pto_put"], 1)

            def put_out(b):
                act.wait_ge(s["ot_done"], b + 1)
                act.nop()
                act.activation(oT[:, bass.ds(b, 1), :].rearrange("p a r -> p (a r)"), TB[0][:, 0:P], ACT.Copy).then_inc(s["ot_put"], 1)

            def glu_exps(i):
                act.wait_ge(s["g_exp"], i * 2)
                act.nop()
                act.activation(small[:, 31:32], nbg[:, bass.ds(i, 1)], ACT.Copy).then_inc(s["g_bias"], 1)
                act.wait_ge(s["g_bias"], i + 1)
                act.wait_ge(s["z1_put"], i * 2)
                for half in range(2):
                    act.wait_ge(s["z1_done"], i * 4 + (half + 1))
                    act.activation(sig[:, half * HALF:(half + 1) * HALF], Z[half][:, 0:HALF], ACT.Exp,
                                   bias=small[:, 31:32], scale=-1.0).then_inc(s["g_exp"], 1)

            def put_v(i):
                act.wait_ge(s["v2_done"], i + 1)
                act.wait_ge(s["nb_ready"], i * 2 + 10)
                act.nop()
                act.activation(vT[:, 0:TP_], Z[0][:, :], ACT.Identity, bias=b_in[:, bass.ds(i + 8, 1)]).then_inc(s["v2_put"], 1)

            def put_kv(i):
                act.wait_ge(s["k2_done"], i + 1)
                act.nop()
                act.activation(kP[:, bass.ds(i, 1), :].rearrange("p a t -> p (a t)"), Z[1][:, :], ACT.Identity,
                               bias=b_in[:, bass.ds(i + 4, 1)]).then_inc(s["k2_put"], 1)
                act.wait_ge(s["v2_turned"], i + 1)
                act.nop()
                act.activation(vP[:, 0:4, bass.ds(i * P, P)], TB[0][:, :].rearrange("p (t r) -> p t r", t=4),
                               ACT.Copy).then_inc(s["v2_home"], 1)

            with act.Fori(0, 4) as i:
                put_scores(i)
                glu_exps(i)
                exps(i)
                put_turned(i)
                put_out(i)
                spread_q(i + 1)
            with act.Fori(0, 3) as i:
                put_scores(i + 4)
                exps(i + 4)
                put_v(i)
                put_kv(i)
                put_turned(i + 4)
                put_out(i + 4)
                spread_q(i + 5)
            put_scores(7)
            exps(7)
            put_v(3)
            put_kv(3)
            put_turned(7)
            put_out(7)
            act.wait_ge(s["z1_put"], 8)
            act.wait_ge(s["own_done"], NB)
            act.activation(gluS.rearrange("p c (b t) -> p c b t", b=NB), gs[:, :, :, CW - 1:SX], ACT.Copy).then_inc(s["glus_put"], 1)
            nat = [TB[0], TB[1], SM, TB[0], TB[1]]
            act.wait_ge(s["pv_done"], SUPER * NB)
            act.wait_ge(s["scores_done"], 4 * NB)
            for t in range(TT):
                act.wait_ge(s["knat_done"], t + 1)
                act.activation(kNat[0:tok(t), t, :], nat[t][0:tok(t), :], ACT.Copy).then_inc(s["knat_put"], 1)
            for r in range(2):
                act.wait_ge(s["glun_done"], r + 1)
                n = (CW - 1, TS)[r]
                act.activation(cvN[0:n, r, :], (SM, OB)[r][0:n, :], ACT.Copy).then_inc(s["glun_put"], 1)
            act.wait_ge(s["knat_put"], TT)
            act.wait_ge(s["glun_put"], 2)
            act.wait_ge(s["v2_home"], 4)
            act.wait_ge(s["vs_put"], 1)
            rows = lambda n: a[n][0, 0].rearrange("(t p) h d -> p t (h d)", p=P)
            act.dma_start(rows("k_p"), kNat[:, 0:4, :]).then_inc(s["stored_kv"], 16)
            act.dma_start(rows("v_p"), vP[:, 0:4, :]).then_inc(s["stored_kv"], 16)
            act.dma_start(a["k_s"][0].rearrange("b t h d -> (b t) (h d)"), kNat[0:TS, 4, :]).then_inc(s["stored_kv"], 16)
            act.dma_start(a["v_s"][0].rearrange("b t h d -> (b t) (h d)"), vP[0:TS, 4, :]).then_inc(s["stored_kv"], 16)
            act.dma_start(a["cv_p"][0, 0], cvN[0:CW - 1, 0, :]).then_inc(s["stored_kv"], 16)
            act.dma_start(a["cv_s"][0][:, CW - 1 - NT:CW - 1, :], cvN[0:TS, 1, :]).then_inc(s["stored_kv"], 16)
            act.dma_start(a["cv_s"][0][:, 0:CW - 1 - NT, :], a["state_cv"][0][:, NT:CW - 1, :]).then_inc(s["stored_kv"], 16)
            for half in range(2):
                act.wait_ge(s["st1_done"], half + 1)
                act.activation(mu[:, half * HALF:(half + 1) * HALF], TB[half][:, 0:HALF], ACT.Copy, scale=1.0 / DA).then_inc(s["mu_put"], 1)
            sb_ = [Z[0], Z[1], SC[0], SC[1]]

            def p_exps(h):
                act.wait_ge(s["pnb_ready"], h + 1)
                if h >= 2:
                    act.wait_ge(s["pt2_done"], 4 * (h - 1))
                for t in range(4):
                    n = (t + 1) * P
                    j = 4 * (h % 2) + t
                    act.activation(pP[:, h % 2, t, 0:n], sb_[t][:, 0:n], ACT.Exp, bias=pnb[:, j:j + 1], scale=SCALE,
                                   accum_out=prs[:, j:j + 1]).then_inc(s["pexp"], 1)

            def p_turned(h):
                if h >= 2:
                    act.wait_ge(s["pv2_done"], h - 1)
                for kb in range(4):
                    act.wait_ge(s["pt2_done"], 4 * h + kb + 1)
                    act.activation(pPT[:, h % 2, kb, kb * P:TP_], TB[kb % 2][:, kb * P:TP_], ACT.Copy).then_inc(s["ptt_put"], 1)

            p_exps(0)
            for h in range(H):
                if h + 1 < H:
                    p_exps(h + 1)
                p_turned(h)
                if h == 2:
                    for half in range(2):
                        act.wait_ge(s["st2_done"], half + 1)
                        act.activation(sd[:, half * HALF:(half + 1) * HALF], TB[half][:, 0:HALF], ACT.Sqrt, bias=epsl,
                                       scale=1.0 / DA).then_inc(s["sd_put"], 1)
            act.wait_ge(s["ln_ready"], 1)
            act.activation(sq, conv, ACT.Sigmoid).then_inc(s["sg_put"], 1)
            for m in range(CT):
                for half in range(2):
                    n = 2 * m + half
                    act.wait_ge(s["pw_done"], n + 1)
                    act.activation(mixT[:, 4 + m, half * HALF:(half + 1) * HALF], sb_[n % 4][:, 0:HALF], ACT.Identity,
                                   bias=cst("b_pw")[:, m:m + 1]).then_inc(s["pw_put"], 1)
            act.wait_ge(s["pv2_done"], H)
            for t in range(TT):
                m = tok(t)
                for nh in range(2):
                    act.wait_ge(s["mo_done"], 2 * t + nh + 1)
                    if 2 * t + nh:
                        act.wait_ge(s["mo_sq"], 2 * t + nh)
                    if t and nh == 0:
                        act.wait_ge(s["x1_sq"], t)
                    act.activation(junk[0:m, 0:TP_], sb_[2 * (t % 2) + nh][0:m, :], ACT.Square,
                                   accum_out=ss2[0:m, 2 * t + nh:2 * t + nh + 1]).then_inc(s["mo_sq"], 1)
                act.wait_ge(s["mo_sum"], t + 1)
                act.activation(r2[0:m, t:t + 1], r2[0:m, t:t + 1], ACT.Sqrt, bias=epsr[0:m], scale=1.0 / D).then_inc(s["mo_rt"], 1)
                act.wait_ge(s["x1_ready"], t + 1)
                act.wait_ge(s["mo_sq"], 2 * t + 2)
                act.activation(junk[0:m, :], x1[0:m, t, :], ACT.Square, accum_out=ss3[0:m, t:t + 1]).then_inc(s["x1_sq"], 1)
                act.wait_ge(s["x1_sq"], t + 1)
                act.activation(r3[0:m, t:t + 1], ss3[0:m, t:t + 1], ACT.Sqrt, bias=epsr[0:m], scale=1.0 / D).then_inc(s["x1_rt"], 1)
            act.wait_ge(s["h2_put"], 2 * TT)
            act.wait_ge(s["mo_done"], 2 * TT)
            act.wait_ge(s["t1_put"], 2 * TT)
            bank8 = sb_ + [TB[0], TB[1], OB, SM]
            act.sem_inc(s["ux_put"], 8)
            with act.Fori(0, FT_N // 2) as i:
                for slot in range(2):
                    act.wait_ge(s["cv_done"], i * 2 + (slot + 1))
                    act.wait_ge(s["last_put"], i * 2 + (slot + 1))
                    for u in range(2):
                        for half in range(2):
                            n = 2 * u + half
                            act.wait_ge(s["up_done"], i * 8 + (4 * slot + n + 1))
                            bk = bank8[4 * slot + n]
                            if half == 0:
                                ins = act.activation(ux[:, slot, u, 2:2 + HALF], bk[:, 0:HALF], ACT.Copy)
                            else:
                                r = TP_ - HALF
                                act.activation(ux[:, slot, u, 2 + HALF:2 + TP_], bk[:, 0:r], ACT.Copy)
                                ins = act.activation(ux[:, slot, u, 2 + TP_:UXW].rearrange("p (b x) -> p b x", b=NB)[:, :, 2:UXS],
                                                     bk[:, r:HALF].rearrange("p (b t) -> p b t", b=NB), ACT.Copy)
                            ins.then_inc(s["ux_put"], 1)
                    act.wait_ge(s["g_conv"], i * 2 + (slot + 1))
                    act.activation(sg2[:, slot, :], cvo[:, slot, 0, :], ACT.Sigmoid).then_inc(s["g_sig"], 1)
            y_banks = [[Z[0], Z[1], SC[0], SC[1], TB[0]], [TB[1], OB, SM, Z[0], Z[1]]]
            for nh in range(2):
                act.wait_ge(s["dn_done"], 11 * (nh + 1))
                for t in range(TT):
                    m = tok(t)
                    if 5 * nh + t:
                        act.wait_ge(s["y_sq"], 5 * nh + t)
                    act.activation(junkY[0:m, :], y_banks[nh][t][0:m, :], ACT.Square,
                                   accum_out=ss2[0:m, 2 * t + nh:2 * t + nh + 1]).then_inc(s["y_sq"], 1)
            act.wait_ge(s["y_sum"], 1)
            act.activation(r2[:, 0:TT], r2[:, 0:TT], ACT.Sqrt, bias=epsr, scale=1.0 / D).then_inc(s["y_rt"], 1)

        @block.vector
        def _(dve):
            me = Steps(dve, s["dve_step"])
            dve.wait_ge(s["x_summed"], 1)
            me.then(dve.reciprocal(rstd[:, 0:TT], rstd[:, 0:TT]))
            for t in range(TT):
                dve.tensor_scalar(xA[0:tok(t), t, :], xA[0:tok(t), t, :], rstd[0:tok(t), t:t + 1], None, ALU.mult).then_inc(s["x_scaled"], 1)
            dve.wait_ge(s["c_loaded"], 16)
            dve.tensor_scalar(nbg, b_in[:, 16:20], -1.0, None, ALU.mult)
            turn = [TB[0], TB[1], SC[0], SC[1]]
            gpre = cst("g_pre")
            for t in range(TT):
                for j in range(2):
                    n = 2 * t + j
                    dve.wait_ge(s["xt_done"], n + 1)
                    m = tok(t)
                    dve.tensor_tensor(hT[:, 4 * j:4 * j + 4, t * P:t * P + m],
                                      turn[n % 4][:, :].rearrange("p (k t) -> p k t", k=4)[:, :, 0:m],
                                      gpre[:, 4 * j:4 * j + 4].unsqueeze(2).to_broadcast([P, 4, m]), ALU.mult).then_inc(s["ht_ready"], 1)
            dve.wait_ge(s["pool_set"], 1)
            for hp in range(HP):
                dve.wait_ge(s["zq_done"], 2 * hp + 2)
                for e in range(2):
                    dve.tensor_scalar(qZ[64 * e:64 * e + 64, hp, e, HALF:TP_], Z[1][64 * e:64 * e + 64, 0:TP_ - HALF],
                                      b_in[64 * e:64 * e + 64, hp:hp + 1], None, ALU.add)
                dve.tensor_scalar(qTs[:, hp, :], Z[1][:, TP_ - HALF:HALF], b_in[:, hp:hp + 1], None,
                                  ALU.add).then_inc(s["zq_putV"], 1)
            dve.wait_ge(s["zq_putV"], HP)
            qR5 = qR.rearrange("p (h x) t -> p h x t", x=4)
            for g in range(4):
                for x in range(4):
                    ins = dve.tensor_copy(qR5[32 * g:32 * g + 32, :, x, :], qTs[32 * x:32 * x + 32, :, :])
            ins.then_inc(s["qr_ready"], 1)
            dve.wait_ge(s["ks_put"], 1)
            kO5 = kOwn.rearrange("p (h x) t -> p h x t", x=4)
            for x in range(4):
                ins = dve.tensor_copy(kO5[0:32, :, x, :], kTs[32 * x:32 * x + 32, :, :])
            ins.then_inc(s["kown_put"], 1)
            dve.wait_ge(s["hist_done"], 2)

            def turn_k(b, u, first=False):
                dve.wait_ge(kn_full[u % 4], b * 128 + 64 * (u // 4 + 1))
                if u % 2 == 0 and not first:
                    dve.wait_ge(s["scores_done"], b * 4 + max(u // 2 - 1, 0))
                dve.transpose(kT[:, u % 4, :, :].rearrange("p c (i k) -> p i c k", i=4),
                              kN[:, u % 4, :, :].rearrange("p i (c k) -> p i c k", k=32)).then_inc(s["kt_ready"], 1)

            turn_k(0, 0, True)
            turn_k(0, 1, True)
            dve.wait_ge(s["vs_done"], 1)
            dve.wait_ge(s["bv_loaded"], 16)
            dve.tensor_tensor(vP[0:TS, 4, :], TB[1][0:TS, :], bvB[0:TS, :], ALU.add).then_inc(s["vs_put"], 1)
            dve.wait_ge(s["vs_put"], 1)
            turn_k(0, 2, True)
            turn_k(0, 3, True)

            SOFT = 18

            def softmax(b):
                me = Steps(dve, s["soft_step"], b * SOFT)
                S4 = S.rearrange("p g (n k) -> p (g n) k", k=64)
                for j in range(4):
                    dve.wait_ge(s["s_put"], b * 4 + (j + 1))
                    part = S[:, :, j * 256:(j + 1) * 256].rearrange("p g (n k) -> p g n k", k=64)
                    dve.tensor_reduce(bmax.rearrange("p (g n) -> p g n", g=2)[:, :, 4 * j:4 * j + 4], part, AX.X, ALU.max)
                    ins = dve.tensor_reduce(bsum.rearrange("p (g n) -> p g n", g=2)[:, :, 4 * j:4 * j + 4], part, AX.X, ALU.add)
                me.then(ins)

                def over_quads(src, dst, op):
                    me.then(dve.transpose(tA, src))
                    me.then(dve.tensor_reduce(tB[:, 0:8], tA.rearrange("p (q g) -> p q g", g=4), AX.X, op))
                    me.then(dve.tensor_copy(tC.rearrange("p (q g) -> p q g", g=4), tB[:, 0:8].unsqueeze(2).to_broadcast([P, 8, 4])))
                    me.then(dve.transpose(dst, tC))

                over_quads(bsum, bsum, ALU.add)
                t3 = bsum.rearrange("p (g n) -> p g n", g=2)
                for g in range(2):
                    ins = dve.tensor_tensor(rankv[:, g], t3[:, g].unsqueeze(1).to_broadcast([P, BLK, BLK]),
                                            t3[:, g].unsqueeze(2).to_broadcast([P, BLK, BLK]), ALU.subtract)
                me.then(ins)
                for g in range(2):
                    ins = dve.tensor_tensor(rankv[:, g], rankv[:, g], order, ALU.is_ge)
                me.then(ins)
                me.then(dve.tensor_reduce(pen, rank.rearrange("p (n m) -> p n m", m=BLK), AX.X, ALU.add))
                me.then(dve.tensor_scalar(pen, pen, float(TOPK), -BIG, ALU.is_ge, ALU.mult))
                me.then(dve.tensor_tensor(bmax, bmax, pen, ALU.add))
                me.then(dve.tensor_reduce(mx2[:, 0:2], bmax.rearrange("p (g n) -> p g n", g=2), AX.X, ALU.max))
                dve.wait_ge(s["own_done"], b + 1)
                dve.wait_ge(s["own_turned"], b)
                me.then(dve.tensor_tensor(ownS, own_ps, ownmask[:, bass.ds(b * -NT + (TS - NT), TS)].unsqueeze(1).to_broadcast([P, 2, TS]), ALU.add))
                me.then(dve.tensor_reduce(mx2[:, 2:4], ownS, AX.X, ALU.max))
                me.then(dve.tensor_tensor(mcol[:, 0:2], mx2[:, 0:2], mx2[:, 2:4], ALU.max))
                over_quads(mcol, bsum, ALU.max)
                dve.tensor_scalar(nb, bsum[:, 0:2], -SCALE, None, ALU.mult)
                for g in range(2):
                    dve.tensor_tensor(S4[:, BLK * g:BLK * g + BLK], S4[:, BLK * g:BLK * g + BLK],
                                      pen[:, BLK * g:BLK * g + BLK].unsqueeze(2).to_broadcast([P, BLK, 64]),
                                      ALU.add).then_inc(s["nb_ready"], 1)
                assert me.n == SOFT, me.n

            def row_sums(b):
                dve.wait_ge(s["probs_ready"], b * 3 + 3)
                dve.wait_ge(s["den_done"], b)
                dve.tensor_tensor(rsum, rs[:, 0:2], rs[:, 2:4], ALU.add).then_inc(s["rsum_ready"], 1)

            def norm_out(b):
                dve.wait_ge(s["pv_done"], b * 8 + 8)
                dve.reciprocal(rden, den_ps).then_inc(s["den_inv"], 1)
                dve.wait_ge(s["den_inv"], b + 1)
                dve.wait_ge(s["ot_done"], b)
                dve.tensor_scalar(oN[:, :], OB[:, 0:P], rden, None, ALU.mult).then_inc(s["o_norm"], 1)

            def glu_values(i):
                dve.wait_ge(s["g_exp"], i * 2 + 2)
                dve.tensor_scalar(sig, sig, 1.0, None, ALU.add).then_inc(s["sig_ready"], 1)
                dve.wait_ge(s["sig_ready"], i * 2 + 1)
                dve.reciprocal(sig, sig).then_inc(s["sig_ready"], 1)
                dve.wait_ge(s["sig_ready"], i * 2 + 2)
                gi = glu[:, bass.ds(i, 1), :].rearrange("p a x -> p (a x)")
                ba = b_in[:, bass.ds(i + 12, 1)]
                dve.wait_ge(s["z1_done"], i * 4 + 3)
                dve.scalar_tensor_tensor(gi[:, CW - 1:CW - 1 + HALF], Z[0][:, 0:HALF], ba, sig[:, 0:HALF],
                                         ALU.add, ALU.mult).then_inc(s["z1_put"], 1)
                dve.wait_ge(s["z1_done"], i * 4 + 4)
                r = TP_ - HALF
                dve.scalar_tensor_tensor(gi[:, CW - 1 + HALF:GX], Z[1][:, 0:r], ba, sig[:, HALF:TP_], ALU.add, ALU.mult)
                dve.scalar_tensor_tensor(gi[:, GX:GLUW].rearrange("p (b x) -> p b x", b=NB)[:, :, CW - 1:SX],
                                         Z[1][:, r:HALF].rearrange("p (b t) -> p b t", b=NB), ba,
                                         sig[:, TP_:TOK].rearrange("p (b t) -> p b t", b=NB),
                                         ALU.add, ALU.mult).then_inc(s["z1_put"], 1)

            def step(b, last=False, between=None):
                for u in range(4, 8):
                    turn_k(b, u)
                softmax(b)
                if not last:
                    turn_k(b + 1, 0)
                    turn_k(b + 1, 1)
                row_sums(b)
                if not last:
                    turn_k(b + 1, 2)
                    turn_k(b + 1, 3)
                if between:
                    between()
                norm_out(b)

            with dve.Fori(0, 4) as i:
                step(i, between=lambda: glu_values(i))
            with dve.Fori(0, 3) as i:
                step(i + 4)
            step(7, last=True)
            dve.wait_ge(s["ot_put"], NB)
            dve.wait_ge(s["k2_done"], 4)
            for e in range(2):
                for x in range(2):
                    row = slice(64 * e, 64 * e + 64)
                    src = oT[row].rearrange("p b (g x h q) -> p g b x h q", g=2, x=2, h=4)[:, :, :, x, 2 * x + e, :]
                    dst = mixT[row, 0:HP, TP_:TOK].rearrange("p (g x) (b q) -> p g x b q", x=2, b=NB)[:, :, x]
                    ins = dve.tensor_copy(dst, src)
            ins.then_inc(s["mix_put"], 1)
            sb_ = [Z[0], Z[1], SC[0], SC[1]]
            dve.wait_ge(s["k2_put"], 4)
            me = Steps(dve, s["pst_step"])

            def p_stats(h):
                j = 4 * (h % 2)
                for t in range(4):
                    dve.wait_ge(s["ps_done"], 4 * h + t + 1)
                    ins = dve.tensor_tensor(sb_[t][:, t * P:(t + 1) * P], sb_[t][:, t * P:(t + 1) * P], causal, ALU.add)
                me.then(ins)
                for t in range(4):
                    ins = dve.tensor_reduce(pm[:, j + t:j + t + 1], sb_[t][:, 0:(t + 1) * P], AX.X, ALU.max)
                me.then(ins)
                dve.tensor_scalar(pnb[:, j:j + 4], pm[:, j:j + 4], -SCALE, None, ALU.mult).then_inc(s["pnb_ready"], 1)

            def p_norms(h):
                j = 4 * (h % 2)
                dve.wait_ge(s["pexp"], 4 * h + 4)
                me.then(dve.reciprocal(prr[:, j:j + 4], prs[:, j:j + 4]))
                for t in range(4):
                    n = (t + 1) * P
                    dve.tensor_scalar(pP[:, h % 2, t, 0:n], pP[:, h % 2, t, 0:n], prr[:, j + t:j + t + 1], None,
                                      ALU.mult).then_inc(s["pnorm"], 1)

            def p_out(hp):
                dve.wait_ge(s["pv2_done"], 2 * hp + 2)
                dve.tensor_copy(mixT[:, hp, 0:TP_], (OB, SM)[hp % 2][:, :]).then_inc(s["o2_put"], 1)

            p_stats(0)
            for h in range(H):
                if h + 1 < H:
                    p_stats(h + 1)
                p_norms(h)
                if h % 2 == 0 and h:
                    p_out(h // 2 - 1)
                if h == 3:
                    dve.wait_ge(s["sd_put"], 2)
                    dve.reciprocal(sd, sd).then_inc(s["sd_inv"], 1)
            p_out(HP - 1)
            for r in range(2):
                dve.wait_ge(s["hf_done"], r + 1)
                if r == 0:
                    dve.wait_ge(s["ln_ready"], 1)
                    dve.wait_ge(s["sg_put"], 1)
                    dve.tensor_tensor(conv, conv, sq, ALU.mult).then_inc(s["c_ready"], 1)
                    dve.wait_ge(s["pw_done"], 2 * CT)
                dve.tensor_copy(histT[:, r, :, :], TB[r][:, 0:FT_N * 16].rearrange("p (f x) -> p f x", x=16)).then_inc(s["hf_put"], 1)
            dve.wait_ge(s["gpost_loaded"], 16)
            dve.wait_ge(s["xr_loaded"], 32)
            me2 = Steps(dve, s["mo_step"])
            turn2 = [TB[0], TB[1], OB, SM]
            gffn = cst("g_ffn")

            def put_h2(t):
                m = tok(t)
                for j in range(2):
                    n = 2 * t + j
                    dve.wait_ge(s["h2_done"], n + 1)
                    dve.tensor_tensor(h2T[:, 4 * j:4 * j + 4, t * P:t * P + m],
                                      turn2[n % 4][:, :].rearrange("p (k t) -> p k t", k=4)[:, :, 0:m],
                                      gffn[:, 4 * j:4 * j + 4].unsqueeze(2).to_broadcast([P, 4, m]), ALU.mult).then_inc(s["h2_put"], 1)

            for t in range(TT):
                m = tok(t)
                dve.wait_ge(s["mo_sq"], 2 * t + 2)
                dve.tensor_tensor(r2[0:m, t:t + 1], ss2[0:m, 2 * t:2 * t + 1], ss2[0:m, 2 * t + 1:2 * t + 2], ALU.add).then_inc(s["mo_sum"], 1)
                dve.wait_ge(s["mo_rt"], t + 1)
                me2.then(dve.reciprocal(r2[0:m, t:t + 1], r2[0:m, t:t + 1]))
                if t >= 2:
                    dve.wait_ge(s["h2_done"], 2 * (t - 2) + 2)
                for nh in range(2):
                    cols = slice(nh * TP_, (nh + 1) * TP_)
                    dve.scalar_tensor_tensor(t1[0:m, t % 2, cols], sb_[2 * (t % 2) + nh][0:m, :], r2[0:m, t:t + 1],
                                             gPost[0:m, cols], ALU.mult, ALU.mult).then_inc(s["t1_put"], 1)
                dve.wait_ge(s["t1_put"], 2 * t + 2)
                dve.tensor_tensor(x1[0:m, t, :], x1[0:m, t, :], t1[0:m, t % 2, :], ALU.add).then_inc(s["x1_ready"], 1)
                dve.wait_ge(s["x1_ready"], t + 1)
                if t:
                    put_h2(t - 1)
                dve.wait_ge(s["x1_rt"], t + 1)
                me2.then(dve.reciprocal(r3[0:m, t:t + 1], r3[0:m, t:t + 1]))
                dve.tensor_scalar(t1[0:m, t % 2, :], x1[0:m, t, :], r3[0:m, t:t + 1], None, ALU.mult).then_inc(s["h2_ready"], 1)
            put_h2(TT - 1)
            dve.sem_inc(s["cv_done"], 2)
            with dve.Fori(0, FT_N // 2) as i:
                for slot in range(2):
                    me3 = Steps(dve, s["f_step"], i * 10 + 5 * slot)
                    dve.wait_ge(s["taps_put"], i * 2 + (slot + 1))
                    for u in range(2):
                        dve.wait_ge(s["ux_put"], i * 8 + (8 + 4 * slot + 2 * u + 2))
                        src, dst = ux[:, slot, u, :], cvo[:, slot, u, :]
                        ps_in = src[:, 2 + TP_:UXW].rearrange("p (b x) -> p b x", b=NB)
                        ps_out = dst[:, TP_:TOK].rearrange("p (b t) -> p b t", b=NB)
                        w = wdw[:, slot, u, :]
                        dve.tensor_scalar(dst[:, 0:TP_], src[:, 0:TP_], w[:, 0:1], w[:, 3:4], ALU.mult, ALU.add)
                        me3.then(dve.tensor_scalar(ps_out, ps_in[:, :, 0:NT], w[:, 0:1], w[:, 3:4], ALU.mult, ALU.add))
                        for j in (1, 2):
                            dve.scalar_tensor_tensor(dst[:, 0:TP_], src[:, j:j + TP_], w[:, j:j + 1], dst[:, 0:TP_], ALU.mult, ALU.add)
                            ins = dve.scalar_tensor_tensor(ps_out, ps_in[:, :, j:j + NT], w[:, j:j + 1], ps_out, ALU.mult, ALU.add)
                            if j == 2:
                                ins.then_inc(s[("g_conv", "cv_done")[u]], 1)
                            else:
                                me3.then(ins)
                    dve.wait_ge(s["g_sig"], i * 2 + (slot + 1))
                    me3.then(dve.tensor_tensor(cvo[:, slot, 0, :], cvo[:, slot, 0, :], sg2[:, slot, :], ALU.mult))
                    dve.wait_ge(s["cv_done"], i * 2 + (slot + 3))
                    dve.tensor_tensor(fT[:, bass.ds(i * 2 + slot, 1), :].rearrange("p a t -> p (a t)"), cvo[:, slot, 0, :],
                                      cvo[:, slot, 1, :], ALU.mult).then_inc(s["ft_ready"], 1)
                    assert me3.n == 5, me3.n
            for n in range(11):
                dve.wait_ge(s["ul_done"], n + 1)
                dve.tensor_copy(histF[0:18, n * TP_:(n + 1) * TP_], (TB[1], OB, SM)[n % 3][0:18, :]).then_inc(s["ul_put"], 1)
            for t in range(TT):
                dve.wait_ge(s["y_sq"], t + 1)
                dve.tensor_copy(y0[0:tok(t), t, :], (Z[0], Z[1], SC[0], SC[1], TB[0])[t][0:tok(t), :]).then_inc(s["y0_put"], 1)
            dve.wait_ge(s["gffn_loaded"], 16)
            dve.wait_ge(s["y_sq"], 2 * TT)
            me4 = Steps(dve, s["y_step"])
            s2 = ss2[:, 0:2 * TT].rearrange("p (t n) -> p n t", n=2)
            dve.tensor_tensor(r2[:, 0:TT], s2[:, 0, :], s2[:, 1, :], ALU.add).then_inc(s["y_sum"], 1)
            dve.wait_ge(s["y_rt"], 1)
            me4.then(dve.reciprocal(r2[:, 0:TT], r2[:, 0:TT]))
            for t in range(TT):
                m = tok(t)
                if t >= 2:
                    dve.wait_ge(s[f"stored_y{t % 2}"], 16 * (t // 2))
                for nh in range(2):
                    src = y0[0:m, t, :] if nh == 0 else (TB[1], OB, SM, Z[0], Z[1])[t][0:m, :]
                    cols = slice(nh * TP_, (nh + 1) * TP_)
                    ins = dve.scalar_tensor_tensor(yo[0:m, t % 2, cols], src, r2[0:m, t:t + 1], gFfn[0:m, cols], ALU.mult, ALU.mult)
                me4.then(ins)
                dve.tensor_tensor(yo[0:m, t % 2, :], yo[0:m, t % 2, :], x1[0:m, t, :], ALU.add).then_inc(s["yo_ready"], 1)

        @block.gpsimd
        def _(pool):
            pool.memset(A[:, 0:4096], 0.0)
            pool.memset(vP[:, 4, :], 0.0)
            pool.memset(glu[:, :, 0:CW - 1], 0.0)
            pool.memset(qS, 0.0)
            pool.memset(kOwn, 0.0)
            pool.memset(small[:, :], 0.0).then_inc(s["pool_step"], 1)
            pool.memset(pTo_[:, :], 0.0)
            pool.wait_ge(s["pool_step"], 1)
            pool.memset(ss, 1.0)
            pool.memset(epsr, 1e-6)
            pool.memset(epsl, 1e-5)
            pool.memset(ones[:, :], 1.0).then_inc(s["pool_set"], 1)
            me = Steps(pool, s["conv_step"])
            pool.wait_ge(s["c_loaded"], 16)
            pool.wait_ge(s["hist_put"], 2)
            for i in range(CT):
                pool.wait_ge(s["z1_put"], 2 * i + 2)
                prod = conv[:, i + 1, :] if i + 1 < CT else sig
                gx = glu[:, i, GX:GLUW].rearrange("p (b x) -> p b x", b=NB)
                for j in range(CW):
                    w = w_cv[:, i, j:j + 1]
                    dst = prod if j else conv[:, i, :]
                    ds = dst[:, TP_:TOK].rearrange("p (b t) -> p b t", b=NB)
                    bias = [ALU.mult] if j else [ALU.mult, ALU.add]
                    b2 = None if j else w_cv[:, i, CW:CW + 1]
                    pool.tensor_scalar(dst[:, 0:TP_], glu[:, i, j:j + TP_], w, b2, *bias)
                    me.then(pool.tensor_scalar(ds, gx[:, :, j:j + NT], w, b2, *bias))
                    if j:
                        ins = pool.tensor_tensor(conv[:, i, :], conv[:, i, :], prod, ALU.add)
                        if j < CW - 1:
                            me.then(ins)
                ins.then_inc(s["conv_done"], 1)
                pool.wait_ge(s["conv_done"], i + 1)
            pool.wait_ge(s["conv_done"], CT)
            pool.wait_ge(s["mu_put"], 2)
            me.then(pool.tensor_tensor(conv, conv, mu.unsqueeze(1).to_broadcast([P, CT, TOK]), ALU.subtract))
            pool.tensor_tensor(sq, conv, conv, ALU.mult).then_inc(s["sq_ready"], 1)
            pool.wait_ge(s["sd_inv"], 1)
            me.then(pool.tensor_tensor(conv, conv, sd.unsqueeze(1).to_broadcast([P, CT, TOK]), ALU.mult))
            for c in range(CT):
                ins = pool.tensor_scalar(conv[:, c, :], conv[:, c, :], cst("g_ln")[:, c:c + 1], cst("b_ln")[:, c:c + 1], ALU.mult, ALU.add)
            ins.then_inc(s["ln_ready"], 1)
            pool.wait_ge(s["mo_done"], 2 * TT)
            pool.wait_ge(s["hf_put"], 2)
            pool.memset(ux[:, :, :, 0:2], 0.0)
            pool.sem_inc(s["last_put"], 2)
            with pool.Fori(0, FT_N // 2) as i:
                for slot in range(2):
                    f = i * 2 + slot
                    uh = ux[:, slot, :, 2 + TP_:UXW].rearrange("p u (b x) -> p u b x", b=NB)
                    pool.wait_ge(s["cv_done"], i * 2 + (slot + 1))
                    for u in range(2):
                        pool.tensor_copy(wdw[:, slot, u, :], dwv[:, u, bass.ds(f, 1), :].rearrange("p a j -> p (a j)"))
                        ins = pool.tensor_copy(uh[:, u, :, 0:2], histT[:, u, bass.ds(f, 1), :].rearrange("p a (b w) -> p (a b) w", w=2))
                    ins.then_inc(s["taps_put"], 1)
                    pool.wait_ge(s["ux_put"], i * 8 + (8 + 4 * slot + 4))
                    for u in range(2):
                        lu = last[:, u, bass.ds(f, 1), :].rearrange("p a x -> p (a x)")
                        pool.tensor_copy(lu[:, 0:2], ux[:, slot, u, TP_:TP_ + 2])
                        ins = pool.tensor_copy(lu[:, 2:18].rearrange("p (b w) -> p b w", w=2), uh[:, u, :, UXS - 2:UXS])
                    ins.then_inc(s["last_put"], 1)


def _tables():
    import numpy as np

    r = np.arange(P)
    ident = np.eye(P, dtype=np.float32)
    causal = np.where(r[None, :] <= r[:, None], 0.0, -BIG).astype(np.float32)
    h4, q, i = r // 32, (r // 4) % 8, r % 4
    key = np.arange(2 * TS) - (TS - NT)
    own = np.where((i[:, None] == 0) & (key[None] >= 0) & (key[None] <= q[:, None]), 0.0, -BIG)
    n = np.arange(BLK)
    order = np.where(n[None, :] < n[:, None], 0.0, np.finfo(np.float32).tiny).astype(np.float32)
    denmap = np.zeros((P, 2, P), np.float32)
    hp, h4o, qo = r // 32, (r // 8) % 4, r % 8
    for g in range(2):
        denmap[:, g] = (h4[:, None] == h4o[None]) & (q[:, None] == qo[None]) & (hp[None] // 2 == g)
    flat = [ident, causal, own, np.broadcast_to(order.reshape(1, -1), (P, BLK * BLK)),
            denmap.reshape(P, -1)]
    return [np.ascontiguousarray(x, np.float32) for x in flat]


def _columns(v):
    import numpy as np

    return np.ascontiguousarray(np.asarray(v).reshape(-1, P).T)


_OUTS = [((1, TP_, D), "float32"), ((NB, NT, D), "float32"), ((1, 1, TP_, H, DH), "float32"),
         ((1, 1, TP_, H, DH), "float32"), ((1, 1, CW - 1, DA), "float32"), ((1, 1, 2, 2 * DFF), "float32"),
         ((1, NB, NT, H, DH), "float32"), ((1, NB, NT, H, DH), "float32"), ((1, NB, CW - 1, DA), "float32"),
         ((1, NB, 2, 2 * DFF), "float32")]
OUT_NAMES = ["y_p", "y_s", "k_p", "v_p", "cv_p", "ffn_p", "k_s", "v_s", "cv_s", "ffn_s"]
PLAIN = ["x_prompt", "x_sample", "cache_k", "cache_v", "page_table", "state_cv", "state_ffn", "w_in", "w_cv_pw",
         "w_out", "g_post_mix", "w_up", "w_down", "g_post_ffn"]


def lay_out(inputs):
    import numpy as np

    arrays = {n: np.ascontiguousarray(inputs[n]) for n in PLAIN}
    arrays["b_in_v"] = np.ascontiguousarray(np.asarray(inputs["b_in"])[0, 2 * DA:3 * DA])
    cvw = np.concatenate([np.asarray(inputs["w_cv_dw"])[0], np.asarray(inputs["b_cv_dw"])], 0)
    cvw = cvw.reshape(CW + 1, CT, P).transpose(2, 1, 0).reshape(P, -1)
    taps = np.concatenate([np.asarray(inputs["w_ffn_dw"])[0], np.asarray(inputs["b_ffn_dw"])], 0)
    dw = taps.reshape(4, 44, P).transpose(2, 1, 0).reshape(P, -1)
    vec = [_columns(inputs["b_in"]), cvw] + [_columns(inputs[n]) for n in
           ("g_cv_ln", "b_cv_ln", "b_cv_pw", "g_pre_mix", "g_pre_ffn")] + [dw]
    arrays["consts"] = np.ascontiguousarray(np.concatenate(_tables() + vec, 1))
    return arrays


def kernel(**inputs):
    import numpy as np
    import concourse.bacc as bacc
    from concourse.bass_utils import run_bass_kernel_spmd

    nc = bacc.Bacc("TRN2", target_bir_lowering=False, num_devices=1, dynamic_dma_scratch_size=1024)
    arrays = {"in_" + n: x for n, x in lay_out(inputs).items()}
    a = {n[3:]: nc.dram_tensor(n, x.shape, mybir.dt.from_np(x.dtype), kind="ExternalInput").ap()
         for n, x in arrays.items()}
    for n, (shape, dtype) in zip(OUT_NAMES, _OUTS):
        a[n] = nc.dram_tensor("out_" + n, shape, mybir.dt.from_np(np.dtype(dtype)), kind="ExternalOutput").ap()
    build_layer(nc, a)
    r = run_bass_kernel_spmd(nc, [arrays], core_ids=[0])
    return tuple(r.results[0]["out_" + n] for n in OUT_NAMES)
```

```python
from contextlib import ExitStack

import concourse.bass as bass
from concourse import mybir

ALU = mybir.AluOpType
ACT = mybir.ActivationFunctionType
AX = mybir.AxisListType
F32 = mybir.dt.float32
F32R = mybir.dt.float32r
I32 = mybir.dt.int32
P = 128

D = 1024
KC = D // P
TP_ = 512
NB, NT = 8, 8
TS = NB * NT
TOK = TP_ + TS
HALF = TOK // 2
TT = 5
H, DH = 8, 64
HP = H // 2
DA = H * DH
PAGES, PAGE = 32, 128
SUPER = 8
BLK = 16
CW = 31
CT = 4
GX = (CW - 1) + TP_
SX = CW - 1 + NT
GLUW = GX + NB * SX
DFF = 2816
FT_N = DFF // P
UXS = 2 + NT
UXW = 2 + TP_ + NB * UXS
SCALE = DH ** -0.5
BIG = 1.0e30
TOPK = 3
START = 1
ST1_AFTER, ST2_AFTER = 2, 4

CONST = {}
_at = 0
for _n, _w in (("ident", 128), ("causal", 128), ("ownmask", 2 * TS), ("order", BLK * BLK), ("denmap", 256),
               ("b_in", 20), ("w_cv", CT * (CW + 1)), ("g_ln", CT), ("b_ln", CT), ("b_pw", CT),
               ("g_pre", KC), ("g_ffn", KC), ("dw", 44 * 4)):
    CONST[_n] = (_at, _w)
    _at += _w
NCONST = _at


def tok(t):
    return P if t < 4 else TS


class Steps:

    def __init__(self, eng, sem, base=0):
        self.eng, self.sem, self.base, self.n = eng, sem, base, 0

    def then(self, ins):
        self.n += 1
        ins.then_inc(self.sem, 1)
        self.eng.wait_ge(self.sem, self.base + self.n)


def build_layer(nc, a):
    ctx = ExitStack()
    with ctx:
        def sem(name):
            return ctx.enter_context(nc.semaphore(name))

        def sb(name, shape, dt=F32):
            return ctx.enter_context(nc.sbuf_tensor(name, shape, dt))

        consts = sb("consts", [P, NCONST])
        small = sb("small", [P, 384])
        ones = sb("ones", [P, P])
        pages = sb("pages", [1, NB * PAGES], I32)
        base = {}
        base["hT"] = nc.sbuf_base
        hT_ = sb("hT", [P, KC * TOK])
        base["A"] = nc.sbuf_base
        A = sb("A", [P, 19064])
        base["B"] = nc.sbuf_base
        B = sb("B", [P, 30720])

        def rounded(name, mem, off, *dims):
            start = base["hT" if mem is hT_ else "A" if mem is A else "B"]
            return nc.alloc_sbuf_tensor_at(name, [P, *dims], F32R, offset=start + 4 * off)

        def cst(name, rows=P):
            o, w = CONST[name]
            return consts[0:rows, o:o + w]

        def at(mem, off, *dims):
            n = 1
            for d in dims:
                n *= d
            v = mem[:, off:off + n]
            if len(dims) == 2:
                return v.rearrange("p (a b) -> p a b", a=dims[0])
            if len(dims) == 3:
                return v.rearrange("p (a b c) -> p a b c", a=dims[0], b=dims[1])
            if len(dims) == 4:
                return v.rearrange("p (a b c d) -> p a b c d", a=dims[0], b=dims[1], c=dims[2])
            return v

        ident = cst("ident")
        causal = cst("causal")
        ownmask = cst("ownmask")
        order = cst("order").rearrange("p (n m) -> p n m", n=BLK)
        denmap = cst("denmap").rearrange("p (g r) -> p g r", g=2)
        b_in = cst("b_in")
        w_cv = cst("w_cv").rearrange("p (c j) -> p c j", c=CT)
        dwv = cst("dw").rearrange("p (u f j) -> p u f j", u=2, f=FT_N)

        hT = hT_[:, :].rearrange("p (k t) -> p k t", k=KC)
        mixT = hT
        qZ = at(A, 0, HP, 2, TP_)
        kP = at(A, 4096, HP, TP_)
        vP = at(A, 6144, TT, DA)
        glu = at(A, 8704, CT, GLUW)
        conv = at(A, 12088, CT, TOK)
        oT = at(A, 14392, NB, P)
        qR = at(A, 15416, 2 * H, TS)
        qS = at(A, 16440, 2 * H, 32)
        kTs = at(A, 16952, HP, TS)
        kOwn = at(A, 17208, 2 * H, TS)
        sig = at(A, 18232, TOK)
        qTs = at(A, 18232, HP, TS)
        kN = at(B, 0, 4, 4, DA)
        kT = at(B, 8192, 4, 2 * H, P)
        vN = at(B, 16384, 4, 4, DA)
        wz = at(B, 24576, KC, 2, P)
        S = at(B, 26624, 2, 1024)
        pT = at(B, 28672, 2, SUPER, P)
        rank = at(B, 28672, 2 * BLK * BLK)
        rankv = rank.rearrange("p (g n m) -> p g n m", g=2, n=BLK)
        vT = at(B, 28672, TP_)
        xA = at(B, 8192, TT, D)
        junkA = at(B, 13312, D)
        histN = at(B, 14336, 2, DA)
        bvB = at(B, 15360, DA)
        wq = at(B, 16384, KC, DA)
        wv = wq
        wk = at(B, 26624, KC, DA)
        pP = at(B, 0, 2, 4, TP_)
        pPT = at(B, 4096, 2, 4, TP_)
        x1 = at(B, 8192, TT, D)
        kNat = at(B, 13312, TT, DA)
        wpw = at(B, 15872, CT, DA)
        gPost = at(B, 17920, D)
        cvN = at(B, 18944, 2, DA)
        mu = at(B, 19968, TOK)
        sd = at(B, 20544, TOK)
        sq = at(B, 21120, CT, TOK)
        histF = at(B, 24576, 2 * DFF)
        gluS = at(A, 17208, CT, TS)
        wo = at(B, 0, KC, D)
        t1 = at(A, 0, 2, D)
        junk = at(A, 2048, D)
        h2raw = at(A, 3072, 2, TP_)
        h2hi = rounded("h2hi", A, 14392, KC, TOK)
        h2lo = rounded("h2lo", B, 24576, KC, TOK)
        fT = at(A, 0, FT_N, TOK)
        histT = at(A, 12672, 2, FT_N, 16)
        last = at(A, 13376, 2, FT_N, 18)
        ux = at(B, 0, 2, 2, UXW)
        cvo = at(B, 2376, 2, 2, TOK)
        sg2 = at(B, 4680, 2, TOK)
        wu = [at(B, 13312 + 2048 * i, KC, 2, P) for i in range(2)]
        wuhi = rounded("wuhi", hT_, 0, 2, KC, 2 * P)
        wulo = rounded("wulo", B, 19968, 2, KC, 2 * P)
        wd = at(B, 5832, 2, 2, TP_)
        wdhi = rounded("wdhi", hT_, 0, 2, 2, TP_)
        wdlo = rounded("wdlo", hT_, 2048, 2, 2, TP_)
        fThi = rounded("fThi", A, 14392, 2, 2, TOK)
        fTlo = rounded("fTlo", A, 14392 + 4 * TOK, 2, 2, TOK)
        gFfn = at(B, 18944, D)
        y0 = at(B, 0, TT, TP_)
        yo = at(B, 2560, 2, D)
        junkY = at(B, 4680, TP_)
        ss = small[:, 0:8]
        rstd = small[:, 8:16]
        bsum, bmax, pen, tA, tB, tC = (small[:, 32 + 32 * i:64 + 32 * i] for i in range(6))
        mcol = small[:, 224:256]
        nb = small[:, 16:18]
        rs = small[:, 18:22]
        rsum = small[:, 22:24]
        rden = small[:, 24:25]
        nbg = small[:, 25:29]
        epsr = small[:, 29:30]
        epsl = small[:, 30:31]
        mx2 = small[:, 256:260]
        pm = small[:, 260:268]
        pnb = small[:, 268:276]
        prs = small[:, 276:284]
        prr = small[:, 284:292]
        ss2 = small[:, 292:312]
        r2 = small[:, 312:332]
        wdw = at(small, 332, 2, 2, 4)
        ss3 = small[:, 348:364]
        r3 = small[:, 364:372]
        own = sb("own", [P, 2 * TS])
        ownS = own[:, :].rearrange("p (g k) -> p g k", g=2)
        pTo_ = sb("pTo", [P, 2 * P])
        pTo = pTo_[:, :].rearrange("p (g r) -> p g r", g=2)
        oN = sb("oN", [P, P])

        banks = {n: ctx.enter_context(nc.psum_tensor(n, [P, 512], F32))
                 for n in ("z0", "z1", "sc0", "sc1", "tp0", "tp1", "ob", "sm")}
        Z = [banks["z0"], banks["z1"]]
        SC = [banks["sc0"], banks["sc1"]]
        TB = [banks["tp0"], banks["tp1"]]
        OB, SM = banks["ob"], banks["sm"]
        own_ps = SM[:, 0:128].rearrange("p (g k) -> p g k", g=2)
        den_ps = OB[:, 384:385]

        names = """c_loaded x_loaded pt_loaded hist_loaded bv_loaded wq_loaded wk_loaded wv_loaded
            pool_set x_summed x_scaled xt_done ht_ready hist_done hist_put zq_done zq_putA zq_putV
            ks_done ks_put kown_put vs_done vs_put qr_ready qs_ready act_step dve_step pool_step
            kn_full0 kn_full1 kn_full2 kn_full3 v_full0 v_full1 v_full2 v_full3 kt_ready scores_done s_put own_done
            soft_step nb_ready probs_ready rsum_ready p_turned pt_put own_turned pto_put den_done
            pv_done den_inv o_norm ot_done ot_put wz_full z1_done g_exp sig_ready g_bias z1_put
            v2_done v2_put v2_turned v2_home k2_done k2_put
            xr_loaded wpw_loaded gpost_loaded histf_loaded wo_loaded wu_full0 wu_full1 wd_full0 wd_full1 h2_raw h2_hi wu_hi wu_lo wd_hi wd_lo ft_hi ft_lo
            gffn_loaded knat_done knat_put glus_put glun_done glun_put st1_done mu_put sq_ready st2_done sd_put sd_inv
            ln_ready sg_put c_ready ps_done pst_step pnb_ready pexp pr_step pnorm pt2_done ptt_put pv2_done o2_put
            mix_put pw_done pw_put hf_done hf_put mo_done mo_sq mo_sum mo_rt mo_step t1_put x1_ready x1_sq x1_step h2_ready h2_done
            h2_put up_done ux_put taps_put hist_in last_put cv_done g_sig ft_ready f_step ul_done ul_put dn_done y_sq
            y0_put y_step y_sum y_rt x1_rt g_conv conv_step yo_ready stored_kv stored_ffn stored_y0 stored_y1 conv_done""".split()
        s = {n: sem(n) for n in names}
        block = ctx.enter_context(nc.Block())

        w_in = a["w_in"][0].rearrange("(k p) n -> p k n", p=P)
        ck = a["cache_k"][0].rearrange("f k h d -> f k (h d)")
        cv = a["cache_v"][0].rearrange("f k h d -> f k (h d)")
        kn_full = [s[f"kn_full{i}"] for i in range(4)]
        v_full = [s[f"v_full{i}"] for i in range(4)]

        @block.sync
        def _(sp):
            sp.dma_start(pages[:], a["page_table"].rearrange("(o b) n -> o (b n)", o=1)).then_inc(s["pt_loaded"], 16)
            sp.dma_start(xA[:, 0:4, :], a["x_prompt"][0].rearrange("(t p) n -> p t n", p=P)).then_inc(s["x_loaded"], 16)
            sp.dma_start(xA[0:TS, 4, :], a["x_sample"].rearrange("b t n -> (b t) n")).then_inc(s["x_loaded"], 16)
            sp.dma_start(wq, w_in[:, :, 0:DA]).then_inc(s["wq_loaded"], 16)
            sp.dma_start(wk, w_in[:, :, DA:2 * DA]).then_inc(s["wk_loaded"], 16)
            sp.wait_ge(s["pt_loaded"], 16)

            def page_numbers(b, u):
                _, numbers = nc.values_load_multi_w_load_instructions(
                    pages[0:1, bass.ds(b * PAGES + 4 * u, 4)], engines=[mybir.EngineType.SP], min_val=0,
                    max_val=ck.shape[0] - 1)
                return numbers

            def load_k(b, u):
                for i, pg in enumerate(page_numbers(b, u)):
                    sp.dma_start(kN[:, u % 4, i, :], ck[bass.ds(pg, 1)].rearrange("a k n -> (a k) n")).then_inc(kn_full[u % 4], 16)

            def load_v(b, u):
                for i, pg in enumerate(page_numbers(b, u)):
                    sp.dma_start(vN[32 * i:32 * i + 32, u % 4, :, :],
                                 cv[bass.ds(pg, 1)].rearrange("a (g r) n -> (a r) g n", g=4)).then_inc(v_full[u % 4], 16)

            for u in range(4):
                load_k(0, u)
            sp.wait_ge(s["zq_done"], 2 * HP)
            sp.dma_start(wv, w_in[:, :, 2 * DA:3 * DA]).then_inc(s["wv_loaded"], 16)
            for u in range(4, 8):
                sp.wait_ge(s["kt_ready"], u - 3)
                load_k(0, u)

            def wz_glu(i):
                sp.dma_start(wz[:, :, 0, :], w_in[:, :, bass.ds(4 * DA + i * P, P)]).then_inc(s["wz_full"], 16)
                sp.dma_start(wz[:, :, 1, :], w_in[:, :, bass.ds(3 * DA + i * P, P)]).then_inc(s["wz_full"], 16)

            def wz_kv(i):
                sp.dma_start(wz[:, :, 0, :], w_in[:, :, bass.ds(2 * DA + i * P, P)]).then_inc(s["wz_full"], 16)
                sp.dma_start(wz[:, :, 1, :], w_in[:, :, bass.ds(DA + i * P, P)]).then_inc(s["wz_full"], 16)

            def step(b, last, load_w):
                load_w()
                sp.wait_ge(s["pv_done"], b * 8 + START)
                for u in range(4):
                    load_v(b, u)
                if not last:
                    for u in range(6):
                        sp.wait_ge(s["kt_ready"], b * 8 + (8 + u - 3))
                        load_k(b + 1, u)
                for u in range(4, 8):
                    sp.wait_ge(s["pv_done"], b * 8 + (u - 3) + START)
                    load_v(b, u)
                if not last:
                    for u in (6, 7):
                        sp.wait_ge(s["kt_ready"], b * 8 + (8 + u - 3))
                        load_k(b + 1, u)

            sp.wait_ge(s["vs_done"], 1)

            def w1(i):
                sp.wait_ge(s["z1_done"], i * 4 + START)
                wz_glu(i)

            def w2(i):
                sp.wait_ge(s["z1_done"], 16 + START)
                sp.wait_ge(s["k2_done"], i + START)
                wz_kv(i)

            with sp.Fori(0, 4) as i:
                step(i, False, lambda: w1(i))
            with sp.Fori(0, 3) as i:
                step(i + 4, False, lambda: w2(i))
            step(7, True, lambda: w2(3))
            sp.wait_ge(s["scores_done"], 4 * NB)
            sp.wait_ge(s["p_turned"], 4 * NB + START)
            sp.wait_ge(s["pv_done"], SUPER * NB + START)
            sp.dma_start(wpw, a["w_cv_pw"][0].rearrange("(k p) n -> p k n", p=P)).then_inc(s["wpw_loaded"], 16)
            sp.dma_start(x1[:, 0:4, :], a["x_prompt"][0].rearrange("(t p) n -> p t n", p=P)).then_inc(s["xr_loaded"], 16)
            sp.dma_start(x1[0:TS, 4, :], a["x_sample"].rearrange("b t n -> (b t) n")).then_inc(s["xr_loaded"], 16)
            sp.dma_start(gPost, a["g_post_mix"][0].partition_broadcast(P)).then_inc(s["gpost_loaded"], 16)
            sp.dma_start(histF[0:16, :], a["state_ffn"][0].rearrange("b w n -> (b w) n")).then_inc(s["histf_loaded"], 16)
            sp.wait_ge(s["pv2_done"], H)
            sp.dma_start(wo, a["w_out"][0].rearrange("(k p) n -> p k n", p=P)).then_inc(s["wo_loaded"], 16)
            w_up = a["w_up"][0].rearrange("(k p) n -> p k n", p=P)
            wu_full = [s["wu_full0"], s["wu_full1"]]

            def load_up(f, slot):
                for u in range(2):
                    sp.dma_start(wu[slot][:, :, u, :], w_up[:, :, bass.ds(f * P + u * DFF, P)]).then_inc(wu_full[slot], 16)

            sp.wait_ge(s["pw_done"], 2 * CT)
            sp.wait_ge(s["stored_kv"], 16 * 7)
            load_up(0, 0)
            load_up(1, 1)
            sp.dma_start(gFfn, a["g_post_ffn"][0].partition_broadcast(P)).then_inc(s["gffn_loaded"], 16)
            with sp.Fori(0, FT_N // 2 - 1) as i:
                for slot in range(2):
                    sp.wait_ge(s["wu_lo"], i * 2 + (slot + 1))
                    load_up(i * 2 + (2 + slot), slot)
            w_dn = a["w_down"][0].rearrange("(k p) n -> p k n", p=P)
            wd_full = [s["wd_full0"], s["wd_full1"]]

            def load_down(nh, kk, slot):
                sp.dma_start(wd[:, slot, :, :], w_dn[:, bass.ds(kk * 2, 2), nh * TP_:(nh + 1) * TP_]).then_inc(wd_full[slot], 16)

            load_down(0, 0, 0)
            load_down(0, 1, 1)
            with sp.Fori(0, 4) as i:
                for j in range(2):
                    sp.wait_ge(s["wd_lo"], i * 2 + (j + 1))
                    load_down(0, i * 2 + (2 + j), j)
            sp.wait_ge(s["wd_lo"], 9)
            load_down(0, 10, 0)
            with sp.Fori(0, 5) as i:
                for j in range(2):
                    sp.wait_ge(s["wd_lo"], i * 2 + (10 + j))
                    load_down(1, i * 2 + j, 1 - j)
            sp.wait_ge(s["wd_lo"], 20)
            load_down(1, 10, 1)
            sp.wait_ge(s["ul_put"], 11)
            sp.dma_start(a["ffn_p"][0, 0], histF[0:2, :]).then_inc(s["stored_ffn"], 16)
            sp.dma_start(a["ffn_s"][0].rearrange("b w n -> (b w) n"), histF[2:18, :]).then_inc(s["stored_ffn"], 16)
            for t in range(TT):
                sp.wait_ge(s["yo_ready"], t + 1)
                dst = a["y_p"][0, t * P:(t + 1) * P, :] if t < 4 else a["y_s"].rearrange("b t n -> (b t) n")
                sp.dma_start(dst, yo[0:tok(t), t % 2, :]).then_inc(s[f"stored_y{t % 2}"], 16)
            sp.wait_ge(s["stored_ffn"], 32)
            sp.wait_ge(s["stored_y0"], 16 * 3)
            sp.wait_ge(s["stored_y1"], 16 * 2)

        @block.tensor
        def _(pe):
            for n in ("up_done", "z1_done", "pv_done", "k2_done", "p_turned", "own_turned", "den_done", "ot_done"):
                pe.sem_inc(s[n], START)
            pe.wait_ge(s["c_loaded"], 16)
            pe.wait_ge(s["pool_set"], 1)
            turn = [TB[0], TB[1], SC[0], SC[1]]
            for t in range(TT):
                pe.wait_ge(s["x_scaled"], t + 1)
                for j in range(2):
                    n = 2 * t + j
                    if n >= 4:
                        pe.wait_ge(s["ht_ready"], n - 3)
                    for k in range(4):
                        ins = pe.transpose(turn[n % 4][:, k * P:k * P + tok(t)],
                                           xA[0:tok(t), t, (4 * j + k) * P:(4 * j + k + 1) * P],
                                           ident[0:tok(t), 0:tok(t)])
                    ins.then_inc(s["xt_done"], 1)
            pe.wait_ge(s["ht_ready"], 2 * TT)
            pe.wait_ge(s["wq_loaded"], 16)
            for hp in range(HP):
                for half in range(2):
                    if hp:
                        pe.wait_ge((s["zq_putA"], s["zq_putV"])[half], hp)
                    for k in range(KC):
                        ins = pe.matmul(Z[half][:, 0:HALF], wq[:, k, hp * P:(hp + 1) * P],
                                        hT[:, k, half * HALF:(half + 1) * HALF], start=(k == 0), stop=(k == KC - 1))
                    ins.then_inc(s["zq_done"], 1)
            pe.wait_ge(s["hist_loaded"], 16)
            for r in range(2):
                for c in range(CT):
                    ins = pe.transpose((OB, SM)[r][:, c * 120:(c + 1) * 120], histN[0:120, r, c * P:(c + 1) * P],
                                       ident[0:120, 0:120])
                ins.then_inc(s["hist_done"], 1)
            pe.wait_ge(s["wk_loaded"], 16)
            for hp in range(HP):
                for k in range(KC):
                    ins = pe.matmul(TB[0][:, hp * TS:(hp + 1) * TS], wk[:, k, hp * P:(hp + 1) * P],
                                    hT[:, k, TP_:TOK], start=(k == 0), stop=(k == KC - 1))
            ins.then_inc(s["ks_done"], 1)
            pe.wait_ge(s["wv_loaded"], 16)
            for k in range(KC):
                ins = pe.matmul(TB[1][0:TS, :], hT[:, k, TP_:TOK], wv[:, k, :], start=(k == 0), stop=(k == KC - 1))
            ins.then_inc(s["vs_done"], 1)

            def scores(b):
                pe.wait_ge(s["qs_ready"], b + 1)
                for j in range(4):
                    pe.wait_ge(s["kt_ready"], b * 8 + (2 * j + 2))
                    pe.wait_ge(s["s_put"], b * 4 + max(j - 1, 0) + START)
                    for g in range(2):
                        for c in range(2):
                            for h4 in range(4):
                                hc = 2 * (4 * g + h4) + c
                                ins = pe.matmul(SC[j % 2][32 * h4:32 * h4 + 32, g * 256:(g + 1) * 256]
                                                .rearrange("p (a k) -> p a k", a=2),
                                                qS[:, hc, :], kT[:, 2 * (j % 2):2 * (j % 2) + 2, hc, :],
                                                start=(c == 0), stop=(c == 1))
                    ins.then_inc(s["scores_done"], 1)
                for g in range(2):
                    for c in range(2):
                        for h4 in range(4):
                            hc = 2 * (4 * g + h4) + c
                            ins = pe.matmul(SM[32 * h4:32 * h4 + 32, g * TS:(g + 1) * TS], qS[:, hc, :], kOwn[:, hc, :],
                                            start=(c == 0), stop=(c == 1))
                ins.then_inc(s["own_done"], 1)

            def values(b):
                for n in range(4):
                    g, quad = n // 2, n % 2
                    pe.wait_ge(s["probs_ready"], b * 3 + (g + 1 if n < 3 else 3))
                    pe.wait_ge(s["pt_put"], b * 4 + max(n - 1, 0) + START)
                    for u in range(4):
                        v = 4 * quad + u
                        ins = pe.transpose(TB[n % 2][:, u * P:(u + 1) * P], S[:, g, v * P:(v + 1) * P], ident)
                    ins.then_inc(s["p_turned"], 1)
                for g in range(2):
                    ins = pe.transpose(SM[0:TS, P + g * P:P + (g + 1) * P], ownS[:, g, :], ident)
                ins.then_inc(s["own_turned"], 1)
                pe.wait_ge(s["rsum_ready"], b + 1)
                pe.wait_ge(s["o_norm"], b + START)
                for g in range(2):
                    ins = pe.matmul(den_ps, denmap[:, g, :], rsum[:, g:g + 1], start=(g == 0), stop=(g == 1))
                ins.then_inc(s["den_done"], 1)
                pe.wait_ge(s["pto_put"], b + 1)
                pTo4 = pTo.rearrange("p g (r i) -> p g i r", i=4)
                for hp in range(HP):
                    pe.matmul(OB[32 * hp:32 * hp + 32, 0:P], pTo4[:, hp // 2, 0, :], vP[:, 4, hp * P:(hp + 1) * P],
                              start=True, stop=False)
                for u in range(SUPER):
                    pe.wait_ge(v_full[u % 4], b * 128 + 64 * (u // 4 + 1))
                    if u == 0:
                        pe.wait_ge(s["pt_put"], b * 4 + 4 + START)
                    for i in range(4):
                        for hp in range(HP):
                            w = pT[:, hp // 2, u, :].rearrange("p (r i) -> p i r", i=4)[:, i, :]
                            ins = pe.matmul(OB[32 * hp:32 * hp + 32, 0:P], w, vN[:, u % 4, i, hp * P:(hp + 1) * P],
                                            start=False, stop=(u == SUPER - 1 and i == 3))
                    ins.then_inc(s["pv_done"], 1)
                pe.wait_ge(s["o_norm"], b + 1 + START)
                pe.wait_ge(s["pt_put"], b * 4 + 4 + START)
                pe.transpose(TB[0][:, 0:P], oN[:, :], ident).then_inc(s["ot_done"], 1)

            def glu_tiles(i):
                pe.wait_ge(s["wz_full"], i * 32 + 32)
                for n in range(4):
                    u, half = n // 2, n % 2
                    if u:
                        pe.wait_ge(s["g_exp"], i * 2 + (half + 1) + START)
                    else:
                        pe.wait_ge(s["z1_put"], i * 2 + START)
                    for k in range(KC):
                        ins = pe.matmul(Z[half][:, 0:HALF], wz[:, k, u, :], hT[:, k, half * HALF:(half + 1) * HALF],
                                        start=(k == 0), stop=(k == KC - 1))
                    ins.then_inc(s["z1_done"], 1)

            def kv_tiles(i):
                pe.wait_ge(s["wz_full"], i * 32 + 160)
                pe.wait_ge(s["z1_put"], 8 + START)
                pe.wait_ge(s["v2_put"], i + START)
                for k in range(KC):
                    ins = pe.matmul(Z[0][:, 0:TP_], wz[:, k, 0, :], hT[:, k, 0:TP_], start=(k == 0), stop=(k == KC - 1))
                ins.then_inc(s["v2_done"], 1)
                pe.wait_ge(s["k2_put"], i + START)
                for k in range(KC):
                    ins = pe.matmul(Z[1][:, 0:TP_], wz[:, k, 1, :], hT[:, k, 0:TP_], start=(k == 0), stop=(k == KC - 1))
                ins.then_inc(s["k2_done"], 1)
                pe.wait_ge(s["v2_put"], i + 1 + START)
                pe.wait_ge(s["ot_put"], i + 4 + START)
                for t in range(4):
                    ins = pe.transpose(TB[0][:, t * P:(t + 1) * P], vT[:, t * P:(t + 1) * P], ident)
                ins.then_inc(s["v2_turned"], 1)
                pe.wait_ge(s["v2_home"], i + 1)

            with pe.Fori(0, 4) as i:
                scores(i)
                glu_tiles(i)
                pe.wait_ge(s["ot_put"], i + START)
                values(i)
            with pe.Fori(0, 4) as i:
                scores(i + 4)
                kv_tiles(i)
                values(i + 4)
            pe.wait_ge(s["k2_put"], 4 + START)
            pe.wait_ge(s["ot_put"], NB + START)
            nat = [TB[0], TB[1], SM, TB[0], TB[1]]
            for t in range(TT):
                if t >= 3:
                    pe.wait_ge(s["knat_put"], t - 2)
                for hp in range(HP):
                    src = kP[:, hp, t * P:(t + 1) * P] if t < 4 else kTs[:, hp, :]
                    ins = pe.transpose(nat[t][0:tok(t), hp * P:(hp + 1) * P], src, ident)
                ins.then_inc(s["knat_done"], 1)
            pe.wait_ge(s["knat_put"], 3)
            pe.wait_ge(s["glus_put"], 1)
            for c in range(CT):
                ins = pe.transpose(SM[0:CW - 1, c * P:(c + 1) * P], glu[:, c, TP_:GX], ident)
            ins.then_inc(s["glun_done"], 1)
            pe.wait_ge(s["o_norm"], NB + START)
            for c in range(CT):
                ins = pe.transpose(OB[0:TS, c * P:(c + 1) * P], gluS[:, c, :], ident)
            ins.then_inc(s["glun_done"], 1)
            pe.wait_ge(s["knat_put"], TT)
            sb_ = [Z[0], Z[1], SC[0], SC[1]]
            pe.wait_ge(s["s_put"], 4 * NB + START)
            pe.wait_ge(s["v2_home"], 4)

            def s_head(h):
                hp, e = h // 2, h % 2
                for t in range(4):
                    if h:
                        pe.wait_ge(s["pexp"], 4 * (h - 1) + t + 1)
                    n = (t + 1) * P
                    pe.matmul(sb_[t][:, 0:n], qZ[:, hp, e, t * P:(t + 1) * P], kP[:, hp, 0:n],
                              start=True, stop=True).then_inc(s["ps_done"], 1)

            def t_head(h):
                pe.wait_ge(s["pnorm"], 4 * h + 4)
                for kb in range(4):
                    n = 4 * h + kb
                    if n >= 2:
                        pe.wait_ge(s["ptt_put"], n - 1)
                    for t in range(kb, 4):
                        ins = pe.transpose(TB[kb % 2][:, t * P:(t + 1) * P], pP[:, h % 2, t, kb * P:(kb + 1) * P], ident)
                    ins.then_inc(s["pt2_done"], 1)

            def pv_head(h):
                hp, e = h // 2, h % 2
                bank = (OB, SM)[hp % 2]
                if hp >= 2:
                    pe.wait_ge(s["o2_put"], hp - 1)
                else:
                    pe.wait_ge(s["glun_put"], 2)
                for kb in range(4):
                    pe.wait_ge(s["ptt_put"], 4 * h + kb + 1)
                    ins = pe.matmul(bank[64 * e:64 * e + 64, kb * P:TP_], vP[:, kb, h * DH:(h + 1) * DH],
                                    pPT[:, h % 2, kb, kb * P:TP_], start=(kb == 0), stop=(kb == 3))
                ins.then_inc(s["pv2_done"], 1)

            s_head(0)
            for h in range(H):
                if h + 1 < H:
                    s_head(h + 1)
                t_head(h)
                pv_head(h)
                if h == ST1_AFTER:
                    pe.wait_ge(s["conv_done"], CT)
                    pe.wait_ge(s["ptt_put"], 4 * h + 4)
                    for half in range(2):
                        for c in range(CT):
                            ins = pe.matmul(TB[half][:, 0:HALF], ones[:, :], conv[:, c, half * HALF:(half + 1) * HALF],
                                            start=(c == 0), stop=(c == CT - 1))
                        ins.then_inc(s["st1_done"], 1)
                    pe.wait_ge(s["mu_put"], 2)
                if h == ST2_AFTER:
                    pe.wait_ge(s["sq_ready"], 1)
                    pe.wait_ge(s["ptt_put"], 4 * h + 4)
                    for half in range(2):
                        for c in range(CT):
                            ins = pe.matmul(TB[half][:, 0:HALF], ones[:, :], sq[:, c, half * HALF:(half + 1) * HALF],
                                            start=(c == 0), stop=(c == CT - 1))
                        ins.then_inc(s["st2_done"], 1)
                    pe.wait_ge(s["sd_put"], 2)
            pe.wait_ge(s["histf_loaded"], 16)
            pe.wait_ge(s["ptt_put"], 4 * H)
            for r in range(2):
                for f in range(FT_N):
                    g = r * FT_N + f
                    ins = pe.transpose(TB[r][:, f * 16:(f + 1) * 16], histF[0:16, g * P:(g + 1) * P], ident[0:16, 0:16])
                ins.then_inc(s["hf_done"], 1)
            pe.wait_ge(s["wpw_loaded"], 16)
            pe.wait_ge(s["c_ready"], 1)
            for m in range(CT):
                for half in range(2):
                    n = 2 * m + half
                    if n >= 4:
                        pe.wait_ge(s["pw_put"], n - 3)
                    for c in range(CT):
                        ins = pe.matmul(sb_[n % 4][:, 0:HALF], wpw[:, c, m * P:(m + 1) * P],
                                        conv[:, c, half * HALF:(half + 1) * HALF], start=(c == 0), stop=(c == CT - 1))
                    ins.then_inc(s["pw_done"], 1)
            pe.wait_ge(s["wo_loaded"], 16)
            pe.wait_ge(s["pw_put"], 2 * CT)
            pe.wait_ge(s["mix_put"], 1)
            pe.wait_ge(s["o2_put"], HP)
            turn2 = [TB[0], TB[1], OB, SM]
            pe.wait_ge(s["hf_put"], 2)

            def mix_tile(t):
                m = tok(t)
                for nh in range(2):
                    if t >= 2:
                        pe.wait_ge(s["t1_put"], 2 * (t - 2) + nh + 1)
                    for k in range(KC):
                        ins = pe.matmul(sb_[2 * (t % 2) + nh][0:m, :], mixT[:, k, t * P:t * P + m],
                                        wo[:, k, nh * TP_:(nh + 1) * TP_], start=(k == 0), stop=(k == KC - 1))
                    ins.then_inc(s["mo_done"], 1)

            def h2_tile(t):
                m = tok(t)
                pe.wait_ge(s["h2_ready"], t + 1)
                for j in range(2):
                    n = 2 * t + j
                    if n >= 4:
                        pe.wait_ge(s["h2_put"], n - 3)
                    for k in range(4):
                        ins = pe.transpose(turn2[n % 4][:, k * P:k * P + m], t1[0:m, t % 2, (4 * j + k) * P:(4 * j + k + 1) * P],
                                           ident[0:m, 0:m])
                    ins.then_inc(s["h2_done"], 1)

            mix_tile(0)
            for t in range(TT):
                if t + 1 < TT:
                    mix_tile(t + 1)
                h2_tile(t)
            bank8 = sb_ + turn2
            pe.wait_ge(s["h2_put"], 2 * TT)
            pe.wait_ge(s["t1_put"], 2 * TT)
            with pe.Fori(0, FT_N // 2) as i:
                for slot in range(2):
                    pe.wait_ge(s["wu_lo"], i * 2 + (slot + 1))
                    for u in range(2):
                        for half in range(2):
                            n = 2 * u + half
                            pe.wait_ge(s["ux_put"], i * 8 + (4 * slot + n + 1))
                            for k in range(KC):
                                for j, (w, x) in enumerate(((wuhi, h2hi), (wuhi, h2lo), (wulo, h2hi))):
                                    ins = pe.matmul(bank8[4 * slot + n][:, 0:HALF], w[:, slot, k, u * P:(u + 1) * P],
                                                    x[:, k, half * HALF:(half + 1) * HALF],
                                                    start=(k == 0 and j == 0), stop=(k == KC - 1 and j == 2))
                            ins.then_inc(s["up_done"], 1)
            pe.wait_ge(s["last_put"], FT_N + 2)
            pe.wait_ge(s["ux_put"], 8 + 4 * FT_N)
            for n in range(11):
                if n >= 3:
                    pe.wait_ge(s["ul_put"], n - 2)
                for j in range(4):
                    g = 4 * n + j
                    ins = pe.transpose((TB[1], OB, SM)[n % 3][0:18, j * P:(j + 1) * P], last[:, g // FT_N, g % FT_N, :], ident)
                ins.then_inc(s["ul_done"], 1)
            pe.wait_ge(s["ft_ready"], FT_N)
            db = [[Z[0], Z[1], SC[0], SC[1], TB[0]], [TB[1], OB, SM, Z[0], Z[1]]]

            def down_pair(nh, kk, slot, first=False, last=False):
                pe.wait_ge(s["wd_lo"], kk + (11 * nh + 1))
                pe.wait_ge(s["ft_lo"], kk + (11 * nh + 1))
                for k2 in range(2):
                    for t in range(TT):
                        m = tok(t)
                        if nh and first and k2 == 0:
                            if t >= 3:
                                pe.wait_ge(s["y0_put"], t - 2)
                            else:
                                pe.wait_ge(s["ul_put"], 11)
                        for j, (x, w) in enumerate(((fThi, wdhi), (fThi, wdlo), (fTlo, wdhi))):
                            ins = pe.matmul(db[nh][t][0:m, :], x[:, slot, k2, t * P:t * P + m], w[:, slot, k2, :],
                                            start=(first and k2 == 0 and j == 0), stop=(last and k2 == 1 and j == 2))
                ins.then_inc(s["dn_done"], 1)

            for nh in range(2):
                down_pair(nh, 0, nh, first=True)
                with pe.Fori(0, 4) as i:
                    for j in range(2):
                        down_pair(nh, i * 2 + (1 + j), (nh + 1 + j) % 2)
                down_pair(nh, 9, (nh + 1) % 2)
                down_pair(nh, 10, nh, last=True)

        @block.scalar
        def _(act):
            act.dma_start(consts[:], a["consts"]).then_inc(s["c_loaded"], 16)
            act.dma_start(bvB[0:TS, :], a["b_in_v"].partition_broadcast(TS)).then_inc(s["bv_loaded"], 16)
            act.dma_start(histN[0:120, :, :], a["state_cv"][0].rearrange("(r b) w n -> (b w) r n", r=2)).then_inc(s["hist_loaded"], 16)
            for n in ("s_put", "pt_put", "v2_put", "k2_put", "ot_put", "g_exp"):
                act.sem_inc(s[n], START)
            me = Steps(act, s["act_step"])
            act.wait_ge(s["x_loaded"], 32)
            act.wait_ge(s["pool_set"], 1)
            for t in range(TT):
                me.then(act.activation(junkA[0:tok(t), :], xA[0:tok(t), t, :], ACT.Square, accum_out=ss[0:tok(t), t:t + 1]))
            act.activation(rstd[:, 0:TT], ss[:, 0:TT], ACT.Sqrt, bias=epsr, scale=1.0 / D).then_inc(s["x_summed"], 1)
            act.wait_ge(s["c_loaded"], 16)
            for hp in range(HP):
                act.wait_ge(s["zq_done"], 2 * hp + 1)
                for e in range(2):
                    ins = act.activation(qZ[64 * e:64 * e + 64, hp, e, 0:HALF], Z[0][64 * e:64 * e + 64, 0:HALF], ACT.Identity,
                                         bias=b_in[64 * e:64 * e + 64, hp:hp + 1])
                ins.then_inc(s["zq_putA"], 1)
            gs = glu[:, :, GX:GLUW].rearrange("p c (b x) -> p c b x", b=NB)
            for r in range(2):
                act.wait_ge(s["hist_done"], r + 1)
                for c in range(CT):
                    ins = act.activation(gs[:, c, 4 * r:4 * r + 4, 0:CW - 1],
                                         (OB, SM)[r][:, c * 120:(c + 1) * 120].rearrange("p (b w) -> p b w", b=4), ACT.Copy)
                ins.then_inc(s["hist_put"], 1)
            act.wait_ge(s["ks_done"], 1)
            for hp in range(HP):
                ins = act.activation(kTs[:, hp, :], TB[0][:, hp * TS:(hp + 1) * TS], ACT.Identity, bias=b_in[:, 4 + hp:5 + hp])
            ins.then_inc(s["ks_put"], 1)

            qS4 = qS.rearrange("p c (q g) -> p c g q", g=4)

            def spread_q(b):
                act.wait_ge(s["own_done"], b)
                act.nop()
                for g in range(4):
                    ins = act.activation(qS4[32 * g:32 * g + 32, :, g, :],
                                         qR[32 * g:32 * g + 32, :, bass.ds(b * NT, NT)], ACT.Copy)
                ins.then_inc(s["qs_ready"], 1)

            act.wait_ge(s["qr_ready"], 1)
            spread_q(0)

            def put_scores(b):
                act.wait_ge(s["p_turned"], b * 4 + START)
                act.wait_ge(s["vs_done"], 1)
                for j in range(4):
                    act.wait_ge(s["scores_done"], b * 4 + (j + 1))
                    act.activation(S[:, :, j * 256:(j + 1) * 256], SC[j % 2][:, :].rearrange("p (g k) -> p g k", g=2),
                                   ACT.Copy).then_inc(s["s_put"], 1)

            def exps(b):
                for g in range(2):
                    act.wait_ge(s["nb_ready"], b * 2 + (g + 1))
                    act.activation(S[:, g, :], S[:, g, :], ACT.Exp, bias=nb[:, g:g + 1], scale=SCALE,
                                   accum_out=rs[:, g:g + 1]).then_inc(s["probs_ready"], 1)
                for g in range(2):
                    ins = act.activation(ownS[:, g, :], ownS[:, g, :], ACT.Exp, bias=nb[:, g:g + 1], scale=SCALE,
                                         accum_out=rs[:, 2 + g:3 + g])
                ins.then_inc(s["probs_ready"], 1)

            def put_turned(b):
                act.wait_ge(s["pv_done"], b * 8 + START)
                for n in range(4):
                    act.wait_ge(s["p_turned"], b * 4 + (n + 1) + START)
                    act.activation(pT[:, n // 2, 4 * (n % 2):4 * (n % 2) + 4, :],
                                   TB[n % 2][:, :].rearrange("p (u r) -> p u r", u=4), ACT.Copy).then_inc(s["pt_put"], 1)
                act.wait_ge(s["own_turned"], b + 1 + START)
                act.activation(pTo[0:TS, :, :], SM[0:TS, P:3 * P].rearrange("p (g r) -> p g r", g=2), ACT.Copy).then_inc(s["pto_put"], 1)

            def put_out(b):
                act.wait_ge(s["ot_done"], b + 1 + START)
                act.nop()
                act.activation(oT[:, bass.ds(b, 1), :].rearrange("p a r -> p (a r)"), TB[0][:, 0:P], ACT.Copy).then_inc(s["ot_put"], 1)

            def glu_exps(i):
                act.wait_ge(s["g_exp"], i * 2 + START)
                act.nop()
                act.activation(small[:, 31:32], nbg[:, bass.ds(i, 1)], ACT.Copy).then_inc(s["g_bias"], 1)
                act.wait_ge(s["g_bias"], i + 1)
                act.wait_ge(s["z1_put"], i * 2 + START)
                for half in range(2):
                    act.wait_ge(s["z1_done"], i * 4 + (half + 1) + START)
                    act.activation(sig[:, half * HALF:(half + 1) * HALF], Z[half][:, 0:HALF], ACT.Exp,
                                   bias=small[:, 31:32], scale=-1.0).then_inc(s["g_exp"], 1)

            def put_v(i):
                act.wait_ge(s["v2_done"], i + 1)
                act.wait_ge(s["nb_ready"], i * 2 + 10)
                act.nop()
                act.activation(vT[:, 0:TP_], Z[0][:, :], ACT.Identity, bias=b_in[:, bass.ds(i + 8, 1)]).then_inc(s["v2_put"], 1)

            def put_kv(i):
                act.wait_ge(s["k2_done"], i + 1 + START)
                act.nop()
                act.activation(kP[:, bass.ds(i, 1), :].rearrange("p a t -> p (a t)"), Z[1][:, :], ACT.Identity,
                               bias=b_in[:, bass.ds(i + 4, 1)]).then_inc(s["k2_put"], 1)
                act.wait_ge(s["v2_turned"], i + 1)
                act.nop()
                act.activation(vP[:, 0:4, bass.ds(i * P, P)], TB[0][:, :].rearrange("p (t r) -> p t r", t=4),
                               ACT.Copy).then_inc(s["v2_home"], 1)

            with act.Fori(0, 4) as i:
                put_scores(i)
                glu_exps(i)
                exps(i)
                put_turned(i)
                put_out(i)
                spread_q(i + 1)
            with act.Fori(0, 3) as i:
                put_scores(i + 4)
                exps(i + 4)
                put_v(i)
                put_kv(i)
                put_turned(i + 4)
                put_out(i + 4)
                spread_q(i + 5)
            put_scores(7)
            exps(7)
            put_v(3)
            put_kv(3)
            put_turned(7)
            put_out(7)
            act.wait_ge(s["z1_put"], 8 + START)
            act.wait_ge(s["own_done"], NB)
            act.activation(gluS.rearrange("p c (b t) -> p c b t", b=NB), gs[:, :, :, CW - 1:SX], ACT.Copy).then_inc(s["glus_put"], 1)
            nat = [TB[0], TB[1], SM, TB[0], TB[1]]
            act.wait_ge(s["pv_done"], SUPER * NB + START)
            act.wait_ge(s["scores_done"], 4 * NB)
            for t in range(TT):
                act.wait_ge(s["knat_done"], t + 1)
                act.activation(kNat[0:tok(t), t, :], nat[t][0:tok(t), :], ACT.Copy).then_inc(s["knat_put"], 1)
            for r in range(2):
                act.wait_ge(s["glun_done"], r + 1)
                n = (CW - 1, TS)[r]
                act.activation(cvN[0:n, r, :], (SM, OB)[r][0:n, :], ACT.Copy).then_inc(s["glun_put"], 1)
            act.wait_ge(s["knat_put"], TT)
            act.wait_ge(s["glun_put"], 2)
            act.wait_ge(s["v2_home"], 4)
            act.wait_ge(s["vs_put"], 1)
            rows = lambda n: a[n][0, 0].rearrange("(t p) h d -> p t (h d)", p=P)
            act.dma_start(rows("k_p"), kNat[:, 0:4, :]).then_inc(s["stored_kv"], 16)
            act.dma_start(rows("v_p"), vP[:, 0:4, :]).then_inc(s["stored_kv"], 16)
            act.dma_start(a["k_s"][0].rearrange("b t h d -> (b t) (h d)"), kNat[0:TS, 4, :]).then_inc(s["stored_kv"], 16)
            act.dma_start(a["v_s"][0].rearrange("b t h d -> (b t) (h d)"), vP[0:TS, 4, :]).then_inc(s["stored_kv"], 16)
            act.dma_start(a["cv_p"][0, 0], cvN[0:CW - 1, 0, :]).then_inc(s["stored_kv"], 16)
            act.dma_start(a["cv_s"][0][:, CW - 1 - NT:CW - 1, :], cvN[0:TS, 1, :]).then_inc(s["stored_kv"], 16)
            act.dma_start(a["cv_s"][0][:, 0:CW - 1 - NT, :], a["state_cv"][0][:, NT:CW - 1, :]).then_inc(s["stored_kv"], 16)
            sb_ = [Z[0], Z[1], SC[0], SC[1]]

            def p_exps(h):
                act.wait_ge(s["pnb_ready"], h + 1)
                if h >= 2:
                    act.wait_ge(s["pt2_done"], 4 * (h - 1))
                for t in range(4):
                    n = (t + 1) * P
                    j = 4 * (h % 2) + t
                    act.activation(pP[:, h % 2, t, 0:n], sb_[t][:, 0:n], ACT.Exp, bias=pnb[:, j:j + 1], scale=SCALE,
                                   accum_out=prs[:, j:j + 1]).then_inc(s["pexp"], 1)

            def p_turned(h):
                if h >= 2:
                    act.wait_ge(s["pv2_done"], h - 1)
                for kb in range(4):
                    act.wait_ge(s["pt2_done"], 4 * h + kb + 1)
                    act.activation(pPT[:, h % 2, kb, kb * P:TP_], TB[kb % 2][:, kb * P:TP_], ACT.Copy).then_inc(s["ptt_put"], 1)

            p_exps(0)
            for h in range(H):
                if h + 1 < H:
                    p_exps(h + 1)
                p_turned(h)
                if h == ST1_AFTER:
                    for half in range(2):
                        act.wait_ge(s["st1_done"], half + 1)
                        act.activation(mu[:, half * HALF:(half + 1) * HALF], TB[half][:, 0:HALF], ACT.Copy,
                                       scale=1.0 / DA).then_inc(s["mu_put"], 1)
                if h == ST2_AFTER:
                    for half in range(2):
                        act.wait_ge(s["st2_done"], half + 1)
                        act.activation(sd[:, half * HALF:(half + 1) * HALF], TB[half][:, 0:HALF], ACT.Sqrt, bias=epsl,
                                       scale=1.0 / DA).then_inc(s["sd_put"], 1)
            act.wait_ge(s["ln_ready"], 1)
            act.activation(sq, conv, ACT.Sigmoid).then_inc(s["sg_put"], 1)
            for m in range(CT):
                for half in range(2):
                    n = 2 * m + half
                    act.wait_ge(s["pw_done"], n + 1)
                    act.activation(mixT[:, 4 + m, half * HALF:(half + 1) * HALF], sb_[n % 4][:, 0:HALF], ACT.Identity,
                                   bias=cst("b_pw")[:, m:m + 1]).then_inc(s["pw_put"], 1)
            act.wait_ge(s["pv2_done"], H)
            for t in range(TT):
                m = tok(t)
                for nh in range(2):
                    act.wait_ge(s["mo_done"], 2 * t + nh + 1)
                    if 2 * t + nh:
                        act.wait_ge(s["mo_sq"], 2 * t + nh)
                    if t and nh == 0:
                        act.wait_ge(s["x1_sq"], t)
                    act.activation(junk[0:m, 0:TP_], sb_[2 * (t % 2) + nh][0:m, :], ACT.Square,
                                   accum_out=ss2[0:m, 2 * t + nh:2 * t + nh + 1]).then_inc(s["mo_sq"], 1)
                act.wait_ge(s["mo_sum"], t + 1)
                act.activation(r2[0:m, t:t + 1], r2[0:m, t:t + 1], ACT.Sqrt, bias=epsr[0:m], scale=1.0 / D).then_inc(s["mo_rt"], 1)
                act.wait_ge(s["x1_ready"], t + 1)
                act.wait_ge(s["mo_sq"], 2 * t + 2)
                act.activation(junk[0:m, :], x1[0:m, t, :], ACT.Square, accum_out=ss3[0:m, t:t + 1]).then_inc(s["x1_sq"], 1)
                act.wait_ge(s["x1_sq"], t + 1)
                act.activation(r3[0:m, t:t + 1], ss3[0:m, t:t + 1], ACT.Sqrt, bias=epsr[0:m], scale=1.0 / D).then_inc(s["x1_rt"], 1)
            act.wait_ge(s["h2_put"], 2 * TT)
            act.wait_ge(s["mo_done"], 2 * TT)
            act.wait_ge(s["t1_put"], 2 * TT)
            bank8 = sb_ + [TB[0], TB[1], OB, SM]
            act.sem_inc(s["ux_put"], 8)
            wu_full = [s["wu_full0"], s["wu_full1"]]

            def up_step(i, slot, split_next=True):
                if split_next:
                    act.wait_ge(wu_full[1 - slot], i * 32 + 32 * (slot + 1))
                    act.wait_ge(s["up_done"], i * 8 + (4 * slot + START))
                    act.activation(wuhi[:, 1 - slot, :, :], wu[1 - slot].rearrange("p k u n -> p k (u n)"),
                                   ACT.Copy).then_inc(s["wu_hi"], 1)
                act.wait_ge(s["cv_done"], i * 2 + (slot + 1))
                act.wait_ge(s["last_put"], i * 2 + (slot + 1))
                for u in range(2):
                    for half in range(2):
                        n = 2 * u + half
                        act.wait_ge(s["up_done"], i * 8 + (4 * slot + n + 1 + START))
                        bk = bank8[4 * slot + n]
                        if half == 0:
                            ins = act.activation(ux[:, slot, u, 2:2 + HALF], bk[:, 0:HALF], ACT.Copy)
                        else:
                            r = TP_ - HALF
                            act.activation(ux[:, slot, u, 2 + HALF:2 + TP_], bk[:, 0:r], ACT.Copy)
                            ins = act.activation(ux[:, slot, u, 2 + TP_:UXW].rearrange("p (b x) -> p b x", b=NB)[:, :, 2:UXS],
                                                 bk[:, r:HALF].rearrange("p (b t) -> p b t", b=NB), ACT.Copy)
                        ins.then_inc(s["ux_put"], 1)
                act.wait_ge(s["g_conv"], i * 2 + (slot + 1))
                act.activation(sg2[:, slot, :], cvo[:, slot, 0, :], ACT.Sigmoid).then_inc(s["g_sig"], 1)

            act.wait_ge(wu_full[0], 32)
            act.activation(wuhi[:, 0, :, :], wu[0].rearrange("p k u n -> p k (u n)"), ACT.Copy).then_inc(s["wu_hi"], 1)
            with act.Fori(0, FT_N // 2 - 1) as i:
                for slot in range(2):
                    up_step(i, slot)
            up_step(FT_N // 2 - 1, 0)
            up_step(FT_N // 2 - 1, 1, split_next=False)
            wd_full = [s["wd_full0"], s["wd_full1"]]
            act.wait_ge(s["up_done"], 4 * FT_N + START)
            act.wait_ge(s["ft_ready"], FT_N)

            def split_pair(nh, kk, slot):
                c = 11 * nh
                act.wait_ge(wd_full[slot], kk * 8 + 8 * (c + 2 - slot))
                if nh or not isinstance(kk, int) or kk > 1:
                    act.wait_ge(s["dn_done"], kk + (c - 1))
                    act.nop()
                act.activation(wdhi[:, slot, :, :], wd[:, slot, :, :], ACT.Copy).then_inc(s["wd_hi"], 1)
                act.activation(fThi[:, slot, :, :], fT[:, bass.ds(kk * 2, 2), :], ACT.Copy).then_inc(s["ft_hi"], 1)

            y_banks = [[Z[0], Z[1], SC[0], SC[1], TB[0]], [TB[1], OB, SM, Z[0], Z[1]]]

            def y_squares(nh):
                act.wait_ge(s["dn_done"], 11 * (nh + 1))
                for t in range(TT):
                    m = tok(t)
                    if 5 * nh + t:
                        act.wait_ge(s["y_sq"], 5 * nh + t)
                    act.activation(junkY[0:m, :], y_banks[nh][t][0:m, :], ACT.Square,
                                   accum_out=ss2[0:m, 2 * t + nh:2 * t + nh + 1]).then_inc(s["y_sq"], 1)

            for nh in range(2):
                split_pair(nh, 0, nh)
                split_pair(nh, 1, 1 - nh)
                if nh:
                    y_squares(0)
                with act.Fori(0, 4) as i:
                    for j in range(2):
                        split_pair(nh, i * 2 + (2 + j), (nh + j) % 2)
                split_pair(nh, 10, nh)
            y_squares(1)
            act.wait_ge(s["y_sum"], 1)
            act.activation(r2[:, 0:TT], r2[:, 0:TT], ACT.Sqrt, bias=epsr, scale=1.0 / D).then_inc(s["y_rt"], 1)

        @block.vector
        def _(dve):
            for n in ("z1_put", "o_norm"):
                dve.sem_inc(s[n], START)
            me = Steps(dve, s["dve_step"])
            dve.wait_ge(s["x_summed"], 1)
            me.then(dve.reciprocal(rstd[:, 0:TT], rstd[:, 0:TT]))
            for t in range(TT):
                dve.tensor_scalar(xA[0:tok(t), t, :], xA[0:tok(t), t, :], rstd[0:tok(t), t:t + 1], None, ALU.mult).then_inc(s["x_scaled"], 1)
            dve.wait_ge(s["c_loaded"], 16)
            dve.tensor_scalar(nbg, b_in[:, 16:20], -1.0, None, ALU.mult)
            turn = [TB[0], TB[1], SC[0], SC[1]]
            gpre = cst("g_pre")
            for t in range(TT):
                for j in range(2):
                    n = 2 * t + j
                    dve.wait_ge(s["xt_done"], n + 1)
                    m = tok(t)
                    dve.tensor_tensor(hT[:, 4 * j:4 * j + 4, t * P:t * P + m],
                                      turn[n % 4][:, :].rearrange("p (k t) -> p k t", k=4)[:, :, 0:m],
                                      gpre[:, 4 * j:4 * j + 4].unsqueeze(2).to_broadcast([P, 4, m]), ALU.mult).then_inc(s["ht_ready"], 1)
            dve.wait_ge(s["pool_set"], 1)
            for hp in range(HP):
                dve.wait_ge(s["zq_done"], 2 * hp + 2)
                for e in range(2):
                    dve.tensor_scalar(qZ[64 * e:64 * e + 64, hp, e, HALF:TP_], Z[1][64 * e:64 * e + 64, 0:TP_ - HALF],
                                      b_in[64 * e:64 * e + 64, hp:hp + 1], None, ALU.add)
                dve.tensor_scalar(qTs[:, hp, :], Z[1][:, TP_ - HALF:HALF], b_in[:, hp:hp + 1], None,
                                  ALU.add).then_inc(s["zq_putV"], 1)
            dve.wait_ge(s["zq_putV"], HP)
            qR5 = qR.rearrange("p (h x) t -> p h x t", x=4)
            for g in range(4):
                for x in range(4):
                    ins = dve.tensor_copy(qR5[32 * g:32 * g + 32, :, x, :], qTs[32 * x:32 * x + 32, :, :])
            ins.then_inc(s["qr_ready"], 1)
            dve.wait_ge(s["ks_put"], 1)
            kO5 = kOwn.rearrange("p (h x) t -> p h x t", x=4)
            for x in range(4):
                ins = dve.tensor_copy(kO5[0:32, :, x, :], kTs[32 * x:32 * x + 32, :, :])
            ins.then_inc(s["kown_put"], 1)
            dve.wait_ge(s["hist_done"], 2)

            def turn_k(b, u, first=False):
                dve.wait_ge(kn_full[u % 4], b * 128 + 64 * (u // 4 + 1))
                if u % 2 == 0 and not first:
                    dve.wait_ge(s["scores_done"], b * 4 + max(u // 2 - 1, 0))
                dve.transpose(kT[:, u % 4, :, :].rearrange("p c (i k) -> p i c k", i=4),
                              kN[:, u % 4, :, :].rearrange("p i (c k) -> p i c k", k=32)).then_inc(s["kt_ready"], 1)

            turn_k(0, 0, True)
            turn_k(0, 1, True)
            dve.wait_ge(s["vs_done"], 1)
            dve.wait_ge(s["bv_loaded"], 16)
            dve.tensor_tensor(vP[0:TS, 4, :], TB[1][0:TS, :], bvB[0:TS, :], ALU.add).then_inc(s["vs_put"], 1)
            dve.wait_ge(s["vs_put"], 1)
            turn_k(0, 2, True)
            turn_k(0, 3, True)

            SOFT = 18

            def softmax(b):
                me = Steps(dve, s["soft_step"], b * SOFT)
                S4 = S.rearrange("p g (n k) -> p (g n) k", k=64)
                for j in range(4):
                    dve.wait_ge(s["s_put"], b * 4 + (j + 1) + START)
                    part = S[:, :, j * 256:(j + 1) * 256].rearrange("p g (n k) -> p g n k", k=64)
                    dve.tensor_reduce(bmax.rearrange("p (g n) -> p g n", g=2)[:, :, 4 * j:4 * j + 4], part, AX.X, ALU.max)
                    ins = dve.tensor_reduce(bsum.rearrange("p (g n) -> p g n", g=2)[:, :, 4 * j:4 * j + 4], part, AX.X, ALU.add)
                me.then(ins)

                def over_quads(src, dst, op):
                    me.then(dve.transpose(tA, src))
                    me.then(dve.tensor_reduce(tB[:, 0:8], tA.rearrange("p (q g) -> p q g", g=4), AX.X, op))
                    me.then(dve.tensor_copy(tC.rearrange("p (q g) -> p q g", g=4), tB[:, 0:8].unsqueeze(2).to_broadcast([P, 8, 4])))
                    me.then(dve.transpose(dst, tC))

                over_quads(bsum, bsum, ALU.add)
                t3 = bsum.rearrange("p (g n) -> p g n", g=2)
                for g in range(2):
                    ins = dve.tensor_tensor(rankv[:, g], t3[:, g].unsqueeze(1).to_broadcast([P, BLK, BLK]),
                                            t3[:, g].unsqueeze(2).to_broadcast([P, BLK, BLK]), ALU.subtract)
                me.then(ins)
                for g in range(2):
                    ins = dve.tensor_tensor(rankv[:, g], rankv[:, g], order, ALU.is_ge)
                me.then(ins)
                me.then(dve.tensor_reduce(pen, rank.rearrange("p (n m) -> p n m", m=BLK), AX.X, ALU.add))
                me.then(dve.tensor_scalar(pen, pen, float(TOPK), -BIG, ALU.is_ge, ALU.mult))
                me.then(dve.tensor_tensor(bmax, bmax, pen, ALU.add))
                me.then(dve.tensor_reduce(mx2[:, 0:2], bmax.rearrange("p (g n) -> p g n", g=2), AX.X, ALU.max))
                dve.wait_ge(s["own_done"], b + 1)
                dve.wait_ge(s["own_turned"], b + START)
                me.then(dve.tensor_tensor(ownS, own_ps, ownmask[:, bass.ds(b * -NT + (TS - NT), TS)].unsqueeze(1).to_broadcast([P, 2, TS]), ALU.add))
                me.then(dve.tensor_reduce(mx2[:, 2:4], ownS, AX.X, ALU.max))
                me.then(dve.tensor_tensor(mcol[:, 0:2], mx2[:, 0:2], mx2[:, 2:4], ALU.max))
                over_quads(mcol, bsum, ALU.max)
                dve.tensor_scalar(nb, bsum[:, 0:2], -SCALE, None, ALU.mult)
                for g in range(2):
                    dve.tensor_tensor(S4[:, BLK * g:BLK * g + BLK], S4[:, BLK * g:BLK * g + BLK],
                                      pen[:, BLK * g:BLK * g + BLK].unsqueeze(2).to_broadcast([P, BLK, 64]),
                                      ALU.add).then_inc(s["nb_ready"], 1)
                assert me.n == SOFT, me.n

            def row_sums(b):
                dve.wait_ge(s["probs_ready"], b * 3 + 3)
                dve.wait_ge(s["den_done"], b + START)
                dve.tensor_tensor(rsum, rs[:, 0:2], rs[:, 2:4], ALU.add).then_inc(s["rsum_ready"], 1)

            def norm_out(b):
                dve.wait_ge(s["pv_done"], b * 8 + 8 + START)
                dve.reciprocal(rden, den_ps).then_inc(s["den_inv"], 1)
                dve.wait_ge(s["den_inv"], b + 1)
                dve.wait_ge(s["ot_done"], b + START)
                dve.tensor_scalar(oN[:, :], OB[:, 0:P], rden, None, ALU.mult).then_inc(s["o_norm"], 1)

            def glu_values(i):
                dve.wait_ge(s["g_exp"], i * 2 + 2 + START)
                dve.tensor_scalar(sig, sig, 1.0, None, ALU.add).then_inc(s["sig_ready"], 1)
                dve.wait_ge(s["sig_ready"], i * 2 + 1)
                dve.reciprocal(sig, sig).then_inc(s["sig_ready"], 1)
                dve.wait_ge(s["sig_ready"], i * 2 + 2)
                gi = glu[:, bass.ds(i, 1), :].rearrange("p a x -> p (a x)")
                ba = b_in[:, bass.ds(i + 12, 1)]
                dve.wait_ge(s["z1_done"], i * 4 + 3 + START)
                dve.scalar_tensor_tensor(gi[:, CW - 1:CW - 1 + HALF], Z[0][:, 0:HALF], ba, sig[:, 0:HALF],
                                         ALU.add, ALU.mult).then_inc(s["z1_put"], 1)
                dve.wait_ge(s["z1_done"], i * 4 + 4 + START)
                r = TP_ - HALF
                dve.scalar_tensor_tensor(gi[:, CW - 1 + HALF:GX], Z[1][:, 0:r], ba, sig[:, HALF:TP_], ALU.add, ALU.mult)
                dve.scalar_tensor_tensor(gi[:, GX:GLUW].rearrange("p (b x) -> p b x", b=NB)[:, :, CW - 1:SX],
                                         Z[1][:, r:HALF].rearrange("p (b t) -> p b t", b=NB), ba,
                                         sig[:, TP_:TOK].rearrange("p (b t) -> p b t", b=NB),
                                         ALU.add, ALU.mult).then_inc(s["z1_put"], 1)

            def step(b, last=False, between=None):
                for u in range(4, 8):
                    turn_k(b, u)
                softmax(b)
                if not last:
                    turn_k(b + 1, 0)
                    turn_k(b + 1, 1)
                row_sums(b)
                if not last:
                    turn_k(b + 1, 2)
                    turn_k(b + 1, 3)
                if between:
                    between()
                norm_out(b)

            with dve.Fori(0, 4) as i:
                step(i, between=lambda: glu_values(i))
            with dve.Fori(0, 3) as i:
                step(i + 4)
            step(7, last=True)
            dve.wait_ge(s["ot_put"], NB + START)
            dve.wait_ge(s["k2_done"], 4 + START)
            for e in range(2):
                for x in range(2):
                    row = slice(64 * e, 64 * e + 64)
                    src = oT[row].rearrange("p b (g x h q) -> p g b x h q", g=2, x=2, h=4)[:, :, :, x, 2 * x + e, :]
                    dst = mixT[row, 0:HP, TP_:TOK].rearrange("p (g x) (b q) -> p g x b q", x=2, b=NB)[:, :, x]
                    ins = dve.tensor_copy(dst, src)
            ins.then_inc(s["mix_put"], 1)
            sb_ = [Z[0], Z[1], SC[0], SC[1]]
            dve.wait_ge(s["k2_put"], 4 + START)
            me = Steps(dve, s["pst_step"])

            def p_stats(h):
                j = 4 * (h % 2)
                for t in range(4):
                    dve.wait_ge(s["ps_done"], 4 * h + t + 1)
                    ins = dve.tensor_tensor(sb_[t][:, t * P:(t + 1) * P], sb_[t][:, t * P:(t + 1) * P], causal, ALU.add)
                me.then(ins)
                for t in range(4):
                    ins = dve.tensor_reduce(pm[:, j + t:j + t + 1], sb_[t][:, 0:(t + 1) * P], AX.X, ALU.max)
                me.then(ins)
                dve.tensor_scalar(pnb[:, j:j + 4], pm[:, j:j + 4], -SCALE, None, ALU.mult).then_inc(s["pnb_ready"], 1)

            def p_norms(h):
                j = 4 * (h % 2)
                dve.wait_ge(s["pexp"], 4 * h + 4)
                me.then(dve.reciprocal(prr[:, j:j + 4], prs[:, j:j + 4]))
                for t in range(4):
                    n = (t + 1) * P
                    dve.tensor_scalar(pP[:, h % 2, t, 0:n], pP[:, h % 2, t, 0:n], prr[:, j + t:j + t + 1], None,
                                      ALU.mult).then_inc(s["pnorm"], 1)

            def p_out(hp):
                dve.wait_ge(s["pv2_done"], 2 * hp + 2)
                dve.tensor_copy(mixT[:, hp, 0:TP_], (OB, SM)[hp % 2][:, :]).then_inc(s["o2_put"], 1)

            p_stats(0)
            for h in range(H):
                if h + 1 < H:
                    p_stats(h + 1)
                p_norms(h)
                if h % 2 == 0 and h:
                    p_out(h // 2 - 1)
                if h == ST2_AFTER + 1:
                    dve.wait_ge(s["sd_put"], 2)
                    dve.reciprocal(sd, sd).then_inc(s["sd_inv"], 1)
            p_out(HP - 1)
            for r in range(2):
                dve.wait_ge(s["hf_done"], r + 1)
                if r == 0:
                    dve.wait_ge(s["ln_ready"], 1)
                    dve.wait_ge(s["sg_put"], 1)
                    dve.tensor_tensor(conv, conv, sq, ALU.mult).then_inc(s["c_ready"], 1)
                    dve.wait_ge(s["pw_done"], 2 * CT)
                dve.tensor_copy(histT[:, r, :, :], TB[r][:, 0:FT_N * 16].rearrange("p (f x) -> p f x", x=16)).then_inc(s["hf_put"], 1)
            dve.wait_ge(s["gpost_loaded"], 16)
            dve.wait_ge(s["xr_loaded"], 32)
            me2 = Steps(dve, s["mo_step"])
            turn2 = [TB[0], TB[1], OB, SM]
            gffn = cst("g_ffn")

            def put_h2(t):
                m = tok(t)
                for j in range(2):
                    n = 2 * t + j
                    dve.wait_ge(s["h2_done"], n + 1)
                    if n >= 2:
                        dve.wait_ge(s["h2_put"], n - 1)
                    dve.tensor_tensor(h2raw[:, n % 2, :].rearrange("p (k t) -> p k t", k=4)[:, :, 0:m],
                                      turn2[n % 4][:, :].rearrange("p (k t) -> p k t", k=4)[:, :, 0:m],
                                      gffn[:, 4 * j:4 * j + 4].unsqueeze(2).to_broadcast([P, 4, m]), ALU.mult).then_inc(s["h2_raw"], 1)

            for t in range(TT):
                m = tok(t)
                dve.wait_ge(s["mo_sq"], 2 * t + 2)
                dve.tensor_tensor(r2[0:m, t:t + 1], ss2[0:m, 2 * t:2 * t + 1], ss2[0:m, 2 * t + 1:2 * t + 2], ALU.add).then_inc(s["mo_sum"], 1)
                dve.wait_ge(s["mo_rt"], t + 1)
                me2.then(dve.reciprocal(r2[0:m, t:t + 1], r2[0:m, t:t + 1]))
                if t >= 2:
                    dve.wait_ge(s["h2_done"], 2 * (t - 2) + 2)
                for nh in range(2):
                    cols = slice(nh * TP_, (nh + 1) * TP_)
                    dve.scalar_tensor_tensor(t1[0:m, t % 2, cols], sb_[2 * (t % 2) + nh][0:m, :], r2[0:m, t:t + 1],
                                             gPost[0:m, cols], ALU.mult, ALU.mult).then_inc(s["t1_put"], 1)
                dve.wait_ge(s["t1_put"], 2 * t + 2)
                dve.tensor_tensor(x1[0:m, t, :], x1[0:m, t, :], t1[0:m, t % 2, :], ALU.add).then_inc(s["x1_ready"], 1)
                dve.wait_ge(s["x1_ready"], t + 1)
                if t:
                    put_h2(t - 1)
                dve.wait_ge(s["x1_rt"], t + 1)
                me2.then(dve.reciprocal(r3[0:m, t:t + 1], r3[0:m, t:t + 1]))
                dve.tensor_scalar(t1[0:m, t % 2, :], x1[0:m, t, :], r3[0:m, t:t + 1], None, ALU.mult).then_inc(s["h2_ready"], 1)
            put_h2(TT - 1)
            dve.sem_inc(s["cv_done"], 2)
            with dve.Fori(0, FT_N // 2) as i:
                for slot in range(2):
                    me3 = Steps(dve, s["f_step"], i * 10 + 5 * slot)
                    dve.wait_ge(s["taps_put"], i * 2 + (slot + 1))
                    for u in range(2):
                        dve.wait_ge(s["ux_put"], i * 8 + (8 + 4 * slot + 2 * u + 2))
                        src, dst = ux[:, slot, u, :], cvo[:, slot, u, :]
                        ps_in = src[:, 2 + TP_:UXW].rearrange("p (b x) -> p b x", b=NB)
                        ps_out = dst[:, TP_:TOK].rearrange("p (b t) -> p b t", b=NB)
                        w = wdw[:, slot, u, :]
                        dve.tensor_scalar(dst[:, 0:TP_], src[:, 0:TP_], w[:, 0:1], w[:, 3:4], ALU.mult, ALU.add)
                        me3.then(dve.tensor_scalar(ps_out, ps_in[:, :, 0:NT], w[:, 0:1], w[:, 3:4], ALU.mult, ALU.add))
                        for j in (1, 2):
                            dve.scalar_tensor_tensor(dst[:, 0:TP_], src[:, j:j + TP_], w[:, j:j + 1], dst[:, 0:TP_], ALU.mult, ALU.add)
                            ins = dve.scalar_tensor_tensor(ps_out, ps_in[:, :, j:j + NT], w[:, j:j + 1], ps_out, ALU.mult, ALU.add)
                            if j == 2:
                                ins.then_inc(s[("g_conv", "cv_done")[u]], 1)
                            else:
                                me3.then(ins)
                    dve.wait_ge(s["g_sig"], i * 2 + (slot + 1))
                    me3.then(dve.tensor_tensor(cvo[:, slot, 0, :], cvo[:, slot, 0, :], sg2[:, slot, :], ALU.mult))
                    dve.wait_ge(s["cv_done"], i * 2 + (slot + 3))
                    dve.tensor_tensor(fT[:, bass.ds(i * 2 + slot, 1), :].rearrange("p a t -> p (a t)"), cvo[:, slot, 0, :],
                                      cvo[:, slot, 1, :], ALU.mult).then_inc(s["ft_ready"], 1)
                    assert me3.n == 5, me3.n
            for n in range(11):
                dve.wait_ge(s["ul_done"], n + 1)
                dve.tensor_copy(histF[0:18, n * TP_:(n + 1) * TP_], (TB[1], OB, SM)[n % 3][0:18, :]).then_inc(s["ul_put"], 1)
            def rest_pair(nh, kk, slot):
                dve.wait_ge(s["ft_hi"], kk + (11 * nh + 1))
                dve.tensor_tensor(fTlo[:, slot, :, :], fT[:, bass.ds(kk * 2, 2), :], fThi[:, slot, :, :].bitcast(F32),
                                  ALU.subtract).then_inc(s["ft_lo"], 1)

            for nh in range(2):
                rest_pair(nh, 0, nh)
                rest_pair(nh, 1, 1 - nh)
                if nh:
                    for t in range(TT):
                        dve.wait_ge(s["y_sq"], t + 1)
                        dve.tensor_copy(y0[0:tok(t), t, :], (Z[0], Z[1], SC[0], SC[1], TB[0])[t][0:tok(t), :]).then_inc(s["y0_put"], 1)
                with dve.Fori(0, 4) as i:
                    for j in range(2):
                        rest_pair(nh, i * 2 + (2 + j), (nh + j) % 2)
                rest_pair(nh, 10, nh)
            dve.wait_ge(s["gffn_loaded"], 16)
            dve.wait_ge(s["y_sq"], 2 * TT)
            me4 = Steps(dve, s["y_step"])
            s2 = ss2[:, 0:2 * TT].rearrange("p (t n) -> p n t", n=2)
            dve.tensor_tensor(r2[:, 0:TT], s2[:, 0, :], s2[:, 1, :], ALU.add).then_inc(s["y_sum"], 1)
            dve.wait_ge(s["y_rt"], 1)
            me4.then(dve.reciprocal(r2[:, 0:TT], r2[:, 0:TT]))
            for t in range(TT):
                m = tok(t)
                if t >= 2:
                    dve.wait_ge(s[f"stored_y{t % 2}"], 16 * (t // 2))
                for nh in range(2):
                    src = y0[0:m, t, :] if nh == 0 else (TB[1], OB, SM, Z[0], Z[1])[t][0:m, :]
                    cols = slice(nh * TP_, (nh + 1) * TP_)
                    ins = dve.scalar_tensor_tensor(yo[0:m, t % 2, cols], src, r2[0:m, t:t + 1], gFfn[0:m, cols], ALU.mult, ALU.mult)
                me4.then(ins)
                dve.tensor_tensor(yo[0:m, t % 2, :], yo[0:m, t % 2, :], x1[0:m, t, :], ALU.add).then_inc(s["yo_ready"], 1)

        @block.gpsimd
        def _(pool):
            pool.memset(A[:, 0:4096], 0.0)
            pool.memset(vP[:, 4, :], 0.0)
            pool.memset(glu[:, :, 0:CW - 1], 0.0)
            pool.memset(qS, 0.0)
            pool.memset(kOwn, 0.0)
            pool.memset(small[:, :], 0.0).then_inc(s["pool_step"], 1)
            pool.memset(pTo_[:, :], 0.0)
            pool.wait_ge(s["pool_step"], 1)
            pool.memset(ss, 1.0)
            pool.memset(epsr, 1e-6)
            pool.memset(epsl, 1e-5)
            pool.memset(ones[:, :], 1.0).then_inc(s["pool_set"], 1)
            me = Steps(pool, s["conv_step"])
            pool.wait_ge(s["c_loaded"], 16)
            pool.wait_ge(s["hist_put"], 2)
            for i in range(CT):
                pool.wait_ge(s["z1_put"], 2 * i + 2 + START)
                prod = conv[:, i + 1, :] if i + 1 < CT else sig
                gx = glu[:, i, GX:GLUW].rearrange("p (b x) -> p b x", b=NB)
                for j in range(CW):
                    w = w_cv[:, i, j:j + 1]
                    dst = prod if j else conv[:, i, :]
                    ds = dst[:, TP_:TOK].rearrange("p (b t) -> p b t", b=NB)
                    bias = [ALU.mult] if j else [ALU.mult, ALU.add]
                    b2 = None if j else w_cv[:, i, CW:CW + 1]
                    pool.tensor_scalar(dst[:, 0:TP_], glu[:, i, j:j + TP_], w, b2, *bias)
                    me.then(pool.tensor_scalar(ds, gx[:, :, j:j + NT], w, b2, *bias))
                    if j:
                        ins = pool.tensor_tensor(conv[:, i, :], conv[:, i, :], prod, ALU.add)
                        if j < CW - 1:
                            me.then(ins)
                ins.then_inc(s["conv_done"], 1)
                pool.wait_ge(s["conv_done"], i + 1)
            pool.wait_ge(s["conv_done"], CT)
            pool.wait_ge(s["mu_put"], 2)
            me.then(pool.tensor_tensor(conv, conv, mu.unsqueeze(1).to_broadcast([P, CT, TOK]), ALU.subtract))
            pool.tensor_tensor(sq, conv, conv, ALU.mult).then_inc(s["sq_ready"], 1)
            pool.wait_ge(s["sd_inv"], 1)
            me.then(pool.tensor_tensor(conv, conv, sd.unsqueeze(1).to_broadcast([P, CT, TOK]), ALU.mult))
            for c in range(CT):
                ins = pool.tensor_scalar(conv[:, c, :], conv[:, c, :], cst("g_ln")[:, c:c + 1], cst("b_ln")[:, c:c + 1], ALU.mult, ALU.add)
            ins.then_inc(s["ln_ready"], 1)
            for n in range(2 * TT):
                t, j = n // 2, n % 2
                m = tok(t)
                raw = h2raw[:, n % 2, :].rearrange("p (k t) -> p k t", k=4)[:, :, 0:m]
                hi = h2hi[:, 4 * j:4 * j + 4, t * P:t * P + m]
                pool.wait_ge(s["h2_raw"], n + 1)
                pool.tensor_copy(hi, raw).then_inc(s["h2_hi"], 1)
                pool.wait_ge(s["h2_hi"], n + 1)
                pool.tensor_tensor(h2lo[:, 4 * j:4 * j + 4, t * P:t * P + m], raw, hi.bitcast(F32), ALU.subtract).then_inc(s["h2_put"], 1)
            pool.wait_ge(s["mo_done"], 2 * TT)
            pool.wait_ge(s["hf_put"], 2)
            pool.memset(ux[:, :, :, 0:2], 0.0)
            pool.sem_inc(s["last_put"], 2)

            def rest_up(n, slot):
                pool.wait_ge(s["wu_hi"], n + 1)
                pool.tensor_tensor(wulo[:, slot, :, :], wu[slot].rearrange("p k u n -> p k (u n)"), wuhi[:, slot, :, :].bitcast(F32),
                                   ALU.subtract).then_inc(s["wu_lo"], 1)

            def up_step(i, slot, split_next=True):
                f = i * 2 + slot
                uh = ux[:, slot, :, 2 + TP_:UXW].rearrange("p u (b x) -> p u b x", b=NB)
                pool.wait_ge(s["cv_done"], f + 1)
                for u in range(2):
                    pool.tensor_copy(wdw[:, slot, u, :], dwv[:, u, bass.ds(f, 1), :].rearrange("p a j -> p (a j)"))
                    ins = pool.tensor_copy(uh[:, u, :, 0:2], histT[:, u, bass.ds(f, 1), :].rearrange("p a (b w) -> p (a b) w", w=2))
                ins.then_inc(s["taps_put"], 1)
                if split_next:
                    rest_up(f + 1, 1 - slot)
                pool.wait_ge(s["ux_put"], f * 4 + (8 + 4))
                for u in range(2):
                    lu = last[:, u, bass.ds(f, 1), :].rearrange("p a x -> p (a x)")
                    pool.tensor_copy(lu[:, 0:2], ux[:, slot, u, TP_:TP_ + 2])
                    ins = pool.tensor_copy(lu[:, 2:18].rearrange("p (b w) -> p b w", w=2), uh[:, u, :, UXS - 2:UXS])
                ins.then_inc(s["last_put"], 1)

            rest_up(0, 0)
            with pool.Fori(0, FT_N // 2 - 1) as i:
                for slot in range(2):
                    up_step(i, slot)
            up_step(FT_N // 2 - 1, 0)
            up_step(FT_N // 2 - 1, 1, split_next=False)
            with pool.Fori(0, FT_N // 2) as i:
                for slot in range(2):
                    pool.wait_ge(s["wd_hi"], i * 2 + (slot + 1))
                    pool.tensor_tensor(wdlo[:, slot, :, :], wd[:, slot, :, :], wdhi[:, slot, :, :].bitcast(F32), ALU.subtract).then_inc(s["wd_lo"], 1)


def _tables():
    import numpy as np

    r = np.arange(P)
    ident = np.eye(P, dtype=np.float32)
    causal = np.where(r[None, :] <= r[:, None], 0.0, -BIG).astype(np.float32)
    h4, q, i = r // 32, (r // 4) % 8, r % 4
    key = np.arange(2 * TS) - (TS - NT)
    own = np.where((i[:, None] == 0) & (key[None] >= 0) & (key[None] <= q[:, None]), 0.0, -BIG)
    n = np.arange(BLK)
    order = np.where(n[None, :] < n[:, None], 0.0, np.finfo(np.float32).tiny).astype(np.float32)
    denmap = np.zeros((P, 2, P), np.float32)
    hp, h4o, qo = r // 32, (r // 8) % 4, r % 8
    for g in range(2):
        denmap[:, g] = (h4[:, None] == h4o[None]) & (q[:, None] == qo[None]) & (hp[None] // 2 == g)
    flat = [ident, causal, own, np.broadcast_to(order.reshape(1, -1), (P, BLK * BLK)),
            denmap.reshape(P, -1)]
    return [np.ascontiguousarray(x, np.float32) for x in flat]


def _columns(v):
    import numpy as np

    return np.ascontiguousarray(np.asarray(v).reshape(-1, P).T)


_OUTS = [((1, TP_, D), "float32"), ((NB, NT, D), "float32"), ((1, 1, TP_, H, DH), "float32"),
         ((1, 1, TP_, H, DH), "float32"), ((1, 1, CW - 1, DA), "float32"), ((1, 1, 2, 2 * DFF), "float32"),
         ((1, NB, NT, H, DH), "float32"), ((1, NB, NT, H, DH), "float32"), ((1, NB, CW - 1, DA), "float32"),
         ((1, NB, 2, 2 * DFF), "float32")]
OUT_NAMES = ["y_p", "y_s", "k_p", "v_p", "cv_p", "ffn_p", "k_s", "v_s", "cv_s", "ffn_s"]
PLAIN = ["x_prompt", "x_sample", "cache_k", "cache_v", "page_table", "state_cv", "state_ffn", "w_in", "w_cv_pw",
         "w_out", "g_post_mix", "w_up", "w_down", "g_post_ffn"]


def lay_out(inputs):
    import numpy as np

    arrays = {n: np.ascontiguousarray(inputs[n]) for n in PLAIN}
    arrays["b_in_v"] = np.ascontiguousarray(np.asarray(inputs["b_in"])[0, 2 * DA:3 * DA])
    cvw = np.concatenate([np.asarray(inputs["w_cv_dw"])[0], np.asarray(inputs["b_cv_dw"])], 0)
    cvw = cvw.reshape(CW + 1, CT, P).transpose(2, 1, 0).reshape(P, -1)
    taps = np.concatenate([np.asarray(inputs["w_ffn_dw"])[0], np.asarray(inputs["b_ffn_dw"])], 0)
    dw = taps.reshape(4, 44, P).transpose(2, 1, 0).reshape(P, -1)
    vec = [_columns(inputs["b_in"]), cvw] + [_columns(inputs[n]) for n in
           ("g_cv_ln", "b_cv_ln", "b_cv_pw", "g_pre_mix", "g_pre_ffn")] + [dw]
    arrays["consts"] = np.ascontiguousarray(np.concatenate(_tables() + vec, 1))
    return arrays


def kernel(**inputs):
    import numpy as np
    import concourse.bacc as bacc
    from concourse.bass_utils import run_bass_kernel_spmd

    nc = bacc.Bacc("TRN2", target_bir_lowering=False, num_devices=1, dynamic_dma_scratch_size=1024)
    arrays = {"in_" + n: x for n, x in lay_out(inputs).items()}
    a = {n[3:]: nc.dram_tensor(n, x.shape, mybir.dt.from_np(x.dtype), kind="ExternalInput").ap()
         for n, x in arrays.items()}
    for n, (shape, dtype) in zip(OUT_NAMES, _OUTS):
        a[n] = nc.dram_tensor("out_" + n, shape, mybir.dt.from_np(np.dtype(dtype)), kind="ExternalOutput").ap()
    build_layer(nc, a)
    r = run_bass_kernel_spmd(nc, [arrays], core_ids=[0])
    return tuple(r.results[0]["out_" + n] for n in OUT_NAMES)
```

```python
from contextlib import ExitStack

import concourse.bass as bass
from concourse import mybir

ALU = mybir.AluOpType
ACT = mybir.ActivationFunctionType
AX = mybir.AxisListType
F32 = mybir.dt.float32
F32R = mybir.dt.float32r
I32 = mybir.dt.int32
BF16 = mybir.dt.bfloat16
P = 128

D = 1024
KC = D // P
TP_ = 512
NB, NT = 8, 8
TS = NB * NT
TOK = TP_ + TS
HALF = TOK // 2
TT = 5
H, DH = 8, 64
HP = H // 2
DA = H * DH
PAGES, PAGE = 32, 128
SUPER = 8
BLK = 16
CW = 31
CT = 4
GX = (CW - 1) + TP_
SX = CW - 1 + NT
GLUW = GX + NB * SX
DFF = 2816
FT_N = DFF // P
UXS = 2 + NT
UXW = 2 + TP_ + NB * UXS
SCALE = DH ** -0.5
BIG = 1.0e30
TOPK = 3
A_WORDS, B_WORDS = 19064, 30720
START = 1
ST1_AFTER, ST2_AFTER = 0, 2
TAPS = 10

CONST = {}
_at = 0
for _n, _w in (("ident", 128), ("causal", 128), ("ownmask", 2 * TS), ("order", BLK * BLK), ("denmap", 256),
               ("b_in", 20), ("w_cv", CT * (CW + 1)), ("g_ln", CT), ("b_ln", CT), ("b_pw", CT),
               ("g_pre", KC), ("g_ffn", KC), ("dw", 44 * 4)):
    CONST[_n] = (_at, _w)
    _at += _w
NCONST = _at


def tok(t):
    return P if t < 4 else TS


class Steps:

    def __init__(self, eng, sem, base=0):
        self.eng, self.sem, self.base, self.n = eng, sem, base, 0

    def then(self, ins):
        self.n += 1
        ins.then_inc(self.sem, 1)
        self.eng.wait_ge(self.sem, self.base + self.n)


def build_layer(nc, a):
    ctx = ExitStack()
    with ctx:
        def sem(name):
            return ctx.enter_context(nc.semaphore(name))

        def sb(name, shape, dt=F32):
            return ctx.enter_context(nc.sbuf_tensor(name, shape, dt))

        consts = sb("consts", [P, NCONST])
        small = sb("small", [P, 384])
        ones = sb("ones", [P, P])
        pages = sb("pages", [1, NB * PAGES], I32)
        base = {}
        base["hT"] = nc.sbuf_base
        hT_ = sb("hT", [P, KC * TOK])
        base["A"] = nc.sbuf_base
        A = sb("A", [P, A_WORDS])
        base["B"] = nc.sbuf_base
        B = sb("B", [P, B_WORDS])

        def rounded(name, mem, off, *dims):
            start = base["hT" if mem is hT_ else "A" if mem is A else "B"]
            return nc.alloc_sbuf_tensor_at(name, [P, *dims], F32R, offset=start + 4 * off)

        def cst(name, rows=P):
            o, w = CONST[name]
            return consts[0:rows, o:o + w]

        def at(mem, off, *dims):
            n = 1
            for d in dims:
                n *= d
            v = mem[:, off:off + n]
            if len(dims) == 2:
                return v.rearrange("p (a b) -> p a b", a=dims[0])
            if len(dims) == 3:
                return v.rearrange("p (a b c) -> p a b c", a=dims[0], b=dims[1])
            if len(dims) == 4:
                return v.rearrange("p (a b c d) -> p a b c d", a=dims[0], b=dims[1], c=dims[2])
            return v

        ident = cst("ident")
        causal = cst("causal")
        ownmask = cst("ownmask")
        order = cst("order").rearrange("p (n m) -> p n m", n=BLK)
        denmap = cst("denmap").rearrange("p (g r) -> p g r", g=2)
        b_in = cst("b_in")
        w_cv = cst("w_cv").rearrange("p (c j) -> p c j", c=CT)
        dwv = cst("dw").rearrange("p (u f j) -> p u f j", u=2, f=FT_N)

        hT = hT_[:, :].rearrange("p (k t) -> p k t", k=KC)
        mixT = hT
        qZ = at(A, 0, HP, 2, TP_)
        kP = at(A, 4096, HP, TP_)
        vP = at(A, 6144, TT, DA)
        glu = at(A, 8704, CT, GLUW)
        conv = at(A, 12088, CT, TOK)
        oT = at(A, 14392, NB, P)
        qR = at(A, 15416, 2 * H, TS)
        qS = at(A, 16440, 2 * H, 32)
        kTs = at(A, 16952, HP, TS)
        kOwn = at(A, 17208, 2 * H, TS)
        sig = at(A, 18232, TOK)
        qTs = at(A, 18232, HP, TS)
        kN = at(B, 0, 4, 4, DA)
        kT = at(B, 8192, 4, 2 * H, P)
        vN = at(B, 16384, 4, 4, DA)
        wz = at(B, 24576, KC, 2, P)
        S = at(B, 26624, 2, 1024)
        pT = at(B, 28672, 2, SUPER, P)
        rank = at(B, 28672, 2 * BLK * BLK)
        rankv = rank.rearrange("p (g n m) -> p g n m", g=2, n=BLK)
        vT = at(B, 28672, TP_)
        xA = at(B, 8192, TT, D)
        junkA = at(B, 13312, D)
        histN = at(A, 14392, 2, DA)
        bvB = at(A, 12088, DA)
        wq = at(B, 16384, KC, DA)
        wv = at(B, 20480, KC, DA)
        wk = at(B, 26624, KC, DA)
        pP = at(B, 0, 2, 4, TP_)
        pPT = at(B, 4096, 2, 4, TP_)
        x1 = at(B, 8192, TT, D)
        kNat = at(B, 13312, TT, DA)
        wpw = at(B, 15872, CT, DA)
        gPost = at(A, 4096, D)
        cvN = at(B, 18944, 2, DA)
        mu = at(B, 19968, TOK)
        sd = at(B, 20544, TOK)
        sq = at(B, 21120, CT, TOK)
        histF = at(B, 24576, 2 * DFF)
        gluS = at(A, 17208, CT, TS)
        wo = at(B, 0, KC, D)
        t1 = at(A, 0, 2, D)
        junk = at(A, 2048, D)
        h2raw = at(A, 3072, 2, TP_)
        h2hi = rounded("h2hi", A, 14392, KC, TOK)
        h2lo = rounded("h2lo", B, 24576, KC, TOK)
        fT = at(A, 0, FT_N, TOK)
        histT = at(A, 12672, 2, FT_N, 16)
        last = at(A, 13376, 2, FT_N, 18)
        ux = at(B, 0, 2, 2, UXW)
        cvo = at(B, 2376, 2, 2, TOK)
        sg2 = at(B, 4680, 2, TOK)
        wu = [at(B, 13312 + 2048 * i, KC, 2, P) for i in range(2)]
        wuhi = [rounded("wuhi0", B, 17408, KC, 2 * P), rounded("wuhi1", hT_, 2048, KC, 2 * P)]
        wulo = rounded("wulo", B, 19968, 2, KC, 2 * P)
        wd = at(B, 5832, 2, 2, TP_)
        wdhi = rounded("wdhi", hT_, 0, 2, 2, TP_)
        wdlo = rounded("wdlo", hT_, 2048, 2, 2, TP_)
        fThi = rounded("fThi", A, 14392, 2, 2, TOK)
        fTlo = rounded("fTlo", A, 14392 + 4 * TOK, 2, 2, TOK)
        gFfn = at(B, 2560, D)
        y0 = at(B, 0, TT, TP_)
        yo = at(B, 13312, TT, D)
        junkY = at(B, 4680, TP_)
        ss = small[:, 0:8]
        rstd = small[:, 8:16]
        bsum, bmax, pen, tA, tB, tC = (small[:, 32 + 32 * i:64 + 32 * i] for i in range(6))
        mcol = small[:, 224:256]
        nb = small[:, 16:18]
        rs = small[:, 18:22]
        rsum = small[:, 22:24]
        rden = small[:, 24:25]
        nbg = small[:, 25:29]
        epsr = small[:, 29:30]
        epsl = small[:, 30:31]
        mx2 = small[:, 256:260]
        pm = small[:, 260:268]
        pnb = small[:, 268:276]
        prs = small[:, 276:284]
        prr = small[:, 284:292]
        ss2 = small[:, 292:312]
        r2 = small[:, 312:332]
        wdw = at(small, 332, 2, 2, 4)
        ss3 = small[:, 348:364]
        r3 = small[:, 364:372]
        own = sb("own", [P, 2 * TS])
        ownS = own[:, :].rearrange("p (g k) -> p g k", g=2)
        pTo_ = sb("pTo", [P, 2 * P])
        pTo = pTo_[:, :].rearrange("p (g r) -> p g r", g=2)
        oN = sb("oN", [P, P])
        mask16 = oN[:, :].bitcast(BF16)
        ident16, causal16 = mask16[:, 0:P], mask16[:, P:2 * P]

        banks = {n: ctx.enter_context(nc.psum_tensor(n, [P, 512], F32))
                 for n in ("z0", "z1", "sc0", "sc1", "tp0", "tp1", "ob", "sm")}
        Z = [banks["z0"], banks["z1"]]
        SC = [banks["sc0"], banks["sc1"]]
        TB = [banks["tp0"], banks["tp1"]]
        OB, SM = banks["ob"], banks["sm"]
        own_ps = SM[:, 0:128].rearrange("p (g k) -> p g k", g=2)
        den_ps = OB[:, 384:385]

        names = """
            c_loaded pt_loaded hist_loaded bv_loaded wq_loaded wk_loaded wv_loaded
            x_loaded0 x_loaded1 x_loaded2 x_loaded3 x_loaded4
            kn_full0 kn_full1 kn_full2 kn_full3 v_full0 v_full1 v_full2 v_full3 wz_full
            xr_loaded wpw_loaded gpost_loaded histf_loaded wo_loaded gffn_loaded
            wu_full0 wu_full1 wd_full0 wd_full1
            stored_kv stored_ffn stored_y
            act_step dve_step pool_step soft_step pst_step mo_step f_step y_step conv_step pool_set
            x_summed x_scaled xt_done ht_ready hist_done hist_put zq_done zq_putA zq_putV
            ks_done ks_put kown_put vs_done vs_put qr_ready qs_ready
            kt_ready scores_done s_put own_done nb_ready probs_ready rsum_ready
            p_turned pt_put own_turned pto_put den_done den_inv pv_done o_norm ot_done ot_put
            z1_done g_bias g_exp sig_ready z1_put tail_conv
            v2_done v2_put v2_turned v2_home k2_done k2_put
            knat_done knat_put glus_put glun_done glun_put mix_put mask_put
            ps_done pnb_ready pexp pnorm pt2_done ptt_put pv2_done o2_put
            conv_done st1_done mu_put sq_ready st2_done sd_put sd_inv ln_ready sg_put c_ready
            pw_done pw_put hf_done hf_put
            mo_done mo_sq mo_sum mo_rt t1_put x1_ready x1_sq x1_rt h2_ready h2_done h2_raw h2_hi h2_put
            wu_hi wu_lo up_done ux_put taps_put last_put g_conv g_sig cv_done ft_ready ul_done ul_put
            wd_hi wd_lo ft_hi ft_lo dn_done
            y_done y_sq y_sum y_rt y_inv y0_put yo_left yo_ready0 yo_ready1""".split()
        s = {n: sem(n) for n in names}
        block = ctx.enter_context(nc.Block())

        w_in = a["w_in"][0].rearrange("(k p) n -> p k n", p=P)
        ck = a["cache_k"][0].rearrange("f k h d -> f k (h d)")
        cv = a["cache_v"][0].rearrange("f k h d -> f k (h d)")
        kn_full = [s[f"kn_full{i}"] for i in range(4)]
        v_full = [s[f"v_full{i}"] for i in range(4)]

        @block.sync
        def _(sp):
            sp.dma_start(pages[:], a["page_table"].rearrange("(o b) n -> o (b n)", o=1)).then_inc(s["pt_loaded"], 16)
            for t in range(TT):
                src = a["x_prompt"][0, t * P:(t + 1) * P, :] if t < 4 else a["x_sample"].rearrange("b t n -> (b t) n")
                sp.dma_start(xA[0:tok(t), t, :], src).then_inc(s[f"x_loaded{t}"], 16)
            sp.dma_start(wq, w_in[:, :, 0:DA]).then_inc(s["wq_loaded"], 16)
            sp.dma_start(wk, w_in[:, :, DA:2 * DA]).then_inc(s["wk_loaded"], 16)
            sp.wait_ge(s["pt_loaded"], 16)

            def page_numbers(b, u):
                _, numbers = nc.values_load_multi_w_load_instructions(
                    pages[0:1, bass.ds(b * PAGES + 4 * u, 8)], engines=[mybir.EngineType.SP], min_val=0,
                    max_val=ck.shape[0] - 1, skip_runtime_bounds_check_because="a page table holds numbers of pages of the pool")
                return numbers

            def load_k(b, u, freed=None):
                numbers = page_numbers(b, u)
                for v in (u, u + 1):
                    if freed is not None:
                        sp.wait_ge(s["kt_ready"], freed + v)
                    for i in range(4):
                        sp.dma_start(kN[:, v % 4, i, :], ck[bass.ds(numbers[4 * (v - u) + i], 1)].rearrange("a k n -> (a k) n")
                                     ).then_inc(kn_full[v % 4], 16)

            def load_v(b, u, freed=None, home=vN, full=v_full):
                numbers = page_numbers(b, u)
                for v in (u, u + 1):
                    if freed is not None:
                        sp.wait_ge(s["pv_done"], freed + v)
                    for i in range(4):
                        sp.dma_start(home[32 * i:32 * i + 32, v % 4, :, :],
                                     cv[bass.ds(numbers[4 * (v - u) + i], 1)].rearrange("a (g r) n -> (a r) g n", g=4)
                                     ).then_inc(full[v % 4], 16)

            load_k(0, 0)
            sp.dma_start(wv, w_in[:, :, 2 * DA:3 * DA]).then_inc(s["wv_loaded"], 16)
            load_k(0, 2)
            load_k(0, 4, freed=-3)
            load_k(0, 6, freed=-3)

            def wz_glu(i):
                sp.dma_start(wz[:, :, 0, :], w_in[:, :, bass.ds(4 * DA + i * P, P)]).then_inc(s["wz_full"], 16)
                sp.dma_start(wz[:, :, 1, :], w_in[:, :, bass.ds(3 * DA + i * P, P)]).then_inc(s["wz_full"], 16)

            def wz_kv(i):
                sp.dma_start(wz[:, :, 0, :], w_in[:, :, bass.ds(2 * DA + i * P, P)]).then_inc(s["wz_full"], 16)
                sp.dma_start(wz[:, :, 1, :], w_in[:, :, bass.ds(DA + i * P, P)]).then_inc(s["wz_full"], 16)

            def step(b, load_w, first=False, last=False):
                load_w()
                if first:
                    sp.wait_ge(s["zq_done"], 2 * HP)
                else:
                    sp.wait_ge(s["pv_done"], b * 8 + START)
                load_v(b, 0)
                if first:
                    sp.wait_ge(s["vs_done"], 1)
                load_v(b, 2)
                if not last:
                    for u in (0, 2, 4):
                        load_k(b + 1, u, freed=b * 8 + (8 - 3))
                if last:
                    sp.wait_ge(s["kt_ready"], NB * SUPER)
                for u in (4, 6):
                    if last:
                        load_v(b, u, home=kN, full=kn_full)
                    else:
                        load_v(b, u, freed=b * 8 + (START - 3))
                if not last:
                    load_k(b + 1, 6, freed=b * 8 + (8 - 3))

            def w1(i):
                sp.wait_ge(s["z1_done"], i * 4 + START)
                wz_glu(i)

            def w2(i):
                sp.wait_ge(s["z1_done"], 16 + START)
                sp.wait_ge(s["k2_done"], i + START)
                wz_kv(i)

            step(0, lambda: wz_glu(0), first=True)
            with sp.Fori(0, 3) as i:
                step(i + 1, lambda: w1(i + 1))
            with sp.Fori(0, 3) as i:
                step(i + 4, lambda: w2(i))
            step(7, lambda: w2(3), last=True)
            sp.wait_ge(s["scores_done"], 4 * NB)
            sp.wait_ge(s["p_turned"], 4 * NB + START)
            sp.wait_ge(s["pv_done"], SUPER * NB + START)
            sp.dma_start(wpw, a["w_cv_pw"][0].rearrange("(k p) n -> p k n", p=P)).then_inc(s["wpw_loaded"], 16)
            sp.dma_start(x1[:, 0:4, :], a["x_prompt"][0].rearrange("(t p) n -> p t n", p=P)).then_inc(s["xr_loaded"], 16)
            sp.dma_start(x1[0:TS, 4, :], a["x_sample"].rearrange("b t n -> (b t) n")).then_inc(s["xr_loaded"], 16)
            sp.dma_start(histF[0:16, :], a["state_ffn"][0].rearrange("b w n -> (b w) n")).then_inc(s["histf_loaded"], 16)
            sp.wait_ge(s["pv2_done"], H)
            sp.dma_start(wo, a["w_out"][0].rearrange("(k p) n -> p k n", p=P)).then_inc(s["wo_loaded"], 16)
            sp.dma_start(gPost, a["g_post_mix"][0].partition_broadcast(P)).then_inc(s["gpost_loaded"], 16)
            w_up = a["w_up"][0].rearrange("(k p) n -> p k n", p=P)
            wu_full = [s["wu_full0"], s["wu_full1"]]

            def load_up(f, slot):
                for u in range(2):
                    sp.dma_start(wu[slot][:, :, u, :], w_up[:, :, bass.ds(f * P + u * DFF, P)]).then_inc(wu_full[slot], 16)

            sp.wait_ge(s["pw_done"], 2 * CT)
            sp.wait_ge(s["stored_kv"], 16 * 7)
            load_up(0, 0)
            load_up(1, 1)
            with sp.Fori(0, FT_N // 2 - 1) as i:
                for slot in range(2):
                    sp.wait_ge(s["wu_lo"], i * 2 + (slot + 1))
                    load_up(i * 2 + (2 + slot), slot)
            w_dn = a["w_down"][0].rearrange("(k p) n -> p k n", p=P)
            wd_full = [s["wd_full0"], s["wd_full1"]]

            def load_down(nh, kk, slot):
                sp.dma_start(wd[:, slot, :, :], w_dn[:, bass.ds(kk * 2, 2), nh * TP_:(nh + 1) * TP_]).then_inc(wd_full[slot], 16)

            load_down(0, 0, 0)
            load_down(0, 1, 1)
            sp.wait_ge(s["ft_ready"], FT_N)
            sp.wait_ge(s["last_put"], FT_N + 2)
            sp.dma_start(gFfn, a["g_post_ffn"][0].partition_broadcast(P)).then_inc(s["gffn_loaded"], 16)
            with sp.Fori(0, 4) as i:
                for j in range(2):
                    sp.wait_ge(s["wd_lo"], i * 2 + (j + 1))
                    load_down(0, i * 2 + (2 + j), j)
            sp.wait_ge(s["wd_lo"], 9)
            load_down(0, 10, 0)
            with sp.Fori(0, 5) as i:
                for j in range(2):
                    sp.wait_ge(s["wd_lo"], i * 2 + (10 + j))
                    load_down(1, i * 2 + j, 1 - j)
            sp.wait_ge(s["wd_lo"], 20)
            load_down(1, 10, 1)
            sp.wait_ge(s["ul_put"], 11)
            sp.dma_start(a["ffn_p"][0, 0], histF[0:2, :]).then_inc(s["stored_ffn"], 16)
            sp.dma_start(a["ffn_s"][0].rearrange("b w n -> (b w) n"), histF[2:18, :]).then_inc(s["stored_ffn"], 16)
            for t in range(TT):
                sp.wait_ge(s["yo_ready0"], t + 1)
                sp.wait_ge(s["yo_ready1"], t + 1)
                dst = a["y_p"][0, t * P:(t + 1) * P, :] if t < 4 else a["y_s"].rearrange("b t n -> (b t) n")
                sp.dma_start(dst, yo[0:tok(t), t, :]).then_inc(s["stored_y"], 16)
            sp.wait_ge(s["stored_kv"], 16 * 7)
            sp.wait_ge(s["stored_ffn"], 16 * 2)
            sp.wait_ge(s["stored_y"], 16 * TT)

        @block.tensor
        def _(pe):
            for n in ("up_done", "z1_done", "pv_done", "k2_done", "p_turned", "own_turned", "den_done", "ot_done"):
                pe.sem_inc(s[n], START)
            pe.wait_ge(s["c_loaded"], 16)
            pe.wait_ge(s["pool_set"], 1)
            turn = [TB[0], TB[1], SC[0], SC[1]]
            for t in range(TT):
                pe.wait_ge(s["x_scaled"], t + 1)
                for j in range(2):
                    n = 2 * t + j
                    if n >= 4:
                        pe.wait_ge(s["ht_ready"], n - 3)
                    for k in range(4):
                        ins = pe.transpose(turn[n % 4][:, k * P:k * P + tok(t)],
                                           xA[0:tok(t), t, (4 * j + k) * P:(4 * j + k + 1) * P],
                                           ident[0:tok(t), 0:tok(t)])
                    ins.then_inc(s["xt_done"], 1)
            pe.wait_ge(s["ht_ready"], 2 * TT)
            pe.wait_ge(s["wq_loaded"], 16)
            for hp in range(HP):
                for half in range(2):
                    if hp:
                        pe.wait_ge((s["zq_putA"], s["zq_putV"])[half], hp)
                    for k in range(KC):
                        ins = pe.matmul(Z[half][:, 0:HALF], wq[:, k, hp * P:(hp + 1) * P],
                                        hT[:, k, half * HALF:(half + 1) * HALF], start=(k == 0), stop=(k == KC - 1))
                    ins.then_inc(s["zq_done"], 1)
            pe.wait_ge(s["hist_loaded"], 16)
            for r in range(2):
                for c in range(CT):
                    ins = pe.transpose((OB, SM)[r][:, c * 120:(c + 1) * 120], histN[0:120, r, c * P:(c + 1) * P],
                                       ident[0:120, 0:120])
                ins.then_inc(s["hist_done"], 1)
            pe.wait_ge(s["wk_loaded"], 16)
            for hp in range(HP):
                for k in range(KC):
                    ins = pe.matmul(TB[0][:, hp * TS:(hp + 1) * TS], wk[:, k, hp * P:(hp + 1) * P],
                                    hT[:, k, TP_:TOK], start=(k == 0), stop=(k == KC - 1))
            ins.then_inc(s["ks_done"], 1)
            pe.wait_ge(s["wv_loaded"], 16)
            for k in range(KC):
                ins = pe.matmul(TB[1][0:TS, :], hT[:, k, TP_:TOK], wv[:, k, :], start=(k == 0), stop=(k == KC - 1))
            ins.then_inc(s["vs_done"], 1)

            def scores(b, js):
                if js[0] == 0:
                    pe.wait_ge(s["qs_ready"], b + 1)
                for j in js:
                    pe.wait_ge(s["kt_ready"], b * 8 + (2 * j + 2))
                    pe.wait_ge(s["s_put"], b * 4 + max(j - 1, 0) + START)
                    for g in range(2):
                        for c in range(2):
                            for h4 in range(4):
                                hc = 2 * (4 * g + h4) + c
                                ins = pe.matmul(SC[j % 2][32 * h4:32 * h4 + 32, g * 256:(g + 1) * 256]
                                                .rearrange("p (a k) -> p a k", a=2),
                                                qS[:, hc, :], kT[:, 2 * (j % 2):2 * (j % 2) + 2, hc, :],
                                                start=(c == 0), stop=(c == 1))
                    ins.then_inc(s["scores_done"], 1)
                if js[0] == 0:
                    return
                for g in range(2):
                    for c in range(2):
                        for h4 in range(4):
                            hc = 2 * (4 * g + h4) + c
                            ins = pe.matmul(SM[32 * h4:32 * h4 + 32, g * TS:(g + 1) * TS], qS[:, hc, :], kOwn[:, hc, :],
                                            start=(c == 0), stop=(c == 1))
                ins.then_inc(s["own_done"], 1)

            def first_values(b):
                for n in range(4):
                    g, quad = n // 2, n % 2
                    pe.wait_ge(s["probs_ready"], b * 3 + (g + 1 if n < 3 else 3))
                    pe.wait_ge(s["pt_put"], b * 4 + max(n - 1, 0) + START)
                    for u in range(4):
                        v = 4 * quad + u
                        ins = pe.transpose(TB[n % 2][:, u * P:(u + 1) * P], S[:, g, v * P:(v + 1) * P], ident)
                    ins.then_inc(s["p_turned"], 1)
                for g in range(2):
                    ins = pe.transpose(SM[0:TS, P + g * P:P + (g + 1) * P], ownS[:, g, :], ident)
                ins.then_inc(s["own_turned"], 1)
                pe.wait_ge(s["rsum_ready"], b + 1)
                pe.wait_ge(s["o_norm"], b + START)
                for g in range(2):
                    ins = pe.matmul(den_ps, denmap[:, g, :], rsum[:, g:g + 1], start=(g == 0), stop=(g == 1))
                ins.then_inc(s["den_done"], 1)
                pe.wait_ge(s["pto_put"], b + 1)
                pTo4 = pTo.rearrange("p g (r i) -> p g i r", i=4)
                for hp in range(HP):
                    pe.matmul(OB[32 * hp:32 * hp + 32, 0:P], pTo4[:, hp // 2, 0, :], vP[:, 4, hp * P:(hp + 1) * P],
                              start=True, stop=False)
                weigh(b, range(4))

            def weigh(b, us, home=vN):
                for u in us:
                    if home is kN:
                        pe.wait_ge(kn_full[u % 4], NB * 128 + 64)
                    else:
                        pe.wait_ge(v_full[u % 4], b * 128 + 64 * (u // 4 + 1))
                    if u == 0:
                        pe.wait_ge(s["pt_put"], b * 4 + 4 + START)
                    for i in range(4):
                        for hp in range(HP):
                            w = pT[:, hp // 2, u, :].rearrange("p (r i) -> p i r", i=4)[:, i, :]
                            ins = pe.matmul(OB[32 * hp:32 * hp + 32, 0:P], w, home[:, u % 4, i, hp * P:(hp + 1) * P],
                                            start=False, stop=(u == SUPER - 1 and i == 3))
                    ins.then_inc(s["pv_done"], 1)

            def last_values(b, home=vN):
                weigh(b, range(4, SUPER), home)
                pe.wait_ge(s["o_norm"], b + 1 + START)
                pe.wait_ge(s["pt_put"], b * 4 + 4 + START)
                pe.transpose(TB[0][:, 0:P], oN[:, :], ident).then_inc(s["ot_done"], 1)

            def glu_tiles(i):
                pe.wait_ge(s["wz_full"], i * 32 + 32)
                for n in range(4):
                    u, half = n // 2, n % 2
                    if u:
                        pe.wait_ge(s["g_exp"], i * 2 + (half + 1) + START)
                    else:
                        pe.wait_ge(s["z1_put"], i * 2 + START)
                    for k in range(KC):
                        ins = pe.matmul(Z[half][:, 0:HALF], wz[:, k, u, :], hT[:, k, half * HALF:(half + 1) * HALF],
                                        start=(k == 0), stop=(k == KC - 1))
                    ins.then_inc(s["z1_done"], 1)

            def kv_tiles(i):
                pe.wait_ge(s["wz_full"], i * 32 + 160)
                pe.wait_ge(s["z1_put"], 8 + START)
                pe.wait_ge(s["v2_put"], i + START)
                for k in range(KC):
                    ins = pe.matmul(Z[0][:, 0:TP_], wz[:, k, 0, :], hT[:, k, 0:TP_], start=(k == 0), stop=(k == KC - 1))
                ins.then_inc(s["v2_done"], 1)
                pe.wait_ge(s["k2_put"], i + START)
                for k in range(KC):
                    ins = pe.matmul(Z[1][:, 0:TP_], wz[:, k, 1, :], hT[:, k, 0:TP_], start=(k == 0), stop=(k == KC - 1))
                ins.then_inc(s["k2_done"], 1)
                pe.wait_ge(s["v2_put"], i + 1 + START)
                pe.wait_ge(s["ot_put"], i + 4 + START)
                for t in range(4):
                    ins = pe.transpose(TB[0][:, t * P:(t + 1) * P], vT[:, t * P:(t + 1) * P], ident)
                ins.then_inc(s["v2_turned"], 1)
                pe.wait_ge(s["v2_home"], i + 1)

            pe.wait_ge(s["kown_put"], 1)
            scores(0, (0, 1))
            with pe.Fori(0, 4) as i:
                scores(i, (2, 3))
                glu_tiles(i)
                pe.wait_ge(s["ot_put"], i + START)
                first_values(i)
                scores(i + 1, (0, 1))
                last_values(i)
            with pe.Fori(0, 3) as i:
                scores(i + 4, (2, 3))
                kv_tiles(i)
                first_values(i + 4)
                scores(i + 5, (0, 1))
                last_values(i + 4)
            scores(7, (2, 3))
            kv_tiles(3)
            first_values(7)
            last_values(7, kN)
            pe.wait_ge(s["k2_put"], 4 + START)
            pe.wait_ge(s["ot_put"], NB + START)
            nat = [TB[0], TB[1], SM, TB[0], TB[1]]
            for t in range(TT):
                if t >= 3:
                    pe.wait_ge(s["knat_put"], t - 2)
                for hp in range(HP):
                    src = kP[:, hp, t * P:(t + 1) * P] if t < 4 else kTs[:, hp, :]
                    ins = pe.transpose(nat[t][0:tok(t), hp * P:(hp + 1) * P], src, ident)
                ins.then_inc(s["knat_done"], 1)
            pe.wait_ge(s["knat_put"], 3)
            pe.wait_ge(s["glus_put"], 1)
            for c in range(CT):
                ins = pe.transpose(SM[0:CW - 1, c * P:(c + 1) * P], glu[:, c, TP_:GX], ident)
            ins.then_inc(s["glun_done"], 1)
            pe.wait_ge(s["o_norm"], NB + START)
            for c in range(CT):
                ins = pe.transpose(OB[0:TS, c * P:(c + 1) * P], gluS[:, c, :], ident)
            ins.then_inc(s["glun_done"], 1)
            pe.wait_ge(s["knat_put"], TT)
            sb_ = [Z[0], Z[1], SC[0], SC[1]]
            pe.wait_ge(s["s_put"], 4 * NB + START)
            pe.wait_ge(s["v2_home"], 4)
            pe.wait_ge(s["mask_put"], 1)

            def s_head(h):
                hp, e = h // 2, h % 2
                for t in range(4):
                    if h:
                        pe.wait_ge(s["pexp"], 4 * (h - 1) + t + 1)
                    n = (t + 1) * P
                    pe.matmul(sb_[t][:, 0:n], qZ[:, hp, e, t * P:(t + 1) * P], kP[:, hp, 0:n], start=True, stop=False)
                    pe.matmul(sb_[t][:, n - P:n], ident16, causal16, start=False, stop=True).then_inc(s["ps_done"], 1)

            def t_head(h):
                pe.wait_ge(s["pnorm"], 4 * h + 4)
                for kb in range(4):
                    n = 4 * h + kb
                    if n >= 2:
                        pe.wait_ge(s["ptt_put"], n - 1)
                    for t in range(kb, 4):
                        ins = pe.transpose(TB[kb % 2][:, t * P:(t + 1) * P], pP[:, h % 2, t, kb * P:(kb + 1) * P], ident)
                    ins.then_inc(s["pt2_done"], 1)

            def pv_head(h):
                hp, e = h // 2, h % 2
                bank = (OB, SM)[hp % 2]
                if hp >= 2:
                    pe.wait_ge(s["o2_put"], hp - 1)
                else:
                    pe.wait_ge(s["glun_put"], 2)
                for kb in range(4):
                    pe.wait_ge(s["ptt_put"], 4 * h + kb + 1)
                    ins = pe.matmul(bank[64 * e:64 * e + 64, kb * P:TP_], vP[:, kb, h * DH:(h + 1) * DH],
                                    pPT[:, h % 2, kb, kb * P:TP_], start=(kb == 0), stop=(kb == 3))
                ins.then_inc(s["pv2_done"], 1)

            s_head(0)
            for h in range(H):
                if h + 1 < H:
                    s_head(h + 1)
                if h:
                    pv_head(h - 1)
                t_head(h)
                if h == ST1_AFTER:
                    pe.wait_ge(s["conv_done"], CT - 1)
                    pe.wait_ge(s["tail_conv"], 1 + 3 * TAPS)
                    pe.wait_ge(s["ptt_put"], 4 * h + 4)
                    for half in range(2):
                        for c in range(CT):
                            ins = pe.matmul(TB[half][:, 0:HALF], ones[:, :], conv[:, c, half * HALF:(half + 1) * HALF],
                                            start=(c == 0), stop=(c == CT - 1))
                        ins.then_inc(s["st1_done"], 1)
                    pe.wait_ge(s["mu_put"], 2)
                if h == ST2_AFTER:
                    pe.wait_ge(s["sq_ready"], 1)
                    pe.wait_ge(s["ptt_put"], 4 * h + 4)
                    for half in range(2):
                        for c in range(CT):
                            ins = pe.matmul(TB[half][:, 0:HALF], ones[:, :], sq[:, c, half * HALF:(half + 1) * HALF],
                                            start=(c == 0), stop=(c == CT - 1))
                        ins.then_inc(s["st2_done"], 1)
                    pe.wait_ge(s["sd_put"], 2)
            pv_head(H - 1)
            pe.wait_ge(s["histf_loaded"], 16)
            pe.wait_ge(s["ptt_put"], 4 * H)
            for r in range(2):
                for f in range(FT_N):
                    g = r * FT_N + f
                    ins = pe.transpose(TB[r][:, f * 16:(f + 1) * 16], histF[0:16, g * P:(g + 1) * P], ident[0:16, 0:16])
                ins.then_inc(s["hf_done"], 1)
            pe.wait_ge(s["wpw_loaded"], 16)
            pe.wait_ge(s["c_ready"], 1)
            for m in range(CT):
                for half in range(2):
                    n = 2 * m + half
                    if n >= 4:
                        pe.wait_ge(s["pw_put"], n - 3)
                    for c in range(CT):
                        ins = pe.matmul(sb_[n % 4][:, 0:HALF], wpw[:, c, m * P:(m + 1) * P],
                                        conv[:, c, half * HALF:(half + 1) * HALF], start=(c == 0), stop=(c == CT - 1))
                    ins.then_inc(s["pw_done"], 1)
            pe.wait_ge(s["wo_loaded"], 16)
            pe.wait_ge(s["pw_put"], 2 * CT)
            pe.wait_ge(s["mix_put"], 1)
            pe.wait_ge(s["o2_put"], HP)
            turn2 = [TB[0], TB[1], OB, SM]
            pe.wait_ge(s["hf_put"], 2)

            def mix_tile(t):
                m = tok(t)
                for nh in range(2):
                    if t >= 2:
                        pe.wait_ge(s["t1_put"], 2 * (t - 2) + nh + 1)
                    for k in range(KC):
                        ins = pe.matmul(sb_[2 * (t % 2) + nh][0:m, :], mixT[:, k, t * P:t * P + m],
                                        wo[:, k, nh * TP_:(nh + 1) * TP_], start=(k == 0), stop=(k == KC - 1))
                    ins.then_inc(s["mo_done"], 1)

            def h2_tile(t):
                m = tok(t)
                pe.wait_ge(s["h2_ready"], t + 1)
                for j in range(2):
                    n = 2 * t + j
                    if n >= 4:
                        pe.wait_ge(s["h2_put"], n - 3)
                    for k in range(4):
                        ins = pe.transpose(turn2[n % 4][:, k * P:k * P + m], t1[0:m, t % 2, (4 * j + k) * P:(4 * j + k + 1) * P],
                                           ident[0:m, 0:m])
                    ins.then_inc(s["h2_done"], 1)

            bank8 = [OB, SM, TB[0], TB[1]] + sb_

            def up_group(i, slot, n):
                half, u = n // 2, n % 2
                for k in range(KC):
                    for j, (w, x) in enumerate(((wuhi[slot][:, k], h2hi), (wuhi[slot][:, k], h2lo), (wulo[:, slot, k], h2hi))):
                        ins = pe.matmul(bank8[4 * slot + n][:, 0:HALF], w[:, u * P:(u + 1) * P],
                                        x[:, k, half * HALF:(half + 1) * HALF], start=(k == 0 and j == 0),
                                        stop=(k == KC - 1 and j == 2))
                ins.then_inc(s["up_done"], 1)

            def up_tile(i, slot):
                pe.wait_ge(s["wu_lo"], i * 2 + (slot + 1))
                for n in range(4):
                    pe.wait_ge(s["ux_put"], i * 8 + (4 * slot + n + 1))
                    up_group(i, slot, n)

            mix_tile(0)
            for t in range(TT - 1):
                mix_tile(t + 1)
                h2_tile(t)
            pe.wait_ge(s["h2_put"], 6)
            pe.wait_ge(s["h2_raw"], 8)
            pe.wait_ge(s["wu_lo"], 1)
            up_group(0, 0, 0)
            up_group(0, 0, 1)
            h2_tile(TT - 1)
            pe.wait_ge(s["h2_put"], 2 * TT)
            up_group(0, 0, 2)
            up_group(0, 0, 3)
            pe.wait_ge(s["t1_put"], 2 * TT)
            up_tile(0, 1)
            with pe.Fori(0, FT_N // 2 - 1) as i:
                for slot in range(2):
                    up_tile(i + 1, slot)
            db = [[Z[0], Z[1], SC[0], SC[1], TB[0]], [TB[1], OB, SM, Z[0], Z[1]]]

            def down_pair(nh, kk, slot, first=False, last=False):
                pe.wait_ge(s["wd_lo"], kk + (11 * nh + 1))
                pe.wait_ge(s["ft_lo"], kk + (11 * nh + 1))
                order = [(k2, t) for t in range(TT) for k2 in range(2)] if last else [(k2, t) for k2 in range(2) for t in range(TT)]
                for k2, t in order:
                    m = tok(t)
                    if nh and first and k2 == 0:
                        if t >= 3:
                            pe.wait_ge(s["y0_put"], t - 2)
                        elif t == 0:
                            pe.wait_ge(s["ul_put"], 11)
                    for j, (x, w) in enumerate(((fThi, wdhi), (fThi, wdlo), (fTlo, wdhi))):
                        ins = pe.matmul(db[nh][t][0:m, :], x[:, slot, k2, t * P:t * P + m], w[:, slot, k2, :],
                                        start=(first and k2 == 0 and j == 0), stop=(last and k2 == 1 and j == 2))
                    if last and k2 == 1:
                        ins.then_inc(s["y_done"], 1)
                if not last:
                    ins.then_inc(s["dn_done"], 1)

            def states_to_rows():
                pe.wait_ge(s["last_put"], FT_N + 2)
                for n in range(11):
                    if n >= 3:
                        pe.wait_ge(s["ul_put"], n - 2)
                    for j in range(4):
                        g = 4 * n + j
                        ins = pe.transpose((TB[1], OB, SM)[n % 3][0:18, j * P:(j + 1) * P], last[:, g // FT_N, g % FT_N, :], ident)
                    ins.then_inc(s["ul_done"], 1)

            pe.wait_ge(s["ux_put"], 8 + 4 * FT_N)
            for nh in range(2):
                down_pair(nh, 0, nh, first=True)
                if nh == 0:
                    states_to_rows()
                with pe.Fori(0, 4) as i:
                    for j in range(2):
                        down_pair(nh, i * 2 + (1 + j), (nh + 1 + j) % 2)
                down_pair(nh, 9, (nh + 1) % 2)
                down_pair(nh, 10, nh, last=True)

        @block.scalar
        def _(act):
            act.dma_start(consts[:], a["consts"]).then_inc(s["c_loaded"], 16)
            act.dma_start(bvB[0:TS, :], a["b_in_v"].partition_broadcast(TS)).then_inc(s["bv_loaded"], 16)
            act.dma_start(histN[0:120, :, :], a["state_cv"][0].rearrange("(r b) w n -> (b w) r n", r=2)).then_inc(s["hist_loaded"], 16)
            for n in ("s_put", "pt_put", "v2_put", "k2_put", "ot_put", "g_exp"):
                act.sem_inc(s[n], START)
            me = Steps(act, s["act_step"])
            act.wait_ge(s["pool_set"], 1)
            me.then(act.activation(small[:, 31:32], epsr, ACT.Sqrt))
            for t in range(TT):
                act.wait_ge(s[f"x_loaded{t}"], 16)
                me.then(act.activation(junkA[0:tok(t), :], xA[0:tok(t), t, :], ACT.Square, accum_out=ss[0:tok(t), t:t + 1]))
                act.activation(rstd[0:tok(t), t:t + 1], ss[0:tok(t), t:t + 1], ACT.Sqrt, bias=epsr[0:tok(t)],
                               scale=1.0 / D).then_inc(s["x_summed"], 1)
            act.wait_ge(s["c_loaded"], 16)
            for hp in range(HP):
                act.wait_ge(s["zq_done"], 2 * hp + 1)
                for e in range(2):
                    ins = act.activation(qZ[64 * e:64 * e + 64, hp, e, 0:HALF], Z[0][64 * e:64 * e + 64, 0:HALF], ACT.Identity,
                                         bias=b_in[64 * e:64 * e + 64, hp:hp + 1])
                ins.then_inc(s["zq_putA"], 1)
            gs = glu[:, :, GX:GLUW].rearrange("p c (b x) -> p c b x", b=NB)
            for r in range(2):
                act.wait_ge(s["hist_done"], r + 1)
                for c in range(CT):
                    ins = act.activation(gs[:, c, 4 * r:4 * r + 4, 0:CW - 1],
                                         (OB, SM)[r][:, c * 120:(c + 1) * 120].rearrange("p (b w) -> p b w", b=4), ACT.Copy)
                ins.then_inc(s["hist_put"], 1)
            act.wait_ge(s["ks_done"], 1)
            for hp in range(HP):
                ins = act.activation(kTs[:, hp, :], TB[0][:, hp * TS:(hp + 1) * TS], ACT.Identity, bias=b_in[:, 4 + hp:5 + hp])
            ins.then_inc(s["ks_put"], 1)

            qS4 = qS.rearrange("p c (q g) -> p c g q", g=4)

            def spread_q(b):
                act.wait_ge(s["own_done"], b)
                act.nop()
                for g in range(4):
                    ins = act.activation(qS4[32 * g:32 * g + 32, :, g, :],
                                         qR[32 * g:32 * g + 32, :, bass.ds(b * NT, NT)], ACT.Copy)
                ins.then_inc(s["qs_ready"], 1)

            act.wait_ge(s["qr_ready"], 1)
            spread_q(0)

            def put_scores(b, js):
                if js[0] == 0:
                    act.wait_ge(s["p_turned"], b * 4 + START)
                for j in js:
                    act.wait_ge(s["scores_done"], b * 4 + (j + 1))
                    act.activation(S[:, :, j * 256:(j + 1) * 256], SC[j % 2][:, :].rearrange("p (g k) -> p g k", g=2),
                                   ACT.Copy).then_inc(s["s_put"], 1)

            def exps(b):
                for g in range(2):
                    act.wait_ge(s["nb_ready"], b * 2 + (g + 1))
                    act.activation(S[:, g, :], S[:, g, :], ACT.Exp, bias=nb[:, g:g + 1], scale=SCALE,
                                   accum_out=rs[:, g:g + 1]).then_inc(s["probs_ready"], 1)
                for g in range(2):
                    ins = act.activation(ownS[:, g, :], ownS[:, g, :], ACT.Exp, bias=nb[:, g:g + 1], scale=SCALE,
                                         accum_out=rs[:, 2 + g:3 + g])
                ins.then_inc(s["probs_ready"], 1)

            def put_turned(b):
                act.wait_ge(s["pv_done"], b * 8 + START)
                for n in range(4):
                    act.wait_ge(s["p_turned"], b * 4 + (n + 1) + START)
                    act.activation(pT[:, n // 2, 4 * (n % 2):4 * (n % 2) + 4, :],
                                   TB[n % 2][:, :].rearrange("p (u r) -> p u r", u=4), ACT.Copy).then_inc(s["pt_put"], 1)
                act.wait_ge(s["own_turned"], b + 1 + START)
                act.activation(pTo[0:TS, :, :], SM[0:TS, P:3 * P].rearrange("p (g r) -> p g r", g=2), ACT.Copy).then_inc(s["pto_put"], 1)

            def put_out(b):
                act.wait_ge(s["ot_done"], b + 1 + START)
                act.nop()
                act.activation(oT[:, bass.ds(b, 1), :].rearrange("p a r -> p (a r)"), TB[0][:, 0:P], ACT.Copy).then_inc(s["ot_put"], 1)

            def glu_exps(i):
                act.wait_ge(s["g_exp"], i * 2 + START)
                act.nop()
                act.activation(small[:, 31:32], nbg[:, bass.ds(i, 1)], ACT.Copy).then_inc(s["g_bias"], 1)
                act.wait_ge(s["g_bias"], i + 1)
                act.wait_ge(s["z1_put"], i * 2 + START)
                for half in range(2):
                    act.wait_ge(s["z1_done"], i * 4 + (half + 1) + START)
                    act.activation(sig[:, half * HALF:(half + 1) * HALF], Z[half][:, 0:HALF], ACT.Exp,
                                   bias=small[:, 31:32], scale=-1.0).then_inc(s["g_exp"], 1)

            def put_v(i):
                act.wait_ge(s["v2_done"], i + 1)
                act.wait_ge(s["nb_ready"], i * 2 + 10)
                act.nop()
                act.activation(vT[:, 0:TP_], Z[0][:, :], ACT.Identity, bias=b_in[:, bass.ds(i + 8, 1)]).then_inc(s["v2_put"], 1)

            def put_kv(i):
                act.wait_ge(s["k2_done"], i + 1 + START)
                act.nop()
                act.activation(kP[:, bass.ds(i, 1), :].rearrange("p a t -> p (a t)"), Z[1][:, :], ACT.Identity,
                               bias=b_in[:, bass.ds(i + 4, 1)]).then_inc(s["k2_put"], 1)
                act.wait_ge(s["v2_turned"], i + 1)
                act.nop()
                act.activation(vP[:, 0:4, bass.ds(i * P, P)], TB[0][:, :].rearrange("p (t r) -> p t r", t=4),
                               ACT.Copy).then_inc(s["v2_home"], 1)

            act.wait_ge(s["vs_done"], 1)
            put_scores(0, (0, 1))
            with act.Fori(0, 4) as i:
                put_scores(i, (2, 3))
                glu_exps(i)
                exps(i)
                put_turned(i)
                spread_q(i + 1)
                put_scores(i + 1, (0, 1))
                put_out(i)
            with act.Fori(0, 3) as i:
                put_scores(i + 4, (2, 3))
                exps(i + 4)
                put_v(i)
                put_kv(i)
                put_turned(i + 4)
                spread_q(i + 5)
                put_scores(i + 5, (0, 1))
                put_out(i + 4)
            put_scores(7, (2, 3))
            exps(7)
            put_v(3)
            put_kv(3)
            put_turned(7)
            put_out(7)
            act.wait_ge(s["z1_put"], 8 + START)
            act.wait_ge(s["own_done"], NB)
            act.activation(gluS.rearrange("p c (b t) -> p c b t", b=NB), gs[:, :, :, CW - 1:SX], ACT.Copy).then_inc(s["glus_put"], 1)
            nat = [TB[0], TB[1], SM, TB[0], TB[1]]
            act.wait_ge(s["pv_done"], SUPER * NB + START)
            act.wait_ge(s["scores_done"], 4 * NB)
            for t in range(TT):
                act.wait_ge(s["knat_done"], t + 1)
                act.activation(kNat[0:tok(t), t, :], nat[t][0:tok(t), :], ACT.Copy).then_inc(s["knat_put"], 1)
            for r in range(2):
                act.wait_ge(s["glun_done"], r + 1)
                n = (CW - 1, TS)[r]
                act.activation(cvN[0:n, r, :], (SM, OB)[r][0:n, :], ACT.Copy).then_inc(s["glun_put"], 1)
            act.wait_ge(s["knat_put"], TT)
            act.wait_ge(s["glun_put"], 2)
            act.wait_ge(s["v2_home"], 4)
            act.wait_ge(s["vs_put"], 1)
            rows = lambda n: a[n][0, 0].rearrange("(t p) h d -> p t (h d)", p=P)
            act.dma_start(rows("k_p"), kNat[:, 0:4, :]).then_inc(s["stored_kv"], 16)
            act.dma_start(rows("v_p"), vP[:, 0:4, :]).then_inc(s["stored_kv"], 16)
            act.dma_start(a["k_s"][0].rearrange("b t h d -> (b t) (h d)"), kNat[0:TS, 4, :]).then_inc(s["stored_kv"], 16)
            act.dma_start(a["v_s"][0].rearrange("b t h d -> (b t) (h d)"), vP[0:TS, 4, :]).then_inc(s["stored_kv"], 16)
            act.dma_start(a["cv_p"][0, 0], cvN[0:CW - 1, 0, :]).then_inc(s["stored_kv"], 16)
            act.dma_start(a["cv_s"][0][:, CW - 1 - NT:CW - 1, :], cvN[0:TS, 1, :]).then_inc(s["stored_kv"], 16)
            act.dma_start(a["cv_s"][0][:, 0:CW - 1 - NT, :], a["state_cv"][0][:, NT:CW - 1, :]).then_inc(s["stored_kv"], 16)
            sb_ = [Z[0], Z[1], SC[0], SC[1]]

            def p_exps(h):
                if h >= 2:
                    act.wait_ge(s["pt2_done"], 4 * (h - 1))
                for t in range(4):
                    act.wait_ge(s["pnb_ready"], 4 * h + t + 1)
                    n = (t + 1) * P
                    j = 4 * (h % 2) + t
                    act.activation(pP[:, h % 2, t, 0:n], sb_[t][:, 0:n], ACT.Exp, bias=pnb[:, j:j + 1], scale=SCALE,
                                   accum_out=prs[:, j:j + 1]).then_inc(s["pexp"], 1)

            def p_turned(h):
                if h >= 2:
                    act.wait_ge(s["pv2_done"], h - 1)
                for kb in range(4):
                    act.wait_ge(s["pt2_done"], 4 * h + kb + 1)
                    act.activation(pPT[:, h % 2, kb, kb * P:TP_], TB[kb % 2][:, kb * P:TP_], ACT.Copy).then_inc(s["ptt_put"], 1)

            p_exps(0)
            for h in range(H):
                if h + 1 < H:
                    p_exps(h + 1)
                p_turned(h)
                if h == H - 2:
                    act.wait_ge(s["ln_ready"], 1)
                    act.activation(sq, conv, ACT.Sigmoid).then_inc(s["sg_put"], 1)
                if h == ST1_AFTER:
                    for half in range(2):
                        act.wait_ge(s["st1_done"], half + 1)
                        act.activation(mu[:, half * HALF:(half + 1) * HALF], TB[half][:, 0:HALF], ACT.Copy,
                                       scale=1.0 / DA).then_inc(s["mu_put"], 1)
                if h == ST2_AFTER:
                    for half in range(2):
                        act.wait_ge(s["st2_done"], half + 1)
                        act.activation(sd[:, half * HALF:(half + 1) * HALF], TB[half][:, 0:HALF], ACT.Sqrt, bias=epsl,
                                       scale=1.0 / DA).then_inc(s["sd_put"], 1)
            for m in range(CT):
                for half in range(2):
                    n = 2 * m + half
                    act.wait_ge(s["pw_done"], n + 1)
                    act.activation(mixT[:, 4 + m, half * HALF:(half + 1) * HALF], sb_[n % 4][:, 0:HALF], ACT.Identity,
                                   bias=cst("b_pw")[:, m:m + 1]).then_inc(s["pw_put"], 1)
            def h2_upper(t):
                for j in range(2):
                    n = 2 * t + j
                    act.wait_ge(s["h2_raw"], n + 1)
                    raw = h2raw[:, n % 2, :].rearrange("p (k t) -> p k t", k=4)[:, :, 0:tok(t)]
                    act.activation(h2hi[:, 4 * j:4 * j + 4, t * P:t * P + tok(t)], raw, ACT.Copy).then_inc(s["h2_hi"], 1)

            wu_full = [s["wu_full0"], s["wu_full1"]]
            act.wait_ge(s["pv2_done"], H)
            for t in range(TT):
                m = tok(t)
                for nh in range(2):
                    act.wait_ge(s["mo_done"], 2 * t + nh + 1)
                    if 2 * t + nh:
                        act.wait_ge(s["mo_sq"], 2 * t + nh)
                    if t and nh == 0:
                        act.wait_ge(s["x1_sq"], t)
                    act.activation(junk[0:m, 0:TP_], sb_[2 * (t % 2) + nh][0:m, :], ACT.Square,
                                   accum_out=ss2[0:m, 2 * t + nh:2 * t + nh + 1]).then_inc(s["mo_sq"], 1)
                if t == 0:
                    act.wait_ge(wu_full[0], 32)
                    act.activation(wuhi[0][:, :, :], wu[0].rearrange("p k u n -> p k (u n)"), ACT.Copy).then_inc(s["wu_hi"], 1)
                act.wait_ge(s["mo_sum"], t + 1)
                act.activation(r2[0:m, t:t + 1], r2[0:m, t:t + 1], ACT.Sqrt, bias=epsr[0:m], scale=1.0 / D).then_inc(s["mo_rt"], 1)
                act.wait_ge(s["x1_ready"], t + 1)
                act.wait_ge(s["mo_sq"], 2 * t + 2)
                act.activation(junk[0:m, :], x1[0:m, t, :], ACT.Square, accum_out=ss3[0:m, t:t + 1]).then_inc(s["x1_sq"], 1)
                act.wait_ge(s["x1_sq"], t + 1)
                act.activation(r3[0:m, t:t + 1], ss3[0:m, t:t + 1], ACT.Sqrt, bias=epsr[0:m], scale=1.0 / D).then_inc(s["x1_rt"], 1)
                if t:
                    h2_upper(t - 1)
            h2_upper(TT - 1)
            act.wait_ge(s["h2_put"], 2 * TT)
            act.wait_ge(s["mo_done"], 2 * TT)
            act.wait_ge(s["t1_put"], 2 * TT)
            bank8 = [OB, SM, TB[0], TB[1]] + sb_
            act.sem_inc(s["ux_put"], 8)

            def up_step(i, slot, split_next=True):
                if split_next:
                    act.wait_ge(wu_full[1 - slot], i * 32 + 32 * (slot + 1))
                    act.wait_ge(s["up_done"], i * 8 + (4 * slot + START))
                    act.activation(wuhi[1 - slot][:, :, :], wu[1 - slot].rearrange("p k u n -> p k (u n)"),
                                   ACT.Copy).then_inc(s["wu_hi"], 1)
                act.wait_ge(s["cv_done"], i * 2 + (slot + 1))
                act.wait_ge(s["last_put"], i * 2 + (slot + 1))
                for half in range(2):
                    for u in range(2):
                        n = 2 * half + u
                        act.wait_ge(s["up_done"], i * 8 + (4 * slot + n + 1 + START))
                        bk = bank8[4 * slot + n]
                        if half == 0:
                            ins = act.activation(ux[:, slot, u, 2:2 + HALF], bk[:, 0:HALF], ACT.Copy)
                        else:
                            r = TP_ - HALF
                            act.activation(ux[:, slot, u, 2 + HALF:2 + TP_], bk[:, 0:r], ACT.Copy)
                            ins = act.activation(ux[:, slot, u, 2 + TP_:UXW].rearrange("p (b x) -> p b x", b=NB)[:, :, 2:UXS],
                                                 bk[:, r:HALF].rearrange("p (b t) -> p b t", b=NB), ACT.Copy)
                        ins.then_inc(s["ux_put"], 1)
                act.wait_ge(s["g_conv"], i * 2 + (slot + 1))
                act.activation(sg2[:, slot, :], cvo[:, slot, 0, :], ACT.Sigmoid).then_inc(s["g_sig"], 1)

            with act.Fori(0, FT_N // 2 - 1) as i:
                for slot in range(2):
                    up_step(i, slot)
            up_step(FT_N // 2 - 1, 0)
            up_step(FT_N // 2 - 1, 1, split_next=False)
            wd_full = [s["wd_full0"], s["wd_full1"]]
            act.wait_ge(s["up_done"], 4 * FT_N + START)
            def split_pair(nh, kk, slot):
                c = 11 * nh
                act.wait_ge(wd_full[slot], kk * 8 + 8 * (c + 2 - slot))
                if nh and isinstance(kk, int) and kk < 2:
                    act.wait_ge(s[("dn_done", "y_done")[kk]], (10, TT)[kk])
                elif not isinstance(kk, int) or kk >= 2:
                    act.wait_ge(s["dn_done"], kk + (10 * nh - 1))
                    act.nop()
                if nh == 0 and isinstance(kk, int):
                    act.wait_ge(s["ft_ready"], 2 * kk + 2)
                elif nh == 0:
                    act.wait_ge(s["ft_ready"], FT_N)
                    act.nop()
                act.activation(fThi[:, slot, :, :], fT[:, bass.ds(kk * 2, 2), :], ACT.Copy).then_inc(s["ft_hi"], 1)
                act.activation(wdhi[:, slot, :, :], wd[:, slot, :, :], ACT.Copy).then_inc(s["wd_hi"], 1)

            y_banks = [[Z[0], Z[1], SC[0], SC[1], TB[0]], [TB[1], OB, SM, Z[0], Z[1]]]

            def y_square(nh, t):
                m = tok(t)
                act.wait_ge(s["y_done"], 5 * nh + t + 1)
                if 5 * nh + t:
                    act.wait_ge(s["y_sq"], 5 * nh + t)
                act.activation(junkY[0:m, :], y_banks[nh][t][0:m, :], ACT.Square,
                               accum_out=ss2[0:m, 2 * t + nh:2 * t + nh + 1]).then_inc(s["y_sq"], 1)

            for nh in range(2):
                split_pair(nh, 0, nh)
                if nh:
                    for t in range(TT):
                        y_square(0, t)
                split_pair(nh, 1, 1 - nh)
                with act.Fori(0, 4) as i:
                    for j in range(2):
                        split_pair(nh, i * 2 + (2 + j), (nh + j) % 2)
                split_pair(nh, 10, nh)

            def scale_left(t):
                m = tok(t)
                act.wait_ge(s["y_inv"], t + 1)
                act.activation(yo[0:m, t, 0:TP_], y0[0:m, t, :], ACT.Copy, scale=r2[0:m, t:t + 1]).then_inc(s["yo_left"], 1)

            for t in range(TT):
                m = tok(t)
                y_square(1, t)
                act.wait_ge(s["y_sum"], t + 1)
                act.activation(r2[0:m, t:t + 1], r2[0:m, t:t + 1], ACT.Sqrt, bias=epsr[0:m], scale=1.0 / D).then_inc(s["y_rt"], 1)
                if t:
                    scale_left(t - 1)
            scale_left(TT - 1)

        @block.vector
        def _(dve):
            for n in ("z1_put", "o_norm"):
                dve.sem_inc(s[n], START)
            me = Steps(dve, s["dve_step"])
            for t in range(TT):
                dve.wait_ge(s["x_summed"], t + 1)
                me.then(dve.reciprocal(rstd[0:tok(t), t:t + 1], rstd[0:tok(t), t:t + 1]))
                dve.tensor_scalar(xA[0:tok(t), t, :], xA[0:tok(t), t, :], rstd[0:tok(t), t:t + 1], None, ALU.mult).then_inc(s["x_scaled"], 1)
            dve.wait_ge(s["c_loaded"], 16)
            dve.tensor_scalar(nbg, b_in[:, 16:20], -1.0, None, ALU.mult)
            turn = [TB[0], TB[1], SC[0], SC[1]]
            gpre = cst("g_pre")
            for t in range(TT):
                for j in range(2):
                    n = 2 * t + j
                    dve.wait_ge(s["xt_done"], n + 1)
                    m = tok(t)
                    dve.tensor_tensor(hT[:, 4 * j:4 * j + 4, t * P:t * P + m],
                                      turn[n % 4][:, :].rearrange("p (k t) -> p k t", k=4)[:, :, 0:m],
                                      gpre[:, 4 * j:4 * j + 4].unsqueeze(2).to_broadcast([P, 4, m]), ALU.mult).then_inc(s["ht_ready"], 1)
            def turn_k(b, u, first=False):
                dve.wait_ge(kn_full[u % 4], b * 128 + 64 * (u // 4 + 1))
                if u % 2 == 0 and not first:
                    dve.wait_ge(s["scores_done"], b * 4 + max(u // 2 - 1, 0))
                dve.transpose(kT[:, u % 4, :, :].rearrange("p c (i k) -> p i c k", i=4),
                              kN[:, u % 4, :, :].rearrange("p i (c k) -> p i c k", k=32)).then_inc(s["kt_ready"], 1)

            dve.wait_ge(s["pool_set"], 1)
            for hp in range(HP):
                dve.wait_ge(s["zq_done"], 2 * hp + 2)
                for e in range(2):
                    dve.tensor_scalar(qZ[64 * e:64 * e + 64, hp, e, HALF:TP_], Z[1][64 * e:64 * e + 64, 0:TP_ - HALF],
                                      b_in[64 * e:64 * e + 64, hp:hp + 1], None, ALU.add)
                dve.tensor_scalar(qTs[:, hp, :], Z[1][:, TP_ - HALF:HALF], b_in[:, hp:hp + 1], None,
                                  ALU.add).then_inc(s["zq_putV"], 1)
                turn_k(0, hp, True)
            dve.wait_ge(s["zq_putV"], HP)
            qR5 = qR.rearrange("p (h x) t -> p h x t", x=4)
            for g in range(4):
                for x in range(4):
                    ins = dve.tensor_copy(qR5[32 * g:32 * g + 32, :, x, :], qTs[32 * x:32 * x + 32, :, :])
            ins.then_inc(s["qr_ready"], 1)
            dve.wait_ge(s["ks_put"], 1)
            kO5 = kOwn.rearrange("p (h x) t -> p h x t", x=4)
            for x in range(4):
                ins = dve.tensor_copy(kO5[0:32, :, x, :], kTs[32 * x:32 * x + 32, :, :])
            ins.then_inc(s["kown_put"], 1)
            dve.wait_ge(s["vs_done"], 1)
            dve.wait_ge(s["bv_loaded"], 16)
            dve.tensor_tensor(vP[0:TS, 4, :], TB[1][0:TS, :], bvB[0:TS, :], ALU.add).then_inc(s["vs_put"], 1)

            SOFT = 18

            def softmax(b):
                me = Steps(dve, s["soft_step"], b * SOFT)
                S4 = S.rearrange("p g (n k) -> p (g n) k", k=64)
                for j in range(4):
                    dve.wait_ge(s["s_put"], b * 4 + (j + 1) + START)
                    part = S[:, :, j * 256:(j + 1) * 256].rearrange("p g (n k) -> p g n k", k=64)
                    dve.tensor_reduce(bmax.rearrange("p (g n) -> p g n", g=2)[:, :, 4 * j:4 * j + 4], part, AX.X, ALU.max)
                    ins = dve.tensor_reduce(bsum.rearrange("p (g n) -> p g n", g=2)[:, :, 4 * j:4 * j + 4], part, AX.X, ALU.add)
                me.then(ins)

                def over_quads(src, dst, op):
                    me.then(dve.transpose(tA, src))
                    me.then(dve.tensor_reduce(tB[:, 0:8], tA.rearrange("p (q g) -> p q g", g=4), AX.X, op))
                    me.then(dve.tensor_copy(tC.rearrange("p (q g) -> p q g", g=4), tB[:, 0:8].unsqueeze(2).to_broadcast([P, 8, 4])))
                    me.then(dve.transpose(dst, tC))

                over_quads(bsum, bsum, ALU.add)
                t3 = bsum.rearrange("p (g n) -> p g n", g=2)
                for g in range(2):
                    ins = dve.tensor_tensor(rankv[:, g], t3[:, g].unsqueeze(1).to_broadcast([P, BLK, BLK]),
                                            t3[:, g].unsqueeze(2).to_broadcast([P, BLK, BLK]), ALU.subtract)
                me.then(ins)
                for g in range(2):
                    ins = dve.tensor_tensor(rankv[:, g], rankv[:, g], order, ALU.is_ge)
                me.then(ins)
                me.then(dve.tensor_reduce(pen, rank.rearrange("p (n m) -> p n m", m=BLK), AX.X, ALU.add))
                me.then(dve.tensor_scalar(pen, pen, float(TOPK), -BIG, ALU.is_ge, ALU.mult))
                me.then(dve.tensor_tensor(bmax, bmax, pen, ALU.add))
                me.then(dve.tensor_reduce(mx2[:, 0:2], bmax.rearrange("p (g n) -> p g n", g=2), AX.X, ALU.max))
                dve.wait_ge(s["own_done"], b + 1)
                dve.wait_ge(s["own_turned"], b + START)
                me.then(dve.tensor_tensor(ownS, own_ps, ownmask[:, bass.ds(b * -NT + (TS - NT), TS)].unsqueeze(1).to_broadcast([P, 2, TS]), ALU.add))
                me.then(dve.tensor_reduce(mx2[:, 2:4], ownS, AX.X, ALU.max))
                me.then(dve.tensor_tensor(mcol[:, 0:2], mx2[:, 0:2], mx2[:, 2:4], ALU.max))
                over_quads(mcol, bsum, ALU.max)
                dve.tensor_scalar(nb, bsum[:, 0:2], -SCALE, None, ALU.mult)
                for g in range(2):
                    dve.tensor_tensor(S4[:, BLK * g:BLK * g + BLK], S4[:, BLK * g:BLK * g + BLK],
                                      pen[:, BLK * g:BLK * g + BLK].unsqueeze(2).to_broadcast([P, BLK, 64]),
                                      ALU.add).then_inc(s["nb_ready"], 1)
                assert me.n == SOFT, me.n

            def row_sums(b):
                dve.wait_ge(s["probs_ready"], b * 3 + 3)
                dve.wait_ge(s["den_done"], b + START)
                dve.tensor_tensor(rsum, rs[:, 0:2], rs[:, 2:4], ALU.add).then_inc(s["rsum_ready"], 1)

            def norm_out(b):
                dve.wait_ge(s["pv_done"], b * 8 + 8 + START)
                dve.reciprocal(rden, den_ps).then_inc(s["den_inv"], 1)
                dve.wait_ge(s["den_inv"], b + 1)
                dve.wait_ge(s["ot_done"], b + START)
                dve.tensor_scalar(oN[:, :], OB[:, 0:P], rden, None, ALU.mult).then_inc(s["o_norm"], 1)

            def glu_values(i):
                dve.wait_ge(s["g_exp"], i * 2 + 2 + START)
                dve.tensor_scalar(sig, sig, 1.0, None, ALU.add).then_inc(s["sig_ready"], 1)
                dve.wait_ge(s["sig_ready"], i * 2 + 1)
                dve.reciprocal(sig, sig).then_inc(s["sig_ready"], 1)
                dve.wait_ge(s["sig_ready"], i * 2 + 2)
                gi = glu[:, bass.ds(i, 1), :].rearrange("p a x -> p (a x)")
                ba = b_in[:, bass.ds(i + 12, 1)]
                dve.wait_ge(s["z1_done"], i * 4 + 3 + START)
                dve.scalar_tensor_tensor(gi[:, CW - 1:CW - 1 + HALF], Z[0][:, 0:HALF], ba, sig[:, 0:HALF],
                                         ALU.add, ALU.mult).then_inc(s["z1_put"], 1)
                dve.wait_ge(s["z1_done"], i * 4 + 4 + START)
                r = TP_ - HALF
                dve.scalar_tensor_tensor(gi[:, CW - 1 + HALF:GX], Z[1][:, 0:r], ba, sig[:, HALF:TP_], ALU.add, ALU.mult)
                dve.scalar_tensor_tensor(gi[:, GX:GLUW].rearrange("p (b x) -> p b x", b=NB)[:, :, CW - 1:SX],
                                         Z[1][:, r:HALF].rearrange("p (b t) -> p b t", b=NB), ba,
                                         sig[:, TP_:TOK].rearrange("p (b t) -> p b t", b=NB),
                                         ALU.add, ALU.mult).then_inc(s["z1_put"], 1)

            def step(b, last=False, between=None):
                softmax(b)
                if not last:
                    turn_k(b + 1, 0)
                    turn_k(b + 1, 1)
                row_sums(b)
                if not last:
                    turn_k(b + 1, 2)
                    turn_k(b + 1, 3)
                if between:
                    between()
                if not last:
                    for u in range(4, 8):
                        turn_k(b + 1, u)
                norm_out(b)

            prompt_in, sample_in = glu[:, CT - 1, 0:GX], glu[:, CT - 1, GX:GLUW].rearrange("p (b x) -> p b x", b=NB)
            prompt_out, sample_out = conv[:, CT - 1, 0:TP_], conv[:, CT - 1, TP_:TOK].rearrange("p (b t) -> p b t", b=NB)

            def taps(i):
                for n in range(TAPS):
                    j = i * TAPS + (n + 1)
                    w = w_cv[:, CT - 1, bass.ds(j, 1)]
                    dve.wait_ge(s["tail_conv"], j)
                    dve.scalar_tensor_tensor(prompt_out, prompt_in[:, bass.ds(j, TP_)], w, prompt_out, ALU.mult, ALU.add)
                    dve.scalar_tensor_tensor(sample_out, sample_in[:, :, bass.ds(j, NT)], w, sample_out, ALU.mult, ALU.add).then_inc(s["tail_conv"], 1)

            for u in range(4, 8):
                turn_k(0, u)
            with dve.Fori(0, 4) as i:
                step(i, between=lambda: glu_values(i))
            dve.wait_ge(s["z1_put"], 2 * CT + START)
            dve.wait_ge(s["hist_put"], 2)
            w0, b0 = w_cv[:, CT - 1, 0:1], w_cv[:, CT - 1, CW:CW + 1]
            dve.tensor_scalar(prompt_out, prompt_in[:, 0:TP_], w0, b0, ALU.mult, ALU.add)
            dve.tensor_scalar(sample_out, sample_in[:, :, 0:NT], w0, b0, ALU.mult, ALU.add).then_inc(s["tail_conv"], 1)
            with dve.Fori(0, 3) as i:
                step(i + 4, between=lambda: taps(i))
            step(7, last=True)
            dve.wait_ge(s["ot_put"], NB + START)
            dve.wait_ge(s["k2_done"], 4 + START)
            for e in range(2):
                for x in range(2):
                    row = slice(64 * e, 64 * e + 64)
                    src = oT[row].rearrange("p b (g x h q) -> p g b x h q", g=2, x=2, h=4)[:, :, :, x, 2 * x + e, :]
                    dst = mixT[row, 0:HP, TP_:TOK].rearrange("p (g x) (b q) -> p g x b q", x=2, b=NB)[:, :, x]
                    ins = dve.tensor_copy(dst, src)
            ins.then_inc(s["mix_put"], 1)
            sb_ = [Z[0], Z[1], SC[0], SC[1]]
            dve.wait_ge(s["k2_put"], 4 + START)
            dve.tensor_copy(ident16, ident)
            dve.tensor_copy(causal16, causal).then_inc(s["mask_put"], 1)
            me = Steps(dve, s["pst_step"])

            def p_stats(h):
                j = 4 * (h % 2)
                for t in range(4):
                    dve.wait_ge(s["ps_done"], 4 * h + t + 1)
                    me.then(dve.tensor_reduce(pm[:, j + t:j + t + 1], sb_[t][:, 0:(t + 1) * P], AX.X, ALU.max))
                    dve.tensor_scalar(pnb[:, j + t:j + t + 1], pm[:, j + t:j + t + 1], -SCALE, None, ALU.mult).then_inc(s["pnb_ready"], 1)

            def p_norms(h):
                j = 4 * (h % 2)
                dve.wait_ge(s["pexp"], 4 * h + 4)
                me.then(dve.reciprocal(prr[:, j:j + 4], prs[:, j:j + 4]))
                for t in range(4):
                    n = (t + 1) * P
                    dve.tensor_scalar(pP[:, h % 2, t, 0:n], pP[:, h % 2, t, 0:n], prr[:, j + t:j + t + 1], None,
                                      ALU.mult).then_inc(s["pnorm"], 1)

            def p_out(hp):
                dve.wait_ge(s["pv2_done"], 2 * hp + 2)
                dve.tensor_copy(mixT[:, hp, 0:TP_], (OB, SM)[hp % 2][:, :]).then_inc(s["o2_put"], 1)

            p_stats(0)
            for h in range(H):
                p_norms(h)
                if h + 1 < H:
                    p_stats(h + 1)
                if h % 2 == 0 and h:
                    p_out(h // 2 - 1)
                if h == ST2_AFTER + 1:
                    dve.wait_ge(s["sd_put"], 2)
                    dve.reciprocal(sd, sd).then_inc(s["sd_inv"], 1)
            p_out(HP - 1)
            for r in range(2):
                dve.wait_ge(s["hf_done"], r + 1)
                if r == 0:
                    dve.wait_ge(s["ln_ready"], 1)
                    dve.wait_ge(s["sg_put"], 1)
                    dve.tensor_tensor(conv, conv, sq, ALU.mult).then_inc(s["c_ready"], 1)
                    dve.wait_ge(s["pw_done"], 2 * CT)
                dve.tensor_copy(histT[:, r, :, :], TB[r][:, 0:FT_N * 16].rearrange("p (f x) -> p f x", x=16)).then_inc(s["hf_put"], 1)
            dve.wait_ge(s["gpost_loaded"], 16)
            dve.wait_ge(s["xr_loaded"], 32)
            me2 = Steps(dve, s["mo_step"])
            turn2 = [TB[0], TB[1], OB, SM]
            gffn = cst("g_ffn")

            def put_h2(t):
                m = tok(t)
                for j in range(2):
                    n = 2 * t + j
                    dve.wait_ge(s["h2_done"], n + 1)
                    if n >= 2:
                        dve.wait_ge(s["h2_put"], n - 1)
                    dve.tensor_tensor(h2raw[:, n % 2, :].rearrange("p (k t) -> p k t", k=4)[:, :, 0:m],
                                      turn2[n % 4][:, :].rearrange("p (k t) -> p k t", k=4)[:, :, 0:m],
                                      gffn[:, 4 * j:4 * j + 4].unsqueeze(2).to_broadcast([P, 4, m]), ALU.mult).then_inc(s["h2_raw"], 1)

            for t in range(TT):
                m = tok(t)
                dve.wait_ge(s["mo_sq"], 2 * t + 2)
                dve.tensor_tensor(r2[0:m, t:t + 1], ss2[0:m, 2 * t:2 * t + 1], ss2[0:m, 2 * t + 1:2 * t + 2], ALU.add).then_inc(s["mo_sum"], 1)
                dve.wait_ge(s["mo_rt"], t + 1)
                me2.then(dve.reciprocal(r2[0:m, t:t + 1], r2[0:m, t:t + 1]))
                if t >= 2:
                    dve.wait_ge(s["h2_done"], 2 * (t - 2) + 2)
                for nh in range(2):
                    cols = slice(nh * TP_, (nh + 1) * TP_)
                    dve.scalar_tensor_tensor(t1[0:m, t % 2, cols], sb_[2 * (t % 2) + nh][0:m, :], r2[0:m, t:t + 1],
                                             gPost[0:m, cols], ALU.mult, ALU.mult).then_inc(s["t1_put"], 1)
                dve.wait_ge(s["t1_put"], 2 * t + 2)
                dve.tensor_tensor(x1[0:m, t, :], x1[0:m, t, :], t1[0:m, t % 2, :], ALU.add).then_inc(s["x1_ready"], 1)
                dve.wait_ge(s["x1_ready"], t + 1)
                if t:
                    put_h2(t - 1)
                dve.wait_ge(s["x1_rt"], t + 1)
                me2.then(dve.reciprocal(r3[0:m, t:t + 1], r3[0:m, t:t + 1]))
                dve.tensor_scalar(t1[0:m, t % 2, :], x1[0:m, t, :], r3[0:m, t:t + 1], None, ALU.mult).then_inc(s["h2_ready"], 1)
            put_h2(TT - 1)
            dve.sem_inc(s["cv_done"], 2)
            def rest_pair(nh, kk, slot):
                dve.wait_ge(s["ft_hi"], kk + (11 * nh + 1))
                dve.tensor_tensor(fTlo[:, slot, :, :], fT[:, bass.ds(kk * 2, 2), :], fThi[:, slot, :, :].bitcast(F32),
                                  ALU.subtract).then_inc(s["ft_lo"], 1)

            def up_step(i, slot, last=False):
                me3 = Steps(dve, s["f_step"], i * 10 + 5 * slot)
                dve.wait_ge(s["taps_put"], i * 2 + (slot + 1))
                for u in range(2):
                    dve.wait_ge(s["ux_put"], i * 8 + (8 + 4 * slot + 3 + u))
                    src, dst = ux[:, slot, u, :], cvo[:, slot, u, :]
                    ps_in = src[:, 2 + TP_:UXW].rearrange("p (b x) -> p b x", b=NB)
                    ps_out = dst[:, TP_:TOK].rearrange("p (b t) -> p b t", b=NB)
                    w = wdw[:, slot, u, :]
                    dve.tensor_scalar(dst[:, 0:TP_], src[:, 0:TP_], w[:, 0:1], w[:, 3:4], ALU.mult, ALU.add)
                    me3.then(dve.tensor_scalar(ps_out, ps_in[:, :, 0:NT], w[:, 0:1], w[:, 3:4], ALU.mult, ALU.add))
                    for j in (1, 2):
                        dve.scalar_tensor_tensor(dst[:, 0:TP_], src[:, j:j + TP_], w[:, j:j + 1], dst[:, 0:TP_], ALU.mult, ALU.add)
                        ins = dve.scalar_tensor_tensor(ps_out, ps_in[:, :, j:j + NT], w[:, j:j + 1], ps_out, ALU.mult, ALU.add)
                        if j == 2:
                            ins.then_inc(s[("g_conv", "cv_done")[u]], 1)
                        else:
                            me3.then(ins)
                if last:
                    rest_pair(0, 0, 0)
                dve.wait_ge(s["g_sig"], i * 2 + (slot + 1))
                me3.then(dve.tensor_tensor(cvo[:, slot, 0, :], cvo[:, slot, 0, :], sg2[:, slot, :], ALU.mult))
                dve.wait_ge(s["cv_done"], i * 2 + (slot + 3))
                dve.tensor_tensor(fT[:, bass.ds(i * 2 + slot, 1), :].rearrange("p a t -> p (a t)"), cvo[:, slot, 0, :],
                                  cvo[:, slot, 1, :], ALU.mult).then_inc(s["ft_ready"], 1)
                assert me3.n == 5, me3.n
            with dve.Fori(0, FT_N // 2 - 1) as i:
                for slot in range(2):
                    up_step(i, slot)
            up_step(FT_N // 2 - 1, 0)
            up_step(FT_N // 2 - 1, 1, last=True)
            y_banks = [[Z[0], Z[1], SC[0], SC[1], TB[0]], [TB[1], OB, SM, Z[0], Z[1]]]
            dve.wait_ge(s["gffn_loaded"], 16)
            for nh in range(2):
                if nh:
                    rest_pair(nh, 0, nh)
                    for t in range(TT):
                        m = tok(t)
                        dve.wait_ge(s["y_sq"], t + 1)
                        dve.tensor_tensor(y0[0:m, t, :], y_banks[0][t][0:m, :], gFfn[0:m, 0:TP_], ALU.mult).then_inc(s["y0_put"], 1)
                rest_pair(nh, 1, 1 - nh)
                if nh == 0:
                    for n in range(11):
                        dve.wait_ge(s["ul_done"], n + 1)
                        dve.tensor_copy(histF[0:18, n * TP_:(n + 1) * TP_], (TB[1], OB, SM)[n % 3][0:18, :]).then_inc(s["ul_put"], 1)
                with dve.Fori(0, 4) as i:
                    for j in range(2):
                        rest_pair(nh, i * 2 + (2 + j), (nh + j) % 2)
                rest_pair(nh, 10, nh)
            me4 = Steps(dve, s["y_step"])

            def right_half(t):
                m = tok(t)
                cols = slice(TP_, D)
                me4.then(dve.tensor_tensor(yo[0:m, t, cols], y_banks[1][t][0:m, :], gFfn[0:m, cols], ALU.mult))
                dve.wait_ge(s["y_rt"], t + 1)
                dve.reciprocal(r2[0:m, t:t + 1], r2[0:m, t:t + 1]).then_inc(s["y_inv"], 1)
                dve.wait_ge(s["y_inv"], t + 1)
                dve.scalar_tensor_tensor(yo[0:m, t, cols], yo[0:m, t, cols], r2[0:m, t:t + 1], x1[0:m, t, cols],
                                         ALU.mult, ALU.add).then_inc(s["yo_ready1"], 1)

            for t in range(TT):
                m = tok(t)
                dve.wait_ge(s["y_sq"], TT + t + 1)
                dve.tensor_tensor(r2[0:m, t:t + 1], ss2[0:m, 2 * t:2 * t + 1], ss2[0:m, 2 * t + 1:2 * t + 2], ALU.add).then_inc(s["y_sum"], 1)
                right_half(t)

        @block.gpsimd
        def _(pool):
            pool.memset(A[:, 0:4096], 0.0)
            pool.memset(vP[:, 4, :], 0.0)
            pool.memset(glu[:, :, 0:CW - 1], 0.0)
            pool.memset(qS, 0.0)
            pool.memset(kOwn, 0.0)
            pool.memset(small[:, :], 0.0).then_inc(s["pool_step"], 1)
            pool.memset(pTo_[:, :], 0.0)
            pool.wait_ge(s["pool_step"], 1)
            pool.memset(ss, 1.0)
            pool.memset(epsr, 1e-6)
            pool.memset(epsl, 1e-5)
            pool.memset(ones[:, :], 1.0).then_inc(s["pool_set"], 1)
            me = Steps(pool, s["conv_step"])
            pool.wait_ge(s["c_loaded"], 16)
            pool.wait_ge(s["hist_put"], 2)
            for i in range(CT - 1):
                last_tile = i == CT - 2
                pool.wait_ge(s["z1_put"], (2 * CT if last_tile else 2 * i + 2) + START)
                prod = sig if last_tile else conv[:, i + 1, :]
                gx = glu[:, i, GX:GLUW].rearrange("p (b x) -> p b x", b=NB)
                for j in range(CW):
                    w = w_cv[:, i, j:j + 1]
                    dst = prod if j else conv[:, i, :]
                    ds = dst[:, TP_:TOK].rearrange("p (b t) -> p b t", b=NB)
                    bias = [ALU.mult] if j else [ALU.mult, ALU.add]
                    b2 = None if j else w_cv[:, i, CW:CW + 1]
                    pool.tensor_scalar(dst[:, 0:TP_], glu[:, i, j:j + TP_], w, b2, *bias)
                    me.then(pool.tensor_scalar(ds, gx[:, :, j:j + NT], w, b2, *bias))
                    if j:
                        ins = pool.tensor_tensor(conv[:, i, :], conv[:, i, :], prod, ALU.add)
                        if j < CW - 1:
                            me.then(ins)
                ins.then_inc(s["conv_done"], 1)
                pool.wait_ge(s["conv_done"], i + 1)
            pool.wait_ge(s["conv_done"], CT - 1)
            pool.wait_ge(s["mu_put"], 2)
            me.then(pool.tensor_tensor(conv, conv, mu.unsqueeze(1).to_broadcast([P, CT, TOK]), ALU.subtract))
            pool.tensor_tensor(sq, conv, conv, ALU.mult).then_inc(s["sq_ready"], 1)
            pool.wait_ge(s["sd_inv"], 1)
            me.then(pool.tensor_tensor(conv, conv, sd.unsqueeze(1).to_broadcast([P, CT, TOK]), ALU.mult))
            for c in range(CT):
                ins = pool.tensor_scalar(conv[:, c, :], conv[:, c, :], cst("g_ln")[:, c:c + 1], cst("b_ln")[:, c:c + 1], ALU.mult, ALU.add)
            ins.then_inc(s["ln_ready"], 1)
            def rest_up(n, slot):
                pool.wait_ge(s["wu_hi"], n + 1)
                pool.tensor_tensor(wulo[:, slot, :, :], wu[slot].rearrange("p k u n -> p k (u n)"), wuhi[slot][:, :, :].bitcast(F32),
                                   ALU.subtract).then_inc(s["wu_lo"], 1)

            rest_up(0, 0)
            for n in range(2 * TT):
                t, j = n // 2, n % 2
                m = tok(t)
                raw = h2raw[:, n % 2, :].rearrange("p (k t) -> p k t", k=4)[:, :, 0:m]
                hi = h2hi[:, 4 * j:4 * j + 4, t * P:t * P + m]
                pool.wait_ge(s["h2_hi"], n + 1)
                pool.tensor_tensor(h2lo[:, 4 * j:4 * j + 4, t * P:t * P + m], raw, hi.bitcast(F32), ALU.subtract).then_inc(s["h2_put"], 1)
            pool.wait_ge(s["mo_done"], 2 * TT)
            pool.wait_ge(s["hf_put"], 2)
            pool.memset(ux[:, :, :, 0:2], 0.0)
            pool.sem_inc(s["last_put"], 2)

            def up_step(i, slot, split_next=True):
                f = i * 2 + slot
                uh = ux[:, slot, :, 2 + TP_:UXW].rearrange("p u (b x) -> p u b x", b=NB)
                pool.wait_ge(s["cv_done"], f + 1)
                for u in range(2):
                    pool.tensor_copy(wdw[:, slot, u, :], dwv[:, u, bass.ds(f, 1), :].rearrange("p a j -> p (a j)"))
                    ins = pool.tensor_copy(uh[:, u, :, 0:2], histT[:, u, bass.ds(f, 1), :].rearrange("p a (b w) -> p (a b) w", w=2))
                ins.then_inc(s["taps_put"], 1)
                if split_next:
                    rest_up(f + 1, 1 - slot)
                pool.wait_ge(s["ux_put"], f * 4 + (8 + 4))
                for u in range(2):
                    lu = last[:, u, bass.ds(f, 1), :].rearrange("p a x -> p (a x)")
                    pool.tensor_copy(lu[:, 0:2], ux[:, slot, u, TP_:TP_ + 2])
                    ins = pool.tensor_copy(lu[:, 2:18].rearrange("p (b w) -> p b w", w=2), uh[:, u, :, UXS - 2:UXS])
                ins.then_inc(s["last_put"], 1)

            with pool.Fori(0, FT_N // 2 - 1) as i:
                for slot in range(2):
                    up_step(i, slot)
            up_step(FT_N // 2 - 1, 0)
            up_step(FT_N // 2 - 1, 1, split_next=False)
            with pool.Fori(0, FT_N // 2) as i:
                for slot in range(2):
                    pool.wait_ge(s["wd_hi"], i * 2 + (slot + 1))
                    pool.tensor_tensor(wdlo[:, slot, :, :], wd[:, slot, :, :], wdhi[:, slot, :, :].bitcast(F32), ALU.subtract).then_inc(s["wd_lo"], 1)
            for t in range(TT):
                m = tok(t)
                pool.wait_ge(s["yo_left"], t + 1)
                pool.tensor_tensor(yo[0:m, t, 0:TP_], yo[0:m, t, 0:TP_], x1[0:m, t, 0:TP_], ALU.add).then_inc(s["yo_ready0"], 1)


def _tables():
    import numpy as np

    r = np.arange(P)
    ident = np.eye(P, dtype=np.float32)
    causal = np.where(r[None, :] <= r[:, None], 0.0, -BIG).astype(np.float32)
    h4, q, i = r // 32, (r // 4) % 8, r % 4
    key = np.arange(2 * TS) - (TS - NT)
    own = np.where((i[:, None] == 0) & (key[None] >= 0) & (key[None] <= q[:, None]), 0.0, -BIG)
    n = np.arange(BLK)
    order = np.where(n[None, :] < n[:, None], 0.0, np.finfo(np.float32).tiny).astype(np.float32)
    denmap = np.zeros((P, 2, P), np.float32)
    hp, h4o, qo = r // 32, (r // 8) % 4, r % 8
    for g in range(2):
        denmap[:, g] = (h4[:, None] == h4o[None]) & (q[:, None] == qo[None]) & (hp[None] // 2 == g)
    flat = [ident, causal, own, np.broadcast_to(order.reshape(1, -1), (P, BLK * BLK)),
            denmap.reshape(P, -1)]
    return [np.ascontiguousarray(x, np.float32) for x in flat]


def _columns(v):
    import numpy as np

    return np.ascontiguousarray(np.asarray(v).reshape(-1, P).T)


_OUTS = [((1, TP_, D), "float32"), ((NB, NT, D), "float32"), ((1, 1, TP_, H, DH), "float32"),
         ((1, 1, TP_, H, DH), "float32"), ((1, 1, CW - 1, DA), "float32"), ((1, 1, 2, 2 * DFF), "float32"),
         ((1, NB, NT, H, DH), "float32"), ((1, NB, NT, H, DH), "float32"), ((1, NB, CW - 1, DA), "float32"),
         ((1, NB, 2, 2 * DFF), "float32")]
OUT_NAMES = ["y_p", "y_s", "k_p", "v_p", "cv_p", "ffn_p", "k_s", "v_s", "cv_s", "ffn_s"]
PLAIN = ["x_prompt", "x_sample", "cache_k", "cache_v", "page_table", "state_cv", "state_ffn", "w_in", "w_cv_pw",
         "w_out", "g_post_mix", "w_up", "w_down", "g_post_ffn"]


def lay_out(inputs):
    import numpy as np

    arrays = {n: np.ascontiguousarray(inputs[n]) for n in PLAIN}
    arrays["b_in_v"] = np.ascontiguousarray(np.asarray(inputs["b_in"])[0, 2 * DA:3 * DA])
    cvw = np.concatenate([np.asarray(inputs["w_cv_dw"])[0], np.asarray(inputs["b_cv_dw"])], 0)
    cvw = cvw.reshape(CW + 1, CT, P).transpose(2, 1, 0).reshape(P, -1)
    taps = np.concatenate([np.asarray(inputs["w_ffn_dw"])[0], np.asarray(inputs["b_ffn_dw"])], 0)
    dw = taps.reshape(4, 44, P).transpose(2, 1, 0).reshape(P, -1)
    vec = [_columns(inputs["b_in"]), cvw] + [_columns(inputs[n]) for n in
           ("g_cv_ln", "b_cv_ln", "b_cv_pw", "g_pre_mix", "g_pre_ffn")] + [dw]
    arrays["consts"] = np.ascontiguousarray(np.concatenate(_tables() + vec, 1))
    return arrays


def kernel(**inputs):
    import numpy as np
    import concourse.bacc as bacc
    from concourse.bass_utils import run_bass_kernel_spmd

    nc = bacc.Bacc("TRN2", target_bir_lowering=False, num_devices=1, dynamic_dma_scratch_size=1024)
    arrays = {"in_" + n: x for n, x in lay_out(inputs).items()}
    a = {n[3:]: nc.dram_tensor(n, x.shape, mybir.dt.from_np(x.dtype), kind="ExternalInput").ap()
         for n, x in arrays.items()}
    for n, (shape, dtype) in zip(OUT_NAMES, _OUTS):
        a[n] = nc.dram_tensor("out_" + n, shape, mybir.dt.from_np(np.dtype(dtype)), kind="ExternalOutput").ap()
    build_layer(nc, a)
    r = run_bass_kernel_spmd(nc, [arrays], core_ids=[0])
    return tuple(r.results[0]["out_" + n] for n in OUT_NAMES)
```
